# Optimizing a Trainium2 kernel written in Bass

```python
import jax, jax.numpy as jnp
from jax import lax
import numpy as np

D_MODEL = 1024
BATCH = 1
SEQ = 1024
DEPTH = 1

CHUNK = 64
HEAD_DIM = 64
RWKV_WIDTH = D_MODEL // 2
ATT_WIDTH = D_MODEL - RWKV_WIDTH
MIX_WIDTH = RWKV_WIDTH + ATT_WIDTH
RWKV_HEADS = RWKV_WIDTH // HEAD_DIM
ATT_HEADS = ATT_WIDTH // HEAD_DIM
KV_HEADS = 2
GROUP = ATT_HEADS // KV_HEADS
KV_WIDTH = KV_HEADS * HEAD_DIM
WINDOW = 128
WINDOW_CHUNKS = WINDOW // CHUNK
DECAY_LORA = 32
ICLR_LORA = 32
VALUE_LORA = 32
GATE_LORA = 96
D_FF = 2816
CONV_WIDTH = 3
N_ATT_COLS = ATT_WIDTH + 2 * KV_WIDTH
N_RWKV_COLS0 = 3 * RWKV_WIDTH + DECAY_LORA + ICLR_LORA + GATE_LORA
N_RWKV_COLS = N_RWKV_COLS0 + VALUE_LORA
N_IN0 = N_ATT_COLS + N_RWKV_COLS0
N_IN = N_ATT_COLS + N_RWKV_COLS
RMS_EPS = 1e-6
LNX_EPS = 64e-5
NEG_INF = -1e30

kernel_name = "hybrid_rwkv7_swa_sink_convffn_adaln"

def rms_norm(x, gain, eps=RMS_EPS):
    xf = x.astype(jnp.float32)
    y = xf * lax.rsqrt(jnp.mean(xf * xf, axis=-1, keepdims=True) + eps)
    return (y * gain.astype(jnp.float32)).astype(x.dtype)

def modulate(h, shift, scale):
    return h * (1 + scale[:, None, :]) + shift[:, None, :]

def shift_prev(t, n=1):
    pad = [(0, 0)] * t.ndim
    pad[1] = (n, 0)
    return jnp.pad(t, pad)[:, :t.shape[1]]

def rwkv7_scan(r, w, k, v, a, b):
    B, S, H, N = r.shape
    def step(state, inp):
        r_t, w_t, k_t, v_t, a_t, b_t = inp
        sa = jnp.einsum('bhvk,bhk->bhv', state, a_t)
        state = (state * w_t[:, :, None, :] + sa[..., None] * b_t[:, :, None, :]
                 + v_t[..., None] * k_t[:, :, None, :])
        y_t = jnp.einsum('bhvk,bhk->bhv', state, r_t)
        return state, y_t
    tm = lambda t: jnp.moveaxis(t, 1, 0)
    s0 = jnp.zeros((B, H, N, N), jnp.float32)
    _, y = lax.scan(step, s0, (tm(r), tm(w), tm(k), tm(v), tm(a), tm(b)))
    return jnp.moveaxis(y, 0, 1)

def rwkv7_time_mix(p, mu, w0, w_up, a0, a_up, v0, v_up, g_up, k_k, k_a, r_k, lnx_g, lnx_b, v_first):
    B, S, _ = p.shape
    f32 = lambda t: t.astype(jnp.float32)
    heads = lambda t: t.reshape(B, S, RWKV_HEADS, HEAD_DIM)
    p = p + (shift_prev(p) - p) * mu
    W = RWKV_WIDTH
    r, k, v = p[..., :W], p[..., W:2 * W], p[..., 2 * W:3 * W]
    o = 3 * W
    w_lo = p[..., o:o + DECAY_LORA]; o += DECAY_LORA
    a_lo = p[..., o:o + ICLR_LORA]; o += ICLR_LORA
    g_lo = p[..., o:o + GATE_LORA]; o += GATE_LORA
    w_log = -jax.nn.softplus(-(w0 + jnp.tanh(w_lo) @ w_up)) - 0.5
    decay = jnp.exp(-jnp.exp(f32(w_log)))
    if v0 is None:
        v_first = v
    else:
        v_lo = p[..., o:o + VALUE_LORA]
        v = v + (v_first - v) * jax.nn.sigmoid(v0 + v_lo @ v_up)
    a = jax.nn.sigmoid(a0 + a_lo @ a_up)
    g = jax.nn.sigmoid(g_lo) @ g_up
    kk = heads(f32(k * k_k))
    kk = kk / jnp.maximum(jnp.linalg.norm(kk, axis=-1, keepdims=True), 1e-12)
    k = k * (1 + (a - 1) * k_a)
    rh, kh, vh, ah = heads(f32(r)), heads(f32(k)), heads(f32(v)), heads(f32(a))
    y = rwkv7_scan(rh, heads(decay), kh, vh, -kk, kk * ah)
    mean = jnp.mean(y, axis=-1, keepdims=True)
    var = jnp.mean(jnp.square(y - mean), axis=-1, keepdims=True)
    y = ((y - mean) * lax.rsqrt(var + LNX_EPS)).reshape(B, S, W) * f32(lnx_g) + f32(lnx_b)
    bonus = jnp.sum(rh * kh * f32(r_k), axis=-1, keepdims=True) * vh
    y = y + bonus.reshape(B, S, W)
    return (y * f32(g)).astype(p.dtype), v_first

def window_blocks(t):
    parts = [shift_prev(t, j) for j in range(WINDOW_CHUNKS - 1, 0, -1)] + [t]
    return jnp.concatenate(parts, axis=2)

def swa_sink_attention(q, k, v, q_gain, k_gain, sinks):
    B, S, _ = q.shape
    nC = S // CHUNK
    q = rms_norm(q.reshape(B, S, ATT_HEADS, HEAD_DIM), q_gain)
    k = rms_norm(k.reshape(B, S, KV_HEADS, HEAD_DIM), k_gain)
    qc = q.reshape(B, nC, CHUNK, KV_HEADS, GROUP, HEAD_DIM)
    kw = window_blocks(k.reshape(B, nC, CHUNK, KV_HEADS, HEAD_DIM))
    vw = window_blocks(v.reshape(B, nC, CHUNK, KV_HEADS, HEAD_DIM))
    s = jnp.einsum('bcqhgd,bckhd->bhgcqk', qc, kw,
                   preferred_element_type=jnp.float32) * (HEAD_DIM ** -0.5)
    chunk_idx = jnp.arange(nC)[:, None]
    key_blk = jnp.arange(WINDOW_CHUNKS * CHUNK)[None, :] // CHUNK
    valid = chunk_idx >= (WINDOW_CHUNKS - 1 - key_blk)
    s = jnp.where(valid[:, None, :], s, NEG_INF)
    sink = sinks.astype(jnp.float32).reshape(KV_HEADS, GROUP)[None, :, :, None, None, None]
    m = jnp.maximum(jnp.max(s, axis=-1, keepdims=True), sink)
    pe = jnp.exp(s - m)
    denom = jnp.sum(pe, axis=-1, keepdims=True) + jnp.exp(sink - m)
    probs = (pe / denom).astype(v.dtype)
    o = jnp.einsum('bhgcqk,bckhd->bcqhgd', probs, vw)
    return o.reshape(B, S, ATT_WIDTH)

def conv_ffn(h, w_up, conv_w, conv_b, w_down):
    u = h @ w_up
    acc = u * conv_w[CONV_WIDTH - 1] + conv_b
    for j in range(CONV_WIDTH - 1):
        acc = acc + shift_prev(u, CONV_WIDTH - 1 - j) * conv_w[j]
    gate, up = acc[..., :D_FF], acc[..., D_FF:]
    return (jax.nn.silu(gate) * up) @ w_down

def setup_inputs(seed: int = 0) -> dict:
    key = jax.random.key(seed)
    ks = iter(jax.random.split(key, 40))
    nrm = lambda shape, scale: jax.random.normal(next(ks), shape, jnp.float32) * scale
    uni = lambda shape, lo, hi: jax.random.uniform(next(ks), shape, jnp.float32, lo, hi)
    L, L1 = DEPTH, DEPTH - 1
    return {
        "x": nrm((BATCH, SEQ, D_MODEL), 1.0),
        "c": nrm((BATCH, D_MODEL), 1.0),
        "ada_w": nrm((L, D_MODEL, 6 * D_MODEL), D_MODEL ** -0.5),
        "ada_b": nrm((L, 6 * D_MODEL), 0.02),
        "norm_mix_g": 1.0 + nrm((L, D_MODEL), 0.02),
        "norm_ffn_g": 1.0 + nrm((L, D_MODEL), 0.02),
        "w_in0": nrm((D_MODEL, N_IN0), D_MODEL ** -0.5),
        "w_in": nrm((L1, D_MODEL, N_IN), D_MODEL ** -0.5),
        "shift_mu0": uni((N_RWKV_COLS0,), 0.0, 1.0),
        "shift_mu": uni((L1, N_RWKV_COLS), 0.0, 1.0),
        "rwkv_w0": uni((L, RWKV_WIDTH), -6.0, -1.0),
        "rwkv_w_up": nrm((L, DECAY_LORA, RWKV_WIDTH), DECAY_LORA ** -0.5),
        "rwkv_a0": nrm((L, RWKV_WIDTH), 0.1),
        "rwkv_a_up": nrm((L, ICLR_LORA, RWKV_WIDTH), ICLR_LORA ** -0.5),
        "rwkv_v0": nrm((L1, RWKV_WIDTH), 0.1),
        "rwkv_v_up": nrm((L1, VALUE_LORA, RWKV_WIDTH), VALUE_LORA ** -0.5),
        "rwkv_g_up": nrm((L, GATE_LORA, RWKV_WIDTH), GATE_LORA ** -0.5),
        "rwkv_k_k": 0.85 + nrm((L, RWKV_WIDTH), 0.05),
        "rwkv_k_a": 1.0 + nrm((L, RWKV_WIDTH), 0.05),
        "rwkv_r_k": nrm((L, RWKV_HEADS, HEAD_DIM), 0.1),
        "rwkv_lnx_g": 1.0 + nrm((L, RWKV_WIDTH), 0.02),
        "rwkv_lnx_b": nrm((L, RWKV_WIDTH), 0.02),
        "attn_q_gain": 1.0 + nrm((L, HEAD_DIM), 0.02),
        "attn_k_gain": 1.0 + nrm((L, HEAD_DIM), 0.02),
        "attn_sinks": nrm((L, ATT_HEADS), 1.0),
        "w_out": nrm((L, MIX_WIDTH, D_MODEL), MIX_WIDTH ** -0.5),
        "ffn_w_up": nrm((L, D_MODEL, 2 * D_FF), D_MODEL ** -0.5),
        "ffn_conv_w": nrm((L, CONV_WIDTH, 2 * D_FF), CONV_WIDTH ** -0.5),
        "ffn_conv_b": nrm((L, 2 * D_FF), 0.02),
        "ffn_w_down": nrm((L, D_FF, D_MODEL), D_FF ** -0.5),
    }

def reference(x, c, ada_w, ada_b, norm_mix_g, norm_ffn_g, w_in0, w_in, shift_mu0, shift_mu,
              rwkv_w0, rwkv_w_up, rwkv_a0, rwkv_a_up, rwkv_v0, rwkv_v_up, rwkv_g_up, rwkv_k_k,
              rwkv_k_a, rwkv_r_k, rwkv_lnx_g, rwkv_lnx_b, attn_q_gain, attn_k_gain, attn_sinks,
              w_out, ffn_w_up, ffn_conv_w, ffn_conv_b, ffn_w_down):
    cond = jax.nn.silu(c)
    v_first = None
    for l in range(DEPTH):
        first = l == 0
        mod = cond @ ada_w[l] + ada_b[l]
        sh1, sc1, g1, sh2, sc2, g2 = jnp.split(mod, 6, axis=-1)
        h = modulate(rms_norm(x, norm_mix_g[l]), sh1, sc1)
        proj = h @ (w_in0 if first else w_in[l - 1])
        q = proj[..., :ATT_WIDTH]
        k = proj[..., ATT_WIDTH:ATT_WIDTH + KV_WIDTH]
        v = proj[..., ATT_WIDTH + KV_WIDTH:N_ATT_COLS]
        attn_out = swa_sink_attention(q, k, v, attn_q_gain[l], attn_k_gain[l], attn_sinks[l])
        rwkv_out, v_first = rwkv7_time_mix(
            proj[..., N_ATT_COLS:], shift_mu0 if first else shift_mu[l - 1],
            rwkv_w0[l], rwkv_w_up[l], rwkv_a0[l], rwkv_a_up[l],
            None if first else rwkv_v0[l - 1], None if first else rwkv_v_up[l - 1],
            rwkv_g_up[l], rwkv_k_k[l], rwkv_k_a[l], rwkv_r_k[l], rwkv_lnx_g[l], rwkv_lnx_b[l], v_first)
        mix = jnp.concatenate([rwkv_out, attn_out], axis=-1) @ w_out[l]
        x = x + g1[:, None, :] * mix
        h = modulate(rms_norm(x, norm_ffn_g[l]), sh2, sc2)
        x = x + g2[:, None, :] * conv_ffn(h, ffn_w_up[l], ffn_conv_w[l], ffn_conv_b[l], ffn_w_down[l])
    return x


_drawn_inputs = setup_inputs


def setup_inputs(seed=0):
    import zlib

    import numpy as np

    out = dict(_drawn_inputs(seed))
    spreads = {}
    factors = {'norm_mix_g': 6.203,
     'norm_ffn_g': 26.699,
     'rwkv_a0': 6.382,
     'rwkv_lnx_g': 200.0,
     'rwkv_lnx_b': 200.0,
     'attn_q_gain': 40.494,
     'attn_k_gain': 35.539,
     'attn_sinks': 8.0,
     'ffn_conv_b': 32.845,
     'rwkv_w_up': 7.912,
     'rwkv_k_k': 33.483}
    for name, (base, spread) in spreads.items():
        noise = np.random.default_rng([zlib.crc32(name.encode()), seed]).standard_normal(out[name].shape)
        drawn = base * np.exp(spread * noise) if base else spread * noise
        out[name] = __import__('jax').numpy.asarray(drawn.astype(out[name].dtype))
    for name, factor in factors.items():
        out[name] = (out[name] * factor).astype(out[name].dtype)
    return out
```

```python
import math
from contextlib import ExitStack

import numpy as np

import concourse.bass as bass
from concourse import mybir

F32 = mybir.dt.float32
F32R = mybir.dt.float32r
ALU = mybir.AluOpType
ACT = mybir.ActivationFunctionType
AX_X = mybir.AxisListType.X

P = 128
D = 1024
S = 1024
KT = D // P
HALF = 512
CH = 64
HD = 64
RW = 512
NJ = RW // P
FF = 2816
NF = FF // P
NIN = 20
NADA = 48
RMS_EPS = 1e-6
LNX_EPS = 64e-5
DEC = math.exp(-0.5)
NEG = -1e30
DL, IL, GL = 32, 32, 96
NCP = HALF // P
NLEV = 5
NQ = 2 * NCP

V_MU, V_ADAB, V_GMIX, V_GFFN = 0, 20, 68, 76
V_QG, V_KG, V_EPS, V_LEPS, V_SINK = 84, 85, 86, 87, 88
V_CONV = 92
V_N = V_CONV + NF * 2 * 4
J_W0, J_A0, J_KK, J_KA, J_RK, J_G, J_B, J_N = 0, 1, 2, 3, 4, 5, 6, 8
C_ID, C_BLK, C_ONE, C_M4, C_OFF1, C_OFF1T, C_LEV, C_RST = 0, 1, 2, 3, 7, 8, 9, 14
C_N = C_RST + 4


def constants():
    t = np.arange(P)
    same = (t[:, None] // CH) == (t[None, :] // CH)
    lower = same & (t[:, None] > t[None, :])
    mats = [np.eye(P), same, np.ones((P, P)),
            lower.T, same & (t[:, None] <= t[None, :]), lower, lower]
    offs = []
    for m in (1, 2, 4, 8, 16, 32):
        pair = (t[:, None] // (2 * m)) == (t[None, :] // (2 * m))
        offs.append(pair & ((t[:, None] // m) % 2 == 1) & ((t[None, :] // m) % 2 == 0))
    mats += [offs[0], offs[0].T] + offs[1:]
    reset = np.tile((np.arange(HALF) % CH != 0)[None, :], (P, 1))
    return np.concatenate([m.astype(np.float32) for m in mats] + [reset.astype(np.float32)], axis=1)


def build(nc, xT, condb, adaw, vecs, consts, win, loraw, jvecs, wout, wup, wdown, outT):
    with ExitStack() as ctx:
        sems = {}

        def sem(name):
            if name not in sems:
                sems[name] = ctx.enter_context(nc.semaphore(name))
            return sems[name]

        def at(name, kb, shape, dt=F32):
            return nc.alloc_sbuf_tensor_at(name, shape, dt, offset=int(kb * 1024))

        projD = nc.dram_tensor("projD", (NIN, P, S), F32, kind="Internal").ap()
        mixD = nc.dram_tensor("mixD", (KT, P, S), F32, kind="Internal").ap()
        x1D = nc.dram_tensor("x1D", (KT, P, S), F32, kind="Internal").ap()

        A0 = -(-nc.sbuf_base // 32) * 32 / 1024.0
        ctx.enter_context(nc.sbuf_tensor("arena", [P, 206 * 256], F32))
        vec = at("vec", A0 + 0, [P, V_N])
        jv = at("jv", A0 + 1.25, [P, J_N])
        omu = at("omu", A0 + 1.5, [P, NIN])
        mod = at("mod", A0 + 1.75, [P, NADA])
        modA = at("modA", A0 + 2, [P, 2 * KT])
        omka = at("omka", A0 + 2.25, [P, 1])
        con = at("con", A0 + 3, [P, C_N * P])
        wraw = at("wraw", A0 + 13, [P, 2, 1024])
        whi = at("whi", A0 + 21, [P, 2, 1024], F32R)
        wlo = at("wlo", A0 + 29, [P, 2, 1024], F32R)
        B = A0 + 37
        HI = at("HI", B, [P, KT, S], F32R)
        LO = at("LO", B + 32, [P, KT, S], F32R)
        X = at("X", B + 64, [P, KT, S])
        adat = at("adat", B + 96, [P, 4, 1024])
        cond = at("cond", B + 112, [P, 1024])
        junk = at("junk", B + 116, [P, 1024])
        sqt = at("sqt", B + 120, [P, 2, S])
        rstd = at("rstd", B + 128, [P, S])
        pr = at("pr", B + 136, [P, 2, S])
        mst = at("mst", B + 96, [P, 2, S])
        xin = at("xin", B + 104, [P, 2, S])
        actb = at("actb", B + 64, [P, NF, S])
        gu = at("gu", B + 152, [P, 2, S])
        wdn = at("wdn", B, [P, 2, NF * P])
        x1in = at("x1in", B + 24, [P, 2, S])
        yout = at("yout", B + 32, [P, 2, S])
        o = [B]

        def alloc(name, shape):
            words = 1
            for n in shape[1:]:
                words *= n
            t = at(name, o[0], shape)
            o[0] += words * 4 / 1024.0
            return t

        lwa = alloc("lwa", [P, S])
        lg = alloc("lg", [P, S])
        lw = alloc("lw", [P, 2, P])
        rkv = alloc("rkv", [P, 3, S])
        half = {n: alloc(n, [P, HALF]) for n in (
            "sg", "aa", "gg", "cs", "pinv", "kkr", "ksq", "nrm", "rin", "nkk", "tka", "km", "t2",
            "kh", "bh", "t3", "bon", "y", "yc", "ysq", "sd", "rs", "yo")}
        pb = alloc("pb", [P, 8 * 65])
        ar = alloc("ar", [P, NCP, 2, P])
        bk = alloc("bk", [P, NCP, 2, P])
        nat = alloc("nat", [P, NCP, 4, P])
        am = alloc("am", [P, NQ, 4, P])
        ark = alloc("ark", [P, 2, NCP, P])
        Xi = alloc("Xi", [P, NQ, P])
        XiT = alloc("XiT", [P, NQ, P])
        T1 = alloc("T1", [P, NQ, P])
        wd_ = alloc("wd_", [P, NCP, 3, P])
        sh = alloc("sh", [P, 9, P])
        us = alloc("us", [P, NCP, P])
        assert o[0] <= A0 + 205, o[0]
        o[0] = B
        aqk = alloc("aqk", [P, 5, CH + S])
        av = alloc("av", [P, CH + S])
        asq = alloc("asq", [P, 2, HALF])
        asd = alloc("asd", [P, 2, HALF])
        neg = alloc("neg", [P, CH + S])
        stg = alloc("stg", [P, 2, 512])
        sb_s = alloc("sb_s", [P, 2, 4, P])
        pe_ = alloc("pe_", [P, 2, 4, P])
        pt = alloc("pt", [P, 2, 4, P])
        vn = alloc("vn", [P, 2, P])
        sm = alloc("sm", [P, 2, 6, 4])

        ps = ctx.enter_context(nc.psum_tensor("ps", [P, 8, HALF], F32))

        def cm(n, k=1):
            return con[:, n * P:(n + k) * P]

        ident, blk, ones = cm(C_ID), cm(C_BLK), cm(C_ONE)

        def two(b):
            return ps[:, b:b + 2, :].rearrange("p a b -> p (a b)")

        T_OUT, T_UP = NIN, NIN + KT

        block = ctx.enter_context(nc.Block())

        @block.sync
        def _(sp):
            sp.dma_start(vec[:, :], vecs).then_inc(sem("vec_in"), 16)
            sp.dma_start(con[:, :], consts).then_inc(sem("con_in"), 16)
            sp.dma_start(cond[:, :], condb).then_inc(sem("cond_in"), 16)
            for t in range(KT):
                sp.dma_start(X[:, t, :], xT[t]).then_inc(sem(f"x_in{t}"), 16)

            def load_ada(i, s):
                sp.dma_start(adat[:, s, :], adaw[i]).then_inc(sem(f"ada_in{s}"), 16)

            with sp.Fori(0, 4) as i:
                for s in range(4):
                    sp.wait_ge(sem("ada_used"), i * 4)
                    load_ada(i * 4 + s, s)

            def load_w(src, tile, p, n):
                sp.wait_ge(sem("wlo_made"), n)
                sp.dma_start(wraw[:, p, :], src[tile]).then_inc(sem(f"w_in{p}"), 16)

            for p in range(2):
                sp.dma_start(wraw[:, p, :], win[p]).then_inc(sem(f"w_in{p}"), 16)

            def in_proj(i, ada, last=False):
                if ada:
                    for s in range(4):
                        sp.wait_ge(sem("ada_used"), 16 + i * 4 + s - 3 + (3 - s))
                        load_ada(16 + i * 4 + s, s)
                for p in range(2):
                    if not last:
                        load_w(win, i * 2 + 2 + p, p, i * 2 + 1 + p)
                    else:
                        load_w(wout, p, p, i * 2 + 1 + p)
                    sp.wait_ge(sem("mixed"), i * 2 + 1 + p)
                    sp.dma_start(projD[i * 2 + p], pr[:, p, :]).then_inc(sem(f"proj_out{p}"), 16)

            with sp.Fori(0, 8) as i:
                in_proj(i, True)
            in_proj(8, False)
            in_proj(9, False, last=True)
            for p in range(2):
                sp.wait_ge(sem(f"proj_out{p}"), 16 * (NIN // 2))
            sp.wait_ge(sem("tile_mm"), NIN)
            sp.dma_start(lwa[:, :], projD[0]).then_inc(sem("lora_in"), 16)
            sp.dma_start(lg[:, :], projD[1]).then_inc(sem("lora_in"), 16)
            with sp.Fori(0, NJ) as j:
                sp.wait_ge(sem("y_ready"), j * 2)
                sp.dma_start(rkv[:, :, :], projD[bass.ds(j * 3 + 2, 3)].rearrange("a p s -> p a s")).then_inc(sem("rkv_in"), 16)
                sp.dma_start(lw[:, :, :], loraw[j]).then_inc(sem("rkv_in"), 16)
                sp.dma_start(jv[:, :], jvecs[j]).then_inc(sem("rkv_in"), 16)
                for hf in range(2):
                    sp.wait_ge(sem("y_ready"), j * 2 + hf + 1)
                    sp.dma_start(mixD[j, :, hf * HALF:(hf + 1) * HALF], half["yo"][:, :]).then_inc(sem("y_out"), 16)
            sp.wait_ge(sem("y_out"), 16 * 2 * NJ)
            for t in range(5):
                sp.dma_start(aqk[:, t, CH:], projD[14 + t]).then_inc(sem("qkv_in"), 16)
            sp.dma_start(av[:, CH:], projD[19]).then_inc(sem("qkv_in"), 16)
            sp.wait_ge(sem("o_ev"), 16)
            for t in range(4):
                sp.dma_start(mixD[4 + t], aqk[:, t, CH:]).then_inc(sem("o_out"), 16)
            sp.wait_ge(sem("o_out"), 64)
            with sp.Fori(0, KT // 2) as i:
                for p in range(2):
                    sp.wait_ge(sem("mix_split"), i * 2)
                    sp.dma_start(mst[:, p, :], mixD[i * 2 + p]).then_inc(sem(f"mix_in{p}"), 16)

            def out_proj(i, last):
                for p in range(2):
                    sp.wait_ge(sem("x1_made"), i * 2)
                    sp.dma_start(xin[:, p, :], xT[i * 2 + p]).then_inc(sem(f"xin_in{p}"), 16)
                for p in range(2):
                    if not last:
                        load_w(wout, i * 2 + 2 + p, p, i * 2 + 1 + p + T_OUT)
                    else:
                        load_w(wup, p, p, i * 2 + 1 + p + T_OUT)
                    sp.wait_ge(sem("x1_made"), i * 2 + p + 1)
                    sp.dma_start(x1D[i * 2 + p], X[:, bass.ds(i * 2 + p, 1), :].rearrange("p a s -> p (a s)") if not isinstance(i, int) else X[:, i * 2 + p, :]).then_inc(sem("x1_out"), 16)

            with sp.Fori(0, KT // 2 - 1) as i:
                out_proj(i, False)
            out_proj(KT // 2 - 1, True)
            with sp.Fori(0, NF - 1) as f:
                for p in range(2):
                    load_w(wup, f * 2 + 2 + p, p, f * 2 + 1 + p + T_UP)
            sp.wait_ge(sem("x1_out"), 16 * KT)
            sp.wait_ge(sem("tile_mm"), T_UP + 2 * NF)
            with sp.Fori(0, KT // 2) as i:
                for p in range(2):
                    sp.wait_ge(sem("down_mm"), i * 2)
                    sp.wait_ge(sem("y2_made"), i * 2)
                    sp.dma_start(wdn[:, p, :], wdown[i * 2 + p]).then_inc(sem(f"wd_in{p}"), 16)
                    sp.dma_start(x1in[:, p, :], x1D[i * 2 + p]).then_inc(sem(f"x1_in{p}"), 16)
                for p in range(2):
                    sp.wait_ge(sem("y2_made"), i * 2 + p + 1)
                    sp.dma_start(outT[i * 2 + p], yout[:, p, :]).then_inc(sem(f"out_out{p}"), 16)
            for p in range(2):
                sp.wait_ge(sem(f"out_out{p}"), 16 * KT // 2)

        @block.scalar
        def _(act):
            def norm(n):
                for t in range(KT):
                    if n == 0:
                        act.wait_ge(sem(f"x_in{t}"), 16)
                    else:
                        act.wait_ge(sem("x1_made"), t + 1)
                    if t >= 2:
                        act.wait_ge(sem("ssq_mm"), n * KT + t - 1)
                    act.activation(sqt[:, t % 2, :], X[:, t, :], ACT.Square).then_inc(sem("sq"), 1)
                act.wait_ge(sem("ssq_mm"), n * KT + KT)
                act.activation(rstd[:, :], two(4), ACT.Sqrt, bias=vec[:, V_EPS:V_EPS + 1], scale=1.0 / D).then_inc(sem("std"), 1)
                if n == 1:
                    act.wait_ge(sem("tile_mm"), T_UP)
                for t in range(KT):
                    act.wait_ge(sem("h_made"), n * KT + t + 1)
                    act.activation(HI[:, t, :], X[:, t, :], ACT.Copy).then_inc(sem("h_hi"), 1)

            def split_hi(p, nth, tiles_before):
                act.wait_ge(sem(f"w_in{p}"), nth)
                act.wait_ge(sem("tile_mm"), tiles_before)
                act.activation(whi[:, p, :], wraw[:, p, :], ACT.Copy).then_inc(sem("whi_made"), 1)

            act.wait_ge(sem("cond_in"), 16)
            act.activation(cond[:, :], cond[:, :], ACT.Silu).then_inc(sem("cond"), 1)
            act.wait_ge(sem("vec_in"), 16)
            norm(0)

            for p in range(2):
                act.wait_ge(sem(f"w_in{p}"), 16)
                act.activation(whi[:, p, :], wraw[:, p, :], ACT.Copy).then_inc(sem("whi_made"), 1)

            def in_proj(i, last=False):
                for p in range(2):
                    act.wait_ge(sem("tile_mm"), i * 2 + p + 1)
                    act.wait_ge(sem(f"proj_out{p}"), i * 16)
                    act.activation(pr[:, p, :], two(2 * p), ACT.Copy, scale=omu[:, bass.ds(i * 2 + p, 1)]).then_inc(sem("unmixed"), 1)
                    split_hi(p, i * 16 + 32, i * 2 + p + 1)

            act.wait_ge(sem("omu"), 1)
            with act.Fori(0, NIN // 2) as i:
                in_proj(i)

            act.wait_ge(sem("lora_in"), 32)
            act.activation(lwa[0:DL, :], lwa[0:DL, :], ACT.Tanh).then_inc(sem("lora_act"), 1)
            act.activation(lg[0:GL, :], lg[0:GL, :], ACT.Sigmoid).then_inc(sem("lora_act"), 1)

            with act.Fori(0, NJ) as j:
                for hf in range(2):
                    it = j * 2 + hf
                    h = half
                    act.wait_ge(sem("rkv_in"), j * 48 + 48)
                    act.wait_ge(sem("lora_mm"), it * 3 + 3)
                    act.activation(h["sg"][:, :], ps[:, 0, :], ACT.Sigmoid, bias=jv[:, J_W0:J_W0 + 1]).then_inc(sem("lora_ev"), 1)
                    act.activation(h["aa"][:, :], ps[:, 1, :], ACT.Sigmoid, bias=jv[:, J_A0:J_A0 + 1]).then_inc(sem("lora_ev"), 1)
                    act.activation(h["gg"][:, :], ps[:, 2, :], ACT.Copy).then_inc(sem("lora_ev"), 1)
                    act.wait_ge(sem("kkr"), it + 1)
                    act.activation(h["ksq"][:, :], h["kkr"][:, :], ACT.Square).then_inc(sem("ksq"), 1)
                    act.wait_ge(sem("cs"), it + 1)
                    act.activation(pb[:, :].rearrange("p (c t) -> p c t", t=65)[:, :, 1:65],
                                   h["cs"][:, :].rearrange("p (c t) -> p c t", t=CH), ACT.Exp, scale=-DEC).then_inc(sem("pexp"), 1)
                    act.activation(h["pinv"][:, :], h["cs"][:, :], ACT.Exp, scale=DEC).then_inc(sem("pexp"), 1)
                    act.wait_ge(sem("kss_mm"), it + 1)
                    act.activation(h["nrm"][:, :], ps[:, 3, :], ACT.Sqrt).then_inc(sem("nrm"), 1)
                    for cp in range(NCP):
                        act.wait_ge(sem("nat_mm"), it * NCP + cp + 1)
                        act.activation(nat[:, cp, :, :].rearrange("p a b -> p (a b)"), ps[:, cp, :], ACT.Copy).then_inc(sem("nat"), 1)
                    for cp in range(NCP):
                        act.wait_ge(sem("wd_mm"), it * NCP + cp + 1)
                        act.activation(wd_[:, cp, :, :].rearrange("p a b -> p (a b)"), ps[:, 6 + cp % 2, 0:384], ACT.Copy).then_inc(sem("wd"), 1)
                    for c in range(8):
                        cp, e = c // 2, c % 2
                        r = slice(64 * e, 64 * e + 64)
                        act.wait_ge(sem("u_mm"), it * 8 + c + 1)
                        act.activation(us[r, cp, :], ps[r, cp % 2, 0:P], ACT.Copy).then_inc(sem("u"), 1)
                    for cp in range(NCP):
                        act.wait_ge(sem("y_mm"), it * NCP + cp + 1)
                        act.activation(h["y"][:, cp * P:(cp + 1) * P], ps[:, 4 + cp % 2, 0:P], ACT.Copy).then_inc(sem("y"), 1)
                    act.wait_ge(sem("yc"), it + 1)
                    act.activation(h["ysq"][:, :], h["yc"][:, :], ACT.Square).then_inc(sem("ysq"), 1)
                    act.wait_ge(sem("yvar_mm"), it + 1)
                    act.activation(h["sd"][:, :], ps[:, 7, :], ACT.Sqrt, bias=vec[:, V_LEPS:V_LEPS + 1], scale=1.0 / HD).then_inc(sem("sd"), 1)

            act.wait_ge(sem("qkv_in"), 96)
            with act.Fori(0, 5) as t:
                for hf in range(2):
                    act.wait_ge(sem("qn_mm"), t * 2)
                    act.activation(asq[:, hf, :], aqk[:, t, CH + hf * HALF:CH + (hf + 1) * HALF], ACT.Square).then_inc(sem("qsq"), 1)
                for hf in range(2):
                    act.wait_ge(sem("qn_mm"), t * 2 + hf + 1)
                    act.wait_ge(sem("qn"), t * 2)
                    act.activation(asd[:, hf, :], ps[:, hf, :], ACT.Sqrt, bias=vec[:, V_EPS:V_EPS + 1], scale=1.0 / HD).then_inc(sem("qsd"), 1)
            with act.Fori(0, 8) as i:
                for e in range(2):
                    c = i * 2 + e
                    act.wait_ge(sem("s_nmax"), c + 1)
                    act.wait_ge(sem("p_mm"), i * 2)
                    for g in range(4):
                        act.activation(pe_[:, e, g, :], sb_s[:, e, g, :], ACT.Exp, bias=sm[:, e, 1, g:g + 1],
                                       scale=HD ** -0.5, accum_out=sm[:, e, 3, g:g + 1]).then_inc(sem("p_exp"), 1)
                    act.activation(sm[:, e, 4, :], sm[:, e, 2, :], ACT.Exp).then_inc(sem("sink_exp"), 1)
                for e in range(2):
                    c = i * 2 + e
                    act.wait_ge(sem("p_mm"), c + 1)
                    act.wait_ge(sem("o_mm"), i * 2)
                    act.activation(pt[:, e, :, :].rearrange("p a b -> p (a b)"), ps[:, 4 + e, :], ACT.Copy).then_inc(sem("pt"), 1)

            with act.Fori(0, KT // 2) as i:
                for p in range(2):
                    act.wait_ge(sem(f"mix_in{p}"), i * 16 + 16)
                    act.activation(HI[:, i * 2 + p, :], mst[:, p, :], ACT.Copy).then_inc(sem("mix_hi"), 1)

            with act.Fori(0, KT // 2) as i:
                for p in range(2):
                    split_hi(p, 16 * (NIN // 2) + i * 16 + 32, T_OUT + i * 2 + p + 1)
            norm(1)

            def up(f, more):
                for p in range(2):
                    act.wait_ge(sem("tile_mm"), T_UP + f * 2 + p + 1)
                    act.wait_ge(sem("act_made"), f)
                    c = V_CONV + (f * 2 + p) * 4
                    act.activation(gu[:, p, :], two(2 * p + 4 * up.par), ACT.Identity,
                                   bias=vec[:, bass.ds(c + 3, 1)], scale=vec[:, bass.ds(c + 2, 1)]).then_inc(sem("conv0"), 1)
                    if more:
                        split_hi(p, 16 * (NIN // 2 + KT // 2) + f * 16 + 32, T_UP + f * 2 + p + 1)
                act.wait_ge(sem("conv2"), f * 2 + 1)
                act.activation(gu[:, 0, :], gu[:, 0, :], ACT.Silu).then_inc(sem("silu"), 1)

            with act.Fori(0, NF // 2 - 1) as i:
                for par in range(2):
                    up.par = par
                    up(i * 2 + par, True)
            up.par = 0
            up(NF - 2, True)
            up.par = 1
            up(NF - 1, False)

        @block.vector
        def _(dve):
            def norm(n):
                sc, sh_, gain = (8, 0, V_GMIX) if n == 0 else (32, 24, V_GFFN)
                dve.scalar_tensor_tensor(out=modA[:, n * KT:(n + 1) * KT], in0=mod[:, sc:sc + KT], scalar=1.0,
                                         in1=vec[:, gain:gain + KT], op0=ALU.add, op1=ALU.mult).then_inc(sem("modA"), 1)
                dve.wait_ge(sem("std"), n + 1)
                dve.reciprocal(rstd[:, :], rstd[:, :]).then_inc(sem("rstd"), 1)
                dve.wait_ge(sem("rstd"), n + 1)
                dve.wait_ge(sem("modA"), n + 1)
                for t in range(KT):
                    dve.scalar_tensor_tensor(out=X[:, t, :], in0=X[:, t, :], scalar=modA[:, n * KT + t:n * KT + t + 1],
                                             in1=rstd[:, :], op0=ALU.mult, op1=ALU.mult).then_inc(sem("h_scaled"), 1)
                    dve.wait_ge(sem("h_scaled"), n * KT + t + 1)
                    dve.tensor_scalar(X[:, t, :], X[:, t, :], mod[:, sh_ + t:sh_ + t + 1], None, ALU.add).then_inc(sem("h_made"), 1)

            dve.wait_ge(sem("vec_in"), 16)
            dve.tensor_scalar(omu[:, :], vec[:, V_MU:V_MU + NIN], -1.0, 1.0, ALU.mult, ALU.add).then_inc(sem("omu"), 1)
            dve.wait_ge(sem("cond"), 1)

            def ada(col, s, nth):
                dve.wait_ge(sem(f"ada_in{s}"), nth)
                dve.wait_ge(sem("ada_used"), col)
                dve.scalar_tensor_tensor(out=junk[:, :], in0=adat[:, s, :], scalar=1.0, in1=cond[:, :], op0=ALU.mult,
                                         op1=ALU.mult, accum_out=mod[:, bass.ds(col, 1)]).then_inc(sem("ada_used"), 1)

            with dve.Fori(0, 4) as i:
                for s in range(4):
                    ada(i * 4 + s, s, i * 16 + 16)
            dve.wait_ge(sem("ada_used"), 16)
            dve.tensor_tensor(mod[:, 0:16], mod[:, 0:16], vec[:, V_ADAB:V_ADAB + 16], ALU.add).then_inc(sem("mod"), 1)
            dve.wait_ge(sem("mod"), 1)
            norm(0)

            def in_proj(i, with_ada):
                for p in range(2):
                    if with_ada:
                        for s in (2 * p, 2 * p + 1):
                            ada(16 + i * 4 + s, s, 64 + i * 16 + 16)
                    dve.wait_ge(sem("unmixed"), i * 2 + p + 1)
                    dve.scalar_tensor_tensor(out=pr[:, p, 1:S], in0=two(2 * p)[:, 0:S - 1],
                                             scalar=vec[:, bass.ds(V_MU + i * 2 + p, 1)], in1=pr[:, p, 1:S],
                                             op0=ALU.mult, op1=ALU.add).then_inc(sem("mixed"), 1)

            with dve.Fori(0, 8) as i:
                in_proj(i, True)
            with dve.Fori(8, 10) as i:
                in_proj(i, False)
            dve.wait_ge(sem("ada_used"), NADA)
            dve.tensor_tensor(mod[:, 16:48], mod[:, 16:48], vec[:, V_ADAB + 16:V_ADAB + 48], ALU.add).then_inc(sem("mod"), 1)

            dve.wait_ge(sem("tile_mm"), NIN)
            dve.wait_ge(sem("proj_out1"), 16 * (NIN // 2))
            dve.wait_ge(sem("proj_out0"), 16 * (NIN // 2))
            dve.memset(sh[:, :, :], 0.0).then_inc(sem("sh_zero"), 1)
            pb3 = pb[:, :].rearrange("p (c t) -> p c t", t=65)
            dve.memset(pb3[:, :, 0:1], 1.0).then_inc(sem("pb_one"), 1)
            dve.wait_ge(sem("sh_zero"), 1)
            dve.wait_ge(sem("pb_one"), 1)

            def q4(t):
                return t.rearrange("p (c e t) -> p c e t", e=2, t=CH)

            pbv = pb[:, :].rearrange("p (c e t) -> p c e t", e=2, t=65)
            arv = ar[:, :, :, :].rearrange("p c a (e t) -> p c a e t", e=2)
            bkv = bk[:, :, :, :].rearrange("p c a (e t) -> p c a e t", e=2)
            with dve.Fori(0, NJ) as j:
                for hf in range(2):
                    it = j * 2 + hf
                    h = {n: t[:, :] for n, t in half.items()}
                    r, k, v = (rkv[:, a, hf * HALF:(hf + 1) * HALF] for a in range(3))
                    col = lambda a: jv[:, a:a + 1]
                    seq = sem("dve_rwkv")
                    n0 = [0]

                    def done(ins):
                        n0[0] += 1
                        ins.then_inc(seq, 1)
                        dve.wait_ge(seq, it * 6 + n0[0])

                    dve.wait_ge(sem("rkv_in"), j * 48 + 48)
                    if hf == 0:
                        dve.wait_ge(sem("omka"), j)
                        dve.tensor_scalar(omka[:, :], col(J_KA), -1.0, 1.0, ALU.mult, ALU.add).then_inc(sem("omka"), 1)
                    dve.tensor_scalar(h["kkr"], k, col(J_KK), None, ALU.mult).then_inc(sem("kkr"), 1)
                    dve.wait_ge(sem("lora_ev"), it * 3 + 3)
                    dve.tensor_tensor_scan(h["cs"], cm(C_RST, 4), h["sg"], 0.0, ALU.mult, ALU.add).then_inc(sem("cs"), 1)
                    dve.wait_ge(sem("omka"), j + 1)
                    done(dve.tensor_scalar(h["tka"], h["aa"], col(J_KA), omka[:, 0:1], ALU.mult, ALU.add))
                    done(dve.tensor_tensor(h["km"], k, h["tka"], ALU.mult))
                    dve.scalar_tensor_tensor(out=h["t3"], in0=r, scalar=col(J_RK), in1=h["km"], op0=ALU.mult, op1=ALU.mult).then_inc(sem("rk_prod"), 1)
                    dve.wait_ge(sem("nrm"), it + 1)
                    done(dve.tensor_scalar(h["nrm"], h["nrm"], 1e-12, None, ALU.max))
                    done(dve.reciprocal(h["rin"], h["nrm"]))
                    done(dve.scalar_tensor_tensor(out=h["nkk"], in0=h["kkr"], scalar=-1.0, in1=h["rin"], op0=ALU.mult, op1=ALU.mult))
                    dve.wait_ge(sem("pexp"), it * 2 + 2)
                    done(dve.tensor_tensor(h["t2"], h["aa"], h["pinv"], ALU.mult))
                    dve.tensor_tensor(arv[:, :, 0], q4(h["nkk"]), pbv[:, :, :, 0:CH], ALU.mult).then_inc(sem("scaled"), 1)
                    dve.tensor_tensor(arv[:, :, 1], q4(r), pbv[:, :, :, 1:CH + 1], ALU.mult).then_inc(sem("scaled"), 1)
                    dve.scalar_tensor_tensor(out=bk[:, :, 0, :], in0=h["nkk"].rearrange("p (c t) -> p c t", t=P), scalar=-1.0,
                                             in1=h["t2"].rearrange("p (c t) -> p c t", t=P), op0=ALU.mult, op1=ALU.mult).then_inc(sem("scaled"), 1)
                    dve.tensor_tensor(bk[:, :, 1, :], h["km"].rearrange("p (c t) -> p c t", t=P),
                                      h["pinv"].rearrange("p (c t) -> p c t", t=P), ALU.mult).then_inc(sem("scaled"), 1)
                    dve.wait_ge(sem("scaled"), it * 4 + 4)
                    pend = pbv[:, :, :, CH:CH + 1].to_broadcast([P, NCP, 2, CH])
                    dve.tensor_tensor(q4(h["kh"]), bkv[:, :, 1], pend, ALU.mult).then_inc(sem("ended"), 1)
                    dve.tensor_tensor(q4(h["bh"]), bkv[:, :, 0], pend, ALU.mult).then_inc(sem("ended"), 1)
                    dve.wait_ge(sem("bon_mm"), it + 1)
                    dve.tensor_tensor(h["bon"], ps[:, 4, :], v, ALU.mult).then_inc(sem("bon"), 1)
                    dve.wait_ge(sem("y_mm"), it * NCP)
                    if hf == 0:
                        dve.memset(sh[:, 0, :], 0.0).then_inc(sem("s0"), 1)
                    else:
                        dve.tensor_copy(sh[:, 0, :], sh[:, 8, :]).then_inc(sem("s0"), 1)
                    for q in range(NQ):
                        dve.wait_ge(sem("am_mm"), it * NQ + q + 1)
                        dve.tensor_tensor(am[:, q, :, :].rearrange("p a b -> p (a b)"), ps[:, 4 + q % 4, :], cm(C_M4, 4), ALU.mult).then_inc(sem("am"), 1)
                    for a in range(4):
                        hh, cpp = a // 2, a % 2
                        dve.wait_ge(sem("ark_mm"), it * 4 + a + 1)
                        dve.tensor_tensor(ark[:, hh, 2 * cpp:2 * cpp + 2, :], ps[:, a, 0:256].rearrange("p (a b) -> p a b", b=P),
                                          cm(C_M4 + 1).unsqueeze(1).to_broadcast([P, 2, P]), ALU.mult).then_inc(sem("ark"), 1)
                    dve.wait_ge(sem("x0"), it * 2 + 2)
                    for lev in range(NLEV):
                        for gq in range(2):
                            dve.wait_ge(sem("t1_mm"), it * 2 * NLEV + 2 * lev + gq + 1)
                            dve.tensor_tensor(T1[:, 4 * gq:4 * gq + 4, :], ps[:, gq, :].rearrange("p (a b) -> p a b", b=P),
                                              cm(C_LEV + lev).unsqueeze(1).to_broadcast([P, 4, P]), ALU.mult).then_inc(sem("t1"), 1)
                        for gq in range(2):
                            dve.wait_ge(sem("dx_mm"), it * 2 * NLEV + 2 * lev + gq + 1)
                            g4 = slice(4 * gq, 4 * gq + 4)
                            dve.tensor_tensor(XiT[:, g4, :], ps[:, 4 + gq, :].rearrange("p (a b) -> p a b", b=P), XiT[:, g4, :], ALU.add).then_inc(sem("xit"), 1)
                            if lev < NLEV - 1:
                                dve.tensor_tensor(Xi[:, g4, :], ps[:, 2 + gq, :].rearrange("p (a b) -> p a b", b=P), Xi[:, g4, :], ALU.add).then_inc(sem("xi"), 1)
                    dve.wait_ge(sem("s0"), it + 1)
                    for c in range(8):
                        dve.wait_ge(sem("s_mm"), it * 8 + c + 1)
                        for hh in range(2):
                            d = slice(64 * hh, 64 * hh + 64)
                            dve.scalar_tensor_tensor(out=sh[d, c + 1, d], in0=sh[d, c, d], scalar=pb[d, c * 65 + 64:c * 65 + 65],
                                                     in1=ps[d, 2 + c % 2, d], op0=ALU.mult, op1=ALU.add).then_inc(sem("s"), 1)
                        dve.wait_ge(sem("s"), it * 16 + 2 * c + 2)
                    dve.wait_ge(sem("ymean_mm"), it + 1)
                    dve.scalar_tensor_tensor(out=h["yc"], in0=ps[:, 6, :], scalar=-1.0 / HD, in1=h["y"], op0=ALU.mult, op1=ALU.add).then_inc(sem("yc"), 1)
                    dve.wait_ge(sem("sd"), it + 1)
                    tail = sem("dve_tail")

                    def tdone(ins, n):
                        ins.then_inc(tail, 1)
                        dve.wait_ge(tail, it * 4 + n)

                    tdone(dve.reciprocal(h["rs"], h["sd"]), 1)
                    tdone(dve.tensor_tensor(h["rs"], h["yc"], h["rs"], ALU.mult), 2)
                    tdone(dve.tensor_scalar(h["rs"], h["rs"], col(J_G), col(J_B), ALU.mult, ALU.add), 3)
                    tdone(dve.tensor_tensor(h["rs"], h["rs"], h["bon"], ALU.add), 4)
                    dve.wait_ge(sem("y_out"), it * 16)
                    dve.tensor_tensor(h["yo"], h["rs"], h["gg"], ALU.mult).then_inc(sem("y_ready"), 1)

            dve.wait_ge(sem("y_out"), 16 * 2 * NJ)
            dve.memset(aqk[:, 4, 0:CH], 0.0).then_inc(sem("pads"), 1)
            dve.memset(av[:, 0:CH], 0.0).then_inc(sem("pads"), 1)
            dve.memset(neg[:, 0:CH], NEG).then_inc(sem("pads"), 1)
            dve.memset(neg[:, CH:], 0.0).then_inc(sem("pads"), 1)
            dve.wait_ge(sem("pads"), 4)

            def head_norm(t, gain):
                for hf in range(2):
                    dve.wait_ge(sem("qsd"), t * 2 + hf + 1)
                    dve.reciprocal(asd[:, hf, :], asd[:, hf, :]).then_inc(sem("qrs"), 1)
                    dve.wait_ge(sem("qrs"), t * 2 + hf + 1)
                    w = aqk[:, t, CH + hf * HALF:CH + (hf + 1) * HALF]
                    dve.scalar_tensor_tensor(out=w, in0=w, scalar=vec[:, gain:gain + 1], in1=asd[:, hf, :],
                                             op0=ALU.mult, op1=ALU.mult).then_inc(sem("qn"), 1)

            with dve.Fori(0, 4) as t:
                head_norm(t, V_QG)
            head_norm(4, V_KG)

            with dve.Fori(0, 8) as i:
                for e in range(2):
                    c = i * 2 + e
                    dve.wait_ge(sem("s_qk"), c + 1)
                    dve.tensor_tensor(sb_s[:, e, :, :].rearrange("p (g a) b -> p g a b", g=2),
                                      ps[:, 2 * e:2 * e + 2, 0:256].rearrange("p g (a b) -> p g a b", b=P),
                                      neg[:, bass.ds(c * CH, P)].unsqueeze(1).unsqueeze(1).to_broadcast([P, 2, 2, P]), ALU.add).then_inc(sem("s_ev"), 1)
                    dve.wait_ge(sem("s_ev"), c + 1)
                    dve.tensor_reduce(sm[:, e, 0, :], sb_s[:, e, :, :], AX_X, ALU.max).then_inc(sem("s_small"), 1)
                    dve.wait_ge(sem("s_small"), c * 3 + 1)
                    dve.scalar_tensor_tensor(out=sm[:, e, 0, :], in0=sm[:, e, 0, :], scalar=HD ** -0.5,
                                             in1=vec[:, V_SINK:V_SINK + 4], op0=ALU.mult, op1=ALU.max).then_inc(sem("s_small"), 1)
                    dve.wait_ge(sem("s_small"), c * 3 + 2)
                    dve.tensor_tensor(sm[:, e, 2, :], vec[:, V_SINK:V_SINK + 4], sm[:, e, 0, :], ALU.subtract).then_inc(sem("s_small"), 1)
                    dve.wait_ge(sem("s_small"), c * 3 + 3)
                    dve.tensor_scalar(sm[:, e, 1, :], sm[:, e, 0, :], -1.0, None, ALU.mult).then_inc(sem("s_nmax"), 1)
                for e in range(2):
                    c = i * 2 + e
                    dve.wait_ge(sem("v_mm"), c + 1)
                    dve.wait_ge(sem("o_mm"), i * 2)
                    dve.tensor_copy(vn[:, e, :], ps[:, 6 + e, 0:P]).then_inc(sem("vn"), 1)
                    dve.wait_ge(sem("p_exp"), c * 4 + 4)
                    dve.wait_ge(sem("sink_exp"), c + 1)
                    dve.tensor_tensor(sm[:, e, 3, :], sm[:, e, 3, :], sm[:, e, 4, :], ALU.add).then_inc(sem("den"), 1)
                    dve.wait_ge(sem("den"), c * 2 + 1)
                    dve.reciprocal(sm[:, e, 4, :], sm[:, e, 3, :]).then_inc(sem("den"), 1)
                    dve.wait_ge(sem("den"), c * 2 + 2)
                    dve.tensor_tensor(pe_[:, e, :, :], pe_[:, e, :, :], sm[:, e, 4, :].unsqueeze(2).to_broadcast([P, 4, P]), ALU.mult).then_inc(sem("probs"), 1)
                for e in range(2):
                    c = i * 2 + e
                    dve.wait_ge(sem("o_mm"), c + 1)
                    dve.tensor_copy(aqk[:, 0:4, bass.ds(CH + c * CH, CH)], ps[:, 6 + e, P:P + 256].rearrange("p (a b) -> p a b", b=CH)).then_inc(sem("o_ev"), 1)

            with dve.Fori(0, KT // 2) as i:
                for p in range(2):
                    dve.wait_ge(sem("tile_mm"), T_OUT + i * 2 + p + 1)
                    dve.wait_ge(sem(f"xin_in{p}"), i * 16 + 16)
                    dve.scalar_tensor_tensor(out=X[:, i * 2 + p, :], in0=two(2 * p), scalar=mod[:, bass.ds(16 + i * 2 + p, 1)],
                                             in1=xin[:, p, :], op0=ALU.mult, op1=ALU.add).then_inc(sem("x1_made"), 1)
            dve.wait_ge(sem("x1_out"), 16 * KT)
            dve.wait_ge(sem("mod"), 2)
            norm(1)

            def up(f, par):
                for p in range(2):
                    c = V_CONV + (f * 2 + p) * 4
                    u = two(2 * p + 4 * par)
                    dve.wait_ge(sem("conv0"), f * 2 + p + 1)
                    dve.scalar_tensor_tensor(out=gu[:, p, 1:S], in0=u[:, 0:S - 1], scalar=vec[:, bass.ds(c + 1, 1)],
                                             in1=gu[:, p, 1:S], op0=ALU.mult, op1=ALU.add).then_inc(sem("conv1"), 1)
                    dve.wait_ge(sem("conv1"), f * 2 + p + 1)
                    dve.scalar_tensor_tensor(out=gu[:, p, 2:S], in0=u[:, 0:S - 2], scalar=vec[:, bass.ds(c, 1)],
                                             in1=gu[:, p, 2:S], op0=ALU.mult, op1=ALU.add).then_inc(sem("conv2"), 1)
                dve.wait_ge(sem("silu"), f + 1)
                dve.wait_ge(sem("conv2"), f * 2 + 2)
                dve.tensor_tensor(actb[:, f, :], gu[:, 0, :], gu[:, 1, :], ALU.mult).then_inc(sem("act_made"), 1)

            dve.wait_ge(sem("h_lo"), 2 * KT)
            with dve.Fori(0, NF // 2) as i:
                for par in range(2):
                    up(i * 2 + par, par)

            with dve.Fori(0, KT // 2) as i:
                for p in range(2):
                    dve.wait_ge(sem("down_mm"), i * 2 + p + 1)
                    dve.wait_ge(sem(f"x1_in{p}"), i * 16 + 16)
                    dve.wait_ge(sem(f"out_out{p}"), i * 16)
                    dve.scalar_tensor_tensor(out=yout[:, p, :], in0=two(2 * p), scalar=mod[:, bass.ds(40 + i * 2 + p, 1)],
                                             in1=x1in[:, p, :], op0=ALU.mult, op1=ALU.add).then_inc(sem("y2_made"), 1)

        @block.gpsimd
        def _(pool):
            def lo_rows(n):
                for t in range(KT):
                    pool.wait_ge(sem("h_hi"), n * KT + t + 1)
                    pool.tensor_tensor(LO[:, t, :], X[:, t, :], HI[:, t, :].bitcast(F32), ALU.subtract).then_inc(sem("h_lo"), 1)

            def split_lo(p, n):
                pool.wait_ge(sem("whi_made"), n)
                pool.tensor_tensor(wlo[:, p, :], wraw[:, p, :], whi[:, p, :].bitcast(F32), ALU.subtract).then_inc(sem("wlo_made"), 1)

            lo_rows(0)
            with pool.Fori(0, NIN // 2 + 1) as i:
                for p in range(2):
                    split_lo(p, i * 2 + p + 1)

            pool.wait_ge(sem("con_in"), 16)
            with pool.Fori(0, NJ) as j:
                for hf in range(2):
                    it = j * 2 + hf
                    pool.wait_ge(sem("am"), it * NQ + NQ)
                    pool.tensor_tensor(Xi[:, :, :], am[:, :, 2, :], cm(C_OFF1).unsqueeze(1).to_broadcast([P, NQ, P]), ALU.mult).then_inc(sem("x0a"), 1)
                    pool.tensor_tensor(XiT[:, :, :], am[:, :, 0, :], cm(C_OFF1T).unsqueeze(1).to_broadcast([P, NQ, P]), ALU.mult).then_inc(sem("x0a"), 1)
                    pool.wait_ge(sem("x0a"), it * 2 + 2)
                    pool.tensor_tensor(Xi[:, :, :], Xi[:, :, :], ident.unsqueeze(1).to_broadcast([P, NQ, P]), ALU.add).then_inc(sem("x0"), 1)
                    pool.tensor_tensor(XiT[:, :, :], XiT[:, :, :], ident.unsqueeze(1).to_broadcast([P, NQ, P]), ALU.add).then_inc(sem("x0"), 1)

            with pool.Fori(0, 8) as i:
                for e in range(2):
                    c = i * 2 + e
                    pool.wait_ge(sem("v_mm"), i * 2)
                    pool.wait_ge(sem("s_qk"), i * 2)
                    pool.wait_ge(sem("qn"), 10)
                    pool.wait_ge(sem("pads"), 4)
                    pool.tensor_copy(stg[:, e, 0:256].rearrange("p (a b) -> p a b", b=CH), aqk[:, 0:4, bass.ds(CH + c * CH, CH)]).then_inc(sem("staged"), 1)
                    pool.tensor_copy(stg[:, e, 256:384], aqk[:, 4, bass.ds(c * CH, P)]).then_inc(sem("staged"), 1)
                    pool.tensor_copy(stg[:, e, 384:512], av[:, bass.ds(c * CH, P)]).then_inc(sem("staged"), 1)

            with pool.Fori(0, KT // 2) as i:
                for p in range(2):
                    pool.wait_ge(sem("mix_hi"), i * 2 + p + 1)
                    pool.tensor_tensor(LO[:, i * 2 + p, :], mst[:, p, :], HI[:, i * 2 + p, :].bitcast(F32), ALU.subtract).then_inc(sem("mix_split"), 1)

            with pool.Fori(0, KT // 2) as i:
                for p in range(2):
                    split_lo(p, T_OUT + 2 + i * 2 + p + 1)
            lo_rows(1)
            with pool.Fori(0, NF - 1) as i:
                for p in range(2):
                    split_lo(p, T_UP + 2 + i * 2 + p + 1)

        @block.tensor
        def _(pe):
            def ssq(n):
                for t in range(KT):
                    pe.wait_ge(sem("sq"), n * KT + t + 1)
                    for hf in range(2):
                        last = pe.matmul(ps[:, 4 + hf, :], ones, sqt[:, t % 2, hf * HALF:(hf + 1) * HALF], start=(t == 0), stop=(t == KT - 1))
                    last.then_inc(sem("ssq_mm"), 1)

            def tile(p, b):
                for k in range(KT):
                    wh, wl = whi[:, p, k * P:(k + 1) * P], wlo[:, p, k * P:(k + 1) * P]
                    for n, (w, rows) in enumerate(((wh, HI), (wh, LO), (wl, HI))):
                        for hf in range(2):
                            last = pe.matmul(ps[:, b + hf, :], w, rows[:, k, hf * HALF:(hf + 1) * HALF],
                                             start=(k == 0 and n == 0), stop=(k == KT - 1 and n == 2))
                last.then_inc(sem("tile_mm"), 1)

            pe.wait_ge(sem("con_in"), 16)
            ssq(0)
            pe.wait_ge(sem("h_lo"), KT)
            with pe.Fori(0, NIN // 2) as i:
                for p in range(2):
                    pe.wait_ge(sem("wlo_made"), i * 2 + p + 1)
                    pe.wait_ge(sem("mixed"), i * 2)
                    tile(p, 2 * p)

            pe.wait_ge(sem("lora_act"), 2)
            pe.wait_ge(sem("mixed"), NIN)
            with pe.Fori(0, NJ) as j:
                for hf in range(2):
                    it = j * 2 + hf
                    tok = slice(hf * HALF, (hf + 1) * HALF)
                    pe.wait_ge(sem("rkv_in"), j * 48 + 48)
                    pe.wait_ge(sem("y_ready"), it)
                    pe.matmul(ps[:, 0, :], lw[0:DL, 0, :], lwa[0:DL, tok], start=True, stop=True).then_inc(sem("lora_mm"), 1)
                    pe.matmul(ps[:, 1, :], lw[DL:DL + IL, 0, :], lwa[DL:DL + IL, tok], start=True, stop=True).then_inc(sem("lora_mm"), 1)
                    pe.matmul(ps[:, 2, :], lw[0:GL, 1, :], lg[0:GL, tok], start=True, stop=True).then_inc(sem("lora_mm"), 1)
                    pe.wait_ge(sem("ksq"), it + 1)
                    pe.matmul(ps[:, 3, :], blk, half["ksq"][:, :], start=True, stop=True).then_inc(sem("kss_mm"), 1)
                    pe.wait_ge(sem("rk_prod"), it + 1)
                    pe.matmul(ps[:, 4, :], blk, half["t3"][:, :], start=True, stop=True).then_inc(sem("bon_mm"), 1)
                    pe.wait_ge(sem("scaled"), it * 4 + 4)
                    pe.wait_ge(sem("ended"), it * 2 + 2)
                    pe.wait_ge(sem("lora_ev"), it * 3 + 3)
                    pe.wait_ge(sem("nrm"), it + 1)
                    for cp in range(NCP):
                        t128 = slice(cp * P, (cp + 1) * P)
                        srcs = (rkv[:, 2, hf * HALF + cp * P:hf * HALF + (cp + 1) * P], half["kh"][:, t128], half["bh"][:, t128], ar[:, cp, 0, :])
                        for a, src in enumerate(srcs):
                            last = pe.transpose(ps[:, cp, a * P:(a + 1) * P], src, ident)
                        last.then_inc(sem("nat_mm"), 1)
                    pe.wait_ge(sem("bon"), it + 1)
                    for q in range(NQ):
                        cp, hh = q // 2, q % 2
                        r = slice(64 * hh, 64 * hh + 64)
                        if q >= 4:
                            pe.wait_ge(sem("am"), it * NQ + q - 3)
                        b = 4 + q % 4
                        pe.matmul(ps[:, b, 0:256], bk[r, cp, 0, :], ar[r, cp, :, :].rearrange("p a b -> p (a b)"), start=True, stop=True, skip_group_check=True)
                        pe.matmul(ps[:, b, 256:512], ar[r, cp, 0, :], bk[r, cp, :, :].rearrange("p a b -> p (a b)"), start=False, stop=True, skip_group_check=True).then_inc(sem("am_mm"), 1)
                    for a in range(4):
                        hh, cpp = a // 2, a % 2
                        r = slice(64 * hh, 64 * hh + 64)
                        pe.wait_ge(sem("nat"), it * NCP + a + 1)
                        for n in range(2):
                            cp = 2 * cpp + n
                            last = pe.matmul(ps[:, a, n * P:(n + 1) * P], bk[r, cp, 1, :], ar[r, cp, 1, :], start=(n == 0), stop=True, skip_group_check=True)
                        last.then_inc(sem("ark_mm"), 1)
                    pe.wait_ge(sem("x0"), it * 2 + 2)
                    pe.wait_ge(sem("ark"), it * 4 + 4)
                    pe.wait_ge(sem("am"), it * NQ + NQ)
                    for lev in range(NLEV):
                        for gq in range(2):
                            if lev:
                                pe.wait_ge(sem("xi"), (it * (NLEV - 1) + lev - 1) * 2 + gq + 1)
                            for n in range(4):
                                q = 4 * gq + n
                                last = pe.matmul(ps[:, gq, n * P:(n + 1) * P], am[:, q, 0, :], Xi[:, q, :], start=(n == 0), stop=True, skip_group_check=True)
                            last.then_inc(sem("t1_mm"), 1)
                        for gq in range(2):
                            pe.wait_ge(sem("t1"), it * 2 * NLEV + 2 * lev + gq + 1)
                            if lev:
                                pe.wait_ge(sem("xit"), (it * NLEV + lev - 1) * 2 + gq + 1)
                            for n in range(4):
                                q = 4 * gq + n
                                if lev < NLEV - 1:
                                    pe.matmul(ps[:, 2 + gq, n * P:(n + 1) * P], XiT[:, q, :], T1[:, q, :], start=(n == 0), stop=True, skip_group_check=True)
                                last = pe.matmul(ps[:, 4 + gq, n * P:(n + 1) * P], T1[:, q, :], XiT[:, q, :], start=(n == 0), stop=True, skip_group_check=True)
                            last.then_inc(sem("dx_mm"), 1)
                    for cp in range(NCP):
                        pe.wait_ge(sem("xit"), it * 2 * NLEV + 2 * (NLEV - 1) + cp // 2 + 1)
                        if cp >= 2:
                            pe.wait_ge(sem("wd"), it * NCP + cp - 1)
                        b = 6 + cp % 2
                        for hh in range(2):
                            q = 2 * cp + hh
                            pe.matmul(ps[64 * hh:64 * hh + 64, b, 0:P], nat[:, cp, 3, 64 * hh:64 * hh + 64], XiT[:, q, :], start=True, stop=True, skip_group_check=True)
                        for hh in range(2):
                            q = 2 * cp + hh
                            last = pe.matmul(ps[:, b, (1 + hh) * P:(2 + hh) * P], am[:, q, 3, :], XiT[:, q, :], start=False, stop=True, skip_group_check=True)
                        last.then_inc(sem("wd_mm"), 1)
                    pe.wait_ge(sem("s0"), it + 1)
                    for c in range(8):
                        cp, e = c // 2, c % 2
                        r = slice(64 * e, 64 * e + 64)
                        ub = cp % 2
                        if e == 0:
                            pe.wait_ge(sem("wd"), it * NCP + cp + 1)
                            if cp >= 2:
                                pe.wait_ge(sem("u"), it * 8 + 2 * (cp - 1))
                            for hh in range(2):
                                pe.matmul(ps[:, ub, 64 * hh:64 * hh + 64], wd_[:, cp, 1 + hh, :], nat[:, cp, 0, 64 * hh:64 * hh + 64], start=(hh == 0), stop=True, skip_group_check=True)
                        if c:
                            pe.wait_ge(sem("s"), it * 16 + 2 * c)
                        pe.matmul(ps[r, ub, 0:P], wd_[:, cp, 0, r], sh[:, c, :], start=False, stop=True, skip_group_check=True).then_inc(sem("u_mm"), 1)
                        pe.matmul(ps[:, 2 + c % 2, 0:P], nat[r, cp, 1, :], nat[r, cp, 0, :], start=True, stop=False, skip_group_check=True)
                        pe.wait_ge(sem("u"), it * 8 + c + 1)
                        pe.matmul(ps[:, 2 + c % 2, 0:P], nat[r, cp, 2, :], us[r, cp, :], start=False, stop=True, skip_group_check=True).then_inc(sem("s_mm"), 1)
                    for cp in range(NCP):
                        b = 4 + cp % 2
                        if cp >= 2:
                            pe.wait_ge(sem("y"), it * NCP + cp - 1)
                        for e in range(2):
                            pe.matmul(ps[:, b, 64 * e:64 * e + 64], sh[:, 2 * cp + e, :], ar[:, cp, 1, 64 * e:64 * e + 64], start=(e == 0), stop=False, skip_group_check=True)
                        for hh in range(2):
                            q, d = 2 * cp + hh, slice(64 * hh, 64 * hh + 64)
                            pe.matmul(ps[d, b, 0:P], us[:, cp, d], am[:, q, 1, :], start=False, stop=False, skip_group_check=True)
                            last = pe.matmul(ps[d, b, 0:P], nat[:, cp, 0, d], ark[:, hh, cp, :], start=False, stop=True, skip_group_check=True)
                        last.then_inc(sem("y_mm"), 1)
                    pe.wait_ge(sem("y"), it * NCP + NCP)
                    pe.matmul(ps[:, 6, :], blk, half["y"][:, :], start=True, stop=True).then_inc(sem("ymean_mm"), 1)
                    pe.wait_ge(sem("ysq"), it + 1)
                    pe.matmul(ps[:, 7, :], blk, half["ysq"][:, :], start=True, stop=True).then_inc(sem("yvar_mm"), 1)

            pe.wait_ge(sem("y_ready"), 2 * NJ)
            with pe.Fori(0, 5) as t:
                for hf in range(2):
                    pe.wait_ge(sem("qsq"), t * 2 + hf + 1)
                    pe.wait_ge(sem("qsd"), t * 2)
                    pe.matmul(ps[:, hf, :], blk, asq[:, hf, :], start=True, stop=True).then_inc(sem("qn_mm"), 1)
            pe.wait_ge(sem("qn"), 10)
            with pe.Fori(0, 8) as i:
                for e in range(2):
                    c = i * 2 + e
                    pe.wait_ge(sem("staged"), c * 3 + 3)
                    pe.wait_ge(sem("s_ev"), i * 2)
                    for g in range(2):
                        r = slice(64 * g, 64 * g + 64)
                        for pp in range(2):
                            last = pe.matmul(ps[:, 2 * e + g, pp * P:(pp + 1) * P], stg[r, e, pp * P:(pp + 1) * P], stg[r, e, 256:384],
                                             start=(pp == 0), stop=True, skip_group_check=True)
                    last.then_inc(sem("s_qk"), 1)
                    pe.wait_ge(sem("o_ev"), i * 2)
                    pe.transpose(ps[:, 6 + e, 0:P], stg[:, e, 384:512], ident).then_inc(sem("v_mm"), 1)
                for e in range(2):
                    c = i * 2 + e
                    pe.wait_ge(sem("probs"), c + 1)
                    pe.wait_ge(sem("pt"), i * 2)
                    for g in range(4):
                        last = pe.transpose(ps[:, 4 + e, g * P:(g + 1) * P], pe_[:, e, g, :], ident)
                    last.then_inc(sem("p_mm"), 1)
                for e in range(2):
                    c = i * 2 + e
                    pe.wait_ge(sem("pt"), c + 1)
                    pe.wait_ge(sem("vn"), c + 1)
                    for g in range(2):
                        last = pe.matmul(ps[64 * g:64 * g + 64, 6 + e, P:P + 256], vn[:, e, 64 * g:64 * g + 64],
                                         pt[:, e, 2 * g:2 * g + 2, :].rearrange("p a b -> p (a b)"), start=True, stop=True, skip_group_check=True)
                    last.then_inc(sem("o_mm"), 1)

            pe.wait_ge(sem("o_ev"), 16)
            pe.wait_ge(sem("mix_split"), KT)
            with pe.Fori(0, KT // 2) as i:
                for p in range(2):
                    pe.wait_ge(sem("wlo_made"), T_OUT + i * 2 + p + 1)
                    pe.wait_ge(sem("x1_made"), i * 2)
                    tile(p, 2 * p)
            ssq(1)
            pe.wait_ge(sem("h_lo"), 2 * KT)
            with pe.Fori(0, NF // 2) as i:
                for par in range(2):
                    for p in range(2):
                        f = i * 2 + par
                        pe.wait_ge(sem("wlo_made"), T_UP + f * 2 + p + 1)
                        pe.wait_ge(sem("act_made"), i * 2)
                        tile(p, 2 * p + 4 * par)
            pe.wait_ge(sem("act_made"), NF)
            with pe.Fori(0, KT // 2) as i:
                for p in range(2):
                    pe.wait_ge(sem(f"wd_in{p}"), i * 16 + 16)
                    pe.wait_ge(sem("y2_made"), i * 2)
                    for k in range(NF):
                        for hf in range(2):
                            last = pe.matmul(ps[:, 2 * p + hf, :], wdn[:, p, k * P:(k + 1) * P], actb[:, k, hf * HALF:(hf + 1) * HALF],
                                             start=(k == 0), stop=(k == NF - 1))
                    last.then_inc(sem("down_mm"), 1)


def kernel(**inputs):
    import concourse.bacc as _bacc
    from concourse import mybir as _mybir
    from concourse.bass_utils import run_bass_kernel_spmd as _run

    A = {k: np.asarray(v) for k, v in inputs.items()}

    def tiles(w):
        k, n = w.shape
        return np.ascontiguousarray(w.reshape(k // P, P, n // P, P).transpose(2, 1, 0, 3).reshape(n // P, P, k))

    def cols(v):
        return np.ascontiguousarray(v.reshape(-1, P).T)

    w0, mu0 = A["w_in0"], A["shift_mu0"]
    ro = 768
    zw = lambda n: np.zeros((D, n), np.float32)
    q_heads = [h for t in range(4) for h in (t, 4 + t)]
    qcols = np.concatenate([np.arange(h * HD, (h + 1) * HD) for h in q_heads])
    parts, mus = [], []
    lo = 3 * RW
    parts += [w0[:, ro + lo:ro + lo + DL + IL], zw(P - DL - IL), w0[:, ro + lo + DL + IL:ro + lo + DL + IL + GL], zw(P - GL)]
    mus += [mu0[lo:lo + DL + IL], np.zeros(P - DL - IL, np.float32), mu0[lo + DL + IL:], np.zeros(P - GL, np.float32)]
    for j in range(NJ):
        for a in range(3):
            s = a * RW + j * P
            parts.append(w0[:, ro + s:ro + s + P])
            mus.append(mu0[s:s + P])
    parts += [w0[:, qcols], w0[:, RW:ro]]
    mus.append(np.zeros(768, np.float32))
    win = tiles(np.concatenate(parts, axis=1))
    mu = cols(np.concatenate(mus))

    sinks = A["attn_sinks"][0]
    scol = np.zeros((P, 4), np.float32)
    for g in range(2):
        for pp in range(2):
            for m in range(2):
                scol[64 * m:64 * m + 64, g * 2 + pp] = sinks[g * 4 + pp * 2 + m]
    full = lambda v: np.full((P, 1), v, np.float32)
    cw, cb = A["ffn_conv_w"][0], A["ffn_conv_b"][0]
    conv = np.stack([cw[0], cw[1], cw[2], cb]).reshape(4, 2, NF, P).transpose(3, 2, 1, 0).reshape(P, NF * 8)
    vecs = np.concatenate([mu, cols(A["ada_b"][0]), cols(A["norm_mix_g"][0]), cols(A["norm_ffn_g"][0]),
                           np.tile(A["attn_q_gain"][0], 2)[:, None], np.tile(A["attn_k_gain"][0], 2)[:, None],
                           full(RMS_EPS), full(LNX_EPS), scol, conv], axis=1)
    assert vecs.shape[1] == V_N
    loraw = np.zeros((NJ, P, 2, P), np.float32)
    for j in range(NJ):
        c = slice(j * P, (j + 1) * P)
        loraw[j, 0:DL, 0] = A["rwkv_w_up"][0][:, c]
        loraw[j, DL:DL + IL, 0] = A["rwkv_a_up"][0][:, c]
        loraw[j, 0:GL, 1] = A["rwkv_g_up"][0][:, c]
    jn = [A["rwkv_w0"][0], A["rwkv_a0"][0], A["rwkv_k_k"][0], A["rwkv_k_a"][0], A["rwkv_r_k"][0].reshape(-1),
          A["rwkv_lnx_g"][0], A["rwkv_lnx_b"][0], np.zeros(RW, np.float32)]
    jvecs = np.ascontiguousarray(np.stack(jn, axis=-1).reshape(NJ, P, J_N))
    wo = A["w_out"][0]
    wo = np.concatenate([wo[:RW], wo[RW:][qcols]], axis=0)
    up = A["ffn_w_up"][0].reshape(D, 2, NF, P).transpose(0, 2, 1, 3).reshape(D, 2 * FF)
    arrays = {
        "xT": np.ascontiguousarray(A["x"][0].T).reshape(KT, P, S),
        "condb": np.ascontiguousarray(np.broadcast_to(A["c"], (P, D))),
        "adaw": np.ascontiguousarray(A["ada_w"][0].T).reshape(NADA, P, D),
        "vecs": np.ascontiguousarray(vecs.astype(np.float32)),
        "consts": constants(),
        "win": win, "loraw": loraw, "jvecs": jvecs,
        "wout": tiles(wo), "wup": tiles(up), "wdown": tiles(A["ffn_w_down"][0]),
    }
    nc = _bacc.Bacc("TRN2", target_bir_lowering=False, num_devices=1)
    aps = {}
    for name, a in arrays.items():
        aps[name] = nc.dram_tensor(name, a.shape, _mybir.dt.from_np(a.dtype), kind="ExternalInput").ap()
    aps["outT"] = nc.dram_tensor("outT", (KT, P, S), F32, kind="ExternalOutput").ap()
    build(nc, **aps)
    r = _run(nc, [arrays], core_ids=[0])
    y = r.results[0]["outT"]
    return np.ascontiguousarray(y.reshape(D, S).T).reshape(1, S, D)
```

```python
import math
from contextlib import ExitStack

import numpy as np

import concourse.bass as bass
from concourse import mybir

F32 = mybir.dt.float32
F32R = mybir.dt.float32r
ALU = mybir.AluOpType
ACT = mybir.ActivationFunctionType
AX_X = mybir.AxisListType.X

P = 128
D = 1024
S = 1024
KT = D // P
HALF = 512
CH = 64
HD = 64
RW = 512
NJ = RW // P
FF = 2816
NF = FF // P
NIN = 20
NADA = 48
NATT = 6
RMS_EPS = 1e-6
LNX_EPS = 64e-5
DEC = math.exp(-0.5)
NEG = -1e30
DL, IL, GL = 32, 32, 96
NCP = HALF // P
NLEV = 5
NQ = 2 * NCP

V_MU, V_ADAB, V_GMIX, V_GFFN = 0, 20, 68, 76
V_GAIN, V_EPS, V_LEPS, V_SINK = 84, 89, 90, 91
V_TINY, V_CONV = 95, 96
V_N = V_CONV + NF * 2 * 4
J_W0, J_A0, J_KK, J_KA, J_RK, J_G, J_B, J_N = 0, 1, 2, 3, 4, 5, 6, 8
C_ID, C_BLK, C_ONE, C_M4, C_OFF1, C_OFF1T, C_LEV, C_RST = 0, 1, 2, 3, 7, 8, 9, 14
C_N = C_RST + 4


AHEAD = {
    "evac": 2, "x1_made": 2, "act_made": 2, "y2_made": 2, "mix_lo": 1, "mix_lo_odd": 1, "ada_used": 4, "convolved": 4,
    "o_ev": 2, "o_mm": 2, "p_mm": 2, "pt": 2, "qn": 2, "qn_mm": 2, "qsd": 2, "s_ev": 2, "s_qk": 2,
    "v_mm": 2, "vn": 1, "proj_out": 1, "y_out": 1,
    "y_mm": 8,
}


def constants():
    t = np.arange(P)
    same = (t[:, None] // CH) == (t[None, :] // CH)
    lower = same & (t[:, None] > t[None, :])
    mats = [np.eye(P), same, np.ones((P, P)),
            lower.T, same & (t[:, None] <= t[None, :]), lower, lower]
    offs = []
    for m in (1, 2, 4, 8, 16, 32):
        pair = (t[:, None] // (2 * m)) == (t[None, :] // (2 * m))
        offs.append(pair & ((t[:, None] // m) % 2 == 1) & ((t[None, :] // m) % 2 == 0))
    mats += [offs[0], offs[0].T] + offs[1:]
    reset = np.tile((np.arange(HALF) % CH != 0)[None, :], (P, 1))
    return np.concatenate([m.astype(np.float32) for m in mats] + [reset.astype(np.float32)], axis=1)


def build(nc, xT, condb, adaw, vecs, consts, win, loraw, jvecs, wout, wup, wdown, outT):
    with ExitStack() as ctx:
        sems = {}

        def sem(name):
            if name not in sems:
                sems[name] = ctx.enter_context(nc.semaphore(name))
            return sems[name]

        def at(name, kb, shape, dt=F32):
            return nc.alloc_sbuf_tensor_at(name, shape, dt, offset=int(kb * 1024))

        projD = nc.dram_tensor("projD", (NIN - NATT, P, S), F32, kind="Internal").ap()
        mixD = nc.dram_tensor("mixD", (KT, P, S), F32, kind="Internal").ap()
        x1D = nc.dram_tensor("x1D", (KT, P, S), F32, kind="Internal").ap()

        A0 = -(-nc.sbuf_base // 32) * 32 / 1024.0
        ctx.enter_context(nc.sbuf_tensor("arena", [P, 206 * 256], F32))
        vec = at("vec", A0 + 0, [P, V_N])
        jv = at("jv", A0 + 2.5, [P, NJ * J_N])
        omu = at("omu", A0 + 1.5, [P, NIN])
        mod = at("mod", A0 + 1.75, [P, NADA])
        modA = at("modA", A0 + 2, [P, 2 * KT])
        omka = at("omka", A0 + 2.25, [P, 1])
        con = at("con", A0 + 3, [P, C_N * P])
        wraw = at("wraw", A0 + 13, [P, 2, 1024])
        whi = at("whi", A0 + 21, [P, 2, 1024], F32R)
        wlo = at("wlo", A0 + 29, [P, 2, 1024], F32R)
        B = A0 + 37
        HI = at("HI", B, [P, KT, S], F32R)
        LO = at("LO", B + 32, [P, KT, S], F32R)
        X = at("X", B + 64, [P, KT, S])
        adat = at("adat", B + 96, [P, 4, 1024])
        cond = at("cond", B + 112, [P, 1024])
        junk = at("junk", B + 116, [P, 1024])
        sqt = at("sqt", B + 120, [P, 2, S])
        rstd = at("rstd", B + 128, [P, S])
        pr = at("pr", B + 136, [P, 2, S])
        mst = at("mst", B + 96, [P, 2, S])
        xin = at("xin", B + 104, [P, 2, S])
        actb = at("actb", B + 64, [P, NF, S])
        gu = at("gu", B + 152, [P, 2, S])
        actH = [at(f"actH{k}", A0 + 13 + 4 * k, [P, S], F32R) for k in range(NF)]
        actL = [at(f"actL{k}", B + 64 + 4 * k, [P, S], F32R) for k in range(NF)]
        DW = NF // 2 * P
        draw = [at("draw0", A0 + 3, [P, DW]), at("draw1", B + 157.5, [P, DW])]
        dlo = [at("dlo0", A0 + 3, [P, DW], F32R), at("dlo1", B + 157.5, [P, DW], F32R)]
        dhi = [at("dhi0", B + 163, [P, DW], F32R), at("dhi1", B + 152, [P, DW], F32R)]
        x1in = at("x1in", A0 + 8.5, [P, S])
        o = [B]

        def alloc(name, shape):
            words = 1
            for n in shape[1:]:
                words *= n
            t = at(name, o[0], shape)
            o[0] += words * 4 / 1024.0
            return t

        lwa = alloc("lwa", [P, S])
        lg = alloc("lg", [P, S])
        lw = alloc("lw", [P, 2, P])
        rkv = alloc("rkv", [P, 3, S])
        half = {n: alloc(n, [P, HALF])[:, :] for n in (
            "sg", "aa", "gg", "cs", "pinv", "kk", "ksq", "nrm", "km", "t2", "kh", "bh", "t3", "bon",
            "y", "yc", "ysq", "yo")}
        pb = alloc("pb", [P, 8 * 65])
        ar = alloc("ar", [P, NCP, 2, P])
        bk = alloc("bk", [P, NCP, 2, P])
        nat = [alloc(f"nat{i}", [P, NCP, 4, P]) for i in range(2)]
        am = [alloc(f"am{i}", [P, NQ, 4, P]) for i in range(2)]
        ark = [alloc(f"ark{i}", [P, 2, NCP, P]) for i in range(2)]
        wd_ = [alloc(f"wd{i}", [P, NCP, 3, P]) for i in range(2)]
        rtz = [alloc(f"rtz{i}", [P, NCP, P])  for i in range(2)]
        g1 = [alloc(f"g1{i}", [P, HALF]) for i in range(2)]
        g2 = [alloc(f"g2{i}", [P, HALF]) for i in range(2)]
        pend = [alloc(f"pend{i}", [P, 8]) for i in range(2)]
        Xi = alloc("Xi", [P, NQ, P])
        XiT = alloc("XiT", [P, NQ, P])
        T1 = alloc("T1", [P, NQ, P])
        sh = alloc("sh", [P, 9, P])
        us = alloc("us", [P, NCP, P])
        assert o[0] <= A0 + 206, o[0]
        o[0] = B + 64
        aqkv = alloc("aqkv", [P, NATT, CH + S])
        asq = alloc("asq", [P, 2, HALF])
        assert o[0] <= B + 96
        o[0] = B + 144
        asd = alloc("asd", [P, 2, HALF])
        stg = alloc("stg", [P, 2, 512])
        sb_s = alloc("sb_s", [P, 2, 4, P])
        pe_ = alloc("pe_", [P, 2, 4, P])
        pt = alloc("pt", [P, 2, 4, P])
        vn = alloc("vn", [P, 2, P])
        sm = alloc("sm", [P, 2, 5, 4])
        negc = alloc("negc", [P, P])
        assert o[0] <= B + 168.5
        ps = ctx.enter_context(nc.psum_tensor("ps", [P, 8, HALF], F32))

        def cm(n, k=1):
            return con[:, n * P:(n + k) * P]

        ident, blk, ones = cm(C_ID), cm(C_BLK), cm(C_ONE)

        def two(b):
            return ps[:, b:b + 2, :].rearrange("p a b -> p (a b)")

        T_OUT, T_UP = NIN, NIN + KT

        block = ctx.enter_context(nc.Block())

        @block.sync
        def _(sp):
            for name, n in AHEAD.items():
                for full in ((name + "0", name + "1") if name.endswith("_out") and name != "y_out" else (name,)):
                    sp.sem_inc(sem(full), n)
            sp.dma_start(vec[:, :], vecs).then_inc(sem("vec_in"), 16)
            sp.dma_start(cond[:, :], condb).then_inc(sem("cond_in"), 16)

            def load_ada(col, s):
                sp.wait_ge(sem("ada_used"), col - 3 + AHEAD["ada_used"])
                sp.dma_start(adat[:, s, :], adaw[col]).then_inc(sem(f"ada_in{s}"), 16)

            for t in range(KT):
                sp.dma_start(X[:, t, :], xT[t]).then_inc(sem(f"x_in{t}"), 16)
                if t == 3:
                    sp.dma_start(con[:, :], consts).then_inc(sem("con_in"), 16)
            with sp.Fori(0, 4) as i:
                for s in range(4):
                    load_ada(i * 4 + s, s)

            def load_w(src, tile, p, n):
                sp.wait_ge(sem("wlo_made"), n)
                sp.dma_start(wraw[:, p, :], src[tile]).then_inc(sem(f"w_in{p}"), 16)

            for p in range(2):
                sp.dma_start(wraw[:, p, :], win[p]).then_inc(sem(f"w_in{p}"), 16)

            def in_proj(i, ada=False, store=False, last=False):
                for p in range(2):
                    if ada:
                        for s in range(4):
                            load_ada(16 + i * 8 + 4 * p + s, s)
                    if not last:
                        load_w(win, i * 2 + 2 + p, p, i * 2 + 1 + p)
                    else:
                        load_w(wout, p, p, i * 2 + 1 + p)
                    if store:
                        sp.wait_ge(sem("evac"), i * 2 + 1 + p + AHEAD["evac"])
                        sp.dma_start(projD[i * 2 + p - NATT], pr[:, p, :]).then_inc(sem(f"proj_out{p}"), 16)

            with sp.Fori(0, 3) as i:
                in_proj(i, ada=True)
            in_proj(3, ada=True, store=True)
            with sp.Fori(4, 9) as i:
                in_proj(i, store=True)
            in_proj(9, store=True, last=True)
            for p in range(2):
                sp.wait_ge(sem(f"proj_out{p}"), 16 * (NIN - NATT) // 2 + AHEAD["proj_out"])
            sp.wait_ge(sem("o_ev"), 16 + AHEAD["o_ev"])
            for t in range(4):
                sp.dma_start(mixD[4 + t], aqkv[:, t, CH:]).then_inc(sem("o_out"), 16)
            sp.wait_ge(sem("tile_mm"), NIN)
            sp.dma_start(lwa[:, :], projD[0]).then_inc(sem("lora_in"), 16)
            sp.dma_start(lg[:, :], projD[1]).then_inc(sem("lora_in"), 16)
            sp.dma_start(jv[:, :], jvecs).then_inc(sem("jv_in"), 16)

            def load_pair(j):
                sp.dma_start(rkv[:, :, :], projD[bass.ds(j * 3 + 2, 3)].rearrange("a p s -> p a s")).then_inc(sem("rkv_in"), 16)
                sp.dma_start(lw[:, :, :], loraw[j]).then_inc(sem("rkv_in"), 16)

            def store_y(j, hf):
                sp.wait_ge(sem("y_ready"), j * 2 + hf + 1)
                sp.dma_start(mixD[j, :, hf * HALF:(hf + 1) * HALF], half["yo"]).then_inc(sem("y_out"), 16)

            def rwkv(j, last=False):
                if not last:
                    it = j * 2 + 1
                    sp.wait_ge(sem("x0"), it * 4 + 1)
                    load_pair(j + 1)
                store_y(j, 0)

            load_pair(0)
            rwkv(0)
            with sp.Fori(1, NJ - 1) as j:
                store_y(j - 1, 1)
                rwkv(j)
            store_y(NJ - 2, 1)
            rwkv(NJ - 1, True)
            store_y(NJ - 1, 1)
            sp.wait_ge(sem("y_out"), 16 * 2 * NJ + AHEAD["y_out"])
            with sp.Fori(0, KT // 2) as i:
                for p in range(2):
                    sp.wait_ge(sem("mix_lo_odd" if p else "mix_lo"), i + AHEAD.get("mix_lo_odd" if p else "mix_lo", 0))
                    sp.dma_start(mst[:, p, :], mixD[i * 2 + p]).then_inc(sem(f"mix_in{p}"), 16)

            def out_proj(i, last):
                for p in range(2):
                    sp.wait_ge(sem("x1_made"), i * 2 + p - 1 + AHEAD["x1_made"])
                    sp.dma_start(xin[:, p, :], xT[i * 2 + p]).then_inc(sem(f"xin_in{p}"), 16)
                for p in range(2):
                    if not last:
                        load_w(wout, i * 2 + 2 + p, p, i * 2 + 1 + p + T_OUT)
                    else:
                        load_w(wup, p, p, i * 2 + 1 + p + T_OUT)
                    sp.wait_ge(sem("x1_made"), i * 2 + p + 1 + AHEAD["x1_made"])
                    sp.dma_start(x1D[i * 2 + p], X[:, bass.ds(i * 2 + p, 1), :].rearrange("p a s -> p (a s)") ).then_inc(sem("x1_store"), 16)

            with sp.Fori(0, KT // 2 - 1) as i:
                out_proj(i, False)
            out_proj(KT // 2 - 1, True)
            def load_down(d, hf):
                sp.dma_start(draw[hf][:, :], wdown[d, :, hf * DW:(hf + 1) * DW]).then_inc(sem(f"wd_in{hf}"), 16)

            sp.wait_ge(sem("rstd"), 2)
            load_down(0, 0)
            sp.wait_ge(sem("x1_store"), 16 * KT)
            sp.dma_start(x1in[:, :], x1D[0]).then_inc(sem("x1_in"), 16)
            with sp.Fori(0, NF - 1) as f:
                for p in range(2):
                    load_w(wup, f * 2 + 2 + p, p, f * 2 + 1 + p + T_UP)
            sp.wait_ge(sem("act_made"), NF + AHEAD["act_made"])
            load_down(0, 1)
            with sp.Fori(0, KT - 1) as d:
                for hf in range(2):
                    sp.wait_ge(sem("down_mm"), d * 2 + hf + 1)
                    load_down(d + 1, hf)
                sp.wait_ge(sem("y2_made"), d + 1 + AHEAD["y2_made"])
                sp.dma_start(outT[d], x1in[:, :]).then_inc(sem("out_out"), 16)
                sp.wait_ge(sem("out_out"), d * 16 + 16)
                sp.dma_start(x1in[:, :], x1D[d + 1]).then_inc(sem("x1_in"), 16)
            sp.wait_ge(sem("y2_made"), KT + AHEAD["y2_made"])
            sp.dma_start(outT[KT - 1], x1in[:, :]).then_inc(sem("out_out"), 16)
            sp.wait_ge(sem("out_out"), 16 * KT)

        @block.scalar
        def _(act):
            def norm(n):
                for t in range(KT):
                    if n == 0:
                        act.wait_ge(sem(f"x_in{t}"), 16)
                    else:
                        act.wait_ge(sem("x1_made"), t + 1 + AHEAD["x1_made"])
                    if t >= 2:
                        act.wait_ge(sem("ssq_mm"), n * KT + t - 1)
                    act.activation(sqt[:, t % 2, :], X[:, t, :], ACT.Square).then_inc(sem("sq"), 1)
                act.wait_ge(sem("ssq_mm"), n * KT + KT)
                act.activation(rstd[:, :], two(4), ACT.Ln, bias=vec[:, V_EPS:V_EPS + 1], scale=1.0 / D).then_inc(sem("rms_ln"), 1)
                act.wait_ge(sem("rms_ln"), n + 1)
                act.activation(rstd[:, :], rstd[:, :], ACT.Exp, scale=-0.5).then_inc(sem("rstd"), 1)
                if n == 1:
                    act.wait_ge(sem("tile_mm"), T_UP)
                for t in range(KT):
                    act.wait_ge(sem("h_made"), n * KT + t + 1)
                    act.activation(HI[:, t, :], X[:, t, :], ACT.Copy).then_inc(sem("h_hi"), 1)

            def split_hi(p, nth, tiles_before):
                act.wait_ge(sem(f"w_in{p}"), nth)
                act.wait_ge(sem("tile_mm"), tiles_before)
                act.activation(whi[:, p, :], wraw[:, p, :], ACT.Copy).then_inc(sem("whi_made"), 1)

            act.wait_ge(sem("cond_in"), 16)
            act.activation(cond[:, :], cond[:, :], ACT.Silu).then_inc(sem("cond"), 1)
            act.preload_act_table_set("natural_log_exp_and_others")
            act.wait_ge(sem("vec_in"), 16)
            norm(0)

            for p in range(2):
                act.wait_ge(sem(f"w_in{p}"), 16)
                act.activation(whi[:, p, :], wraw[:, p, :], ACT.Copy).then_inc(sem("whi_made"), 1)

            def exps(c, e):
                act.wait_ge(sem("s_nmax"), c + 1)
                act.wait_ge(sem("p_mm"), c - 1 + AHEAD["p_mm"])
                for g in range(4):
                    act.activation(pe_[:, e, g, :], sb_s[:, e, g, :], ACT.Exp, bias=sm[:, e, 1, g:g + 1],
                                   scale=HD ** -0.5, accum_out=sm[:, e, 3, g:g + 1]).then_inc(sem("p_exp"), 1)
                act.activation(sm[:, e, 4, :], sm[:, e, 2, :], ACT.Exp).then_inc(sem("sink_exp"), 1)

            def pt_evac(c, e):
                act.wait_ge(sem("p_mm"), c + 1 + AHEAD["p_mm"])
                act.wait_ge(sem("o_mm"), c - 1 + AHEAD["o_mm"])
                act.activation(pt[:, e, :, :].rearrange("p a b -> p (a b)"), ps[:, 6, :], ACT.Copy).then_inc(sem("pt"), 1)

            def head_std(t):
                for hf in range(2):
                    act.wait_ge(sem("qn_mm"), t * 2 + hf + 1 + AHEAD["qn_mm"])
                    act.wait_ge(sem("qn"), t * 2 + hf - 1 + AHEAD["qn"])
                    act.activation(asd[:, hf, :], ps[:, 4 + hf, :], ACT.Ln, bias=vec[:, V_EPS:V_EPS + 1], scale=1.0 / HD).then_inc(sem("qln"), 1)
                    act.wait_ge(sem("qln"), t * 2 + hf + 1)
                    act.activation(asd[:, hf, :], asd[:, hf, :], ACT.Exp, scale=-0.5).then_inc(sem("qsd"), 1)

            def attn_tile(i, p):
                t = i * 2 + p
                act.wait_ge(sem("tile_mm"), t + 1)
                act.activation(aqkv[:, t, CH:], two(2 * p), ACT.Copy).then_inc(sem("evac"), 1)
                split_hi(p, i * 16 + 32, t + 1)
                for hf in range(2):
                    act.wait_ge(sem("qn_mm"), t * 2 + hf - 1 + AHEAD["qn_mm"])
                    act.wait_ge(sem("evac"), t + 1 + AHEAD["evac"])
                    act.activation(asq[:, hf, :], aqkv[:, t, CH + hf * HALF:CH + (hf + 1) * HALF], ACT.Square).then_inc(sem("qsq"), 1)

            def rwkv_tile(i, p):
                act.wait_ge(sem("tile_mm"), i * 2 + p + 1)
                act.wait_ge(sem(f"proj_out{p}"), (i - 3) * 16 + AHEAD["proj_out"])
                act.activation(pr[:, p, :], two(2 * p), ACT.Copy, scale=omu[:, bass.ds(i * 2 + p, 1)]).then_inc(sem("unmixed"), 1)
                split_hi(p, i * 16 + 32, i * 2 + p + 1)

            act.wait_ge(sem("omu"), 1)
            act.wait_ge(sem("h_lo"), KT // 2)
            act.wait_ge(sem("h_lo_odd"), KT // 2)
            attn_tile(0, 0)
            attn_tile(0, 1)
            head_std(0)
            for i in range(1, 3):
                attn_tile(i, 0)
                head_std(i * 2 - 1)
                attn_tile(i, 1)
                head_std(i * 2)
            rwkv_tile(3, 0)
            rwkv_tile(3, 1)
            with act.Fori(4, NIN // 2) as i:
                c = i * 2 - 8
                exps(c, 0)
                exps(c + 1, 1)
                rwkv_tile(i, 0)
                pt_evac(c, 0)
                pt_evac(c + 1, 1)
                rwkv_tile(i, 1)
            for c in (12, 14):
                exps(c, 0)
                exps(c + 1, 1)
                pt_evac(c, 0)
                pt_evac(c + 1, 1)
            act.wait_ge(sem("o_out"), 64)

            act.wait_ge(sem("lora_in"), 32)
            act.activation(lwa[0:DL, :], lwa[0:DL, :], ACT.Tanh).then_inc(sem("lora_act"), 1)
            act.activation(lg[0:GL, :], lg[0:GL, :], ACT.Sigmoid).then_inc(sem("lora_act"), 1)

            h = half

            def sigmoids(it, j):
                act.wait_ge(sem("lora_mm"), it * 3 + 1)
                act.activation(h["sg"], ps[:, 7, :], ACT.Sigmoid, bias=jv[:, bass.ds(j * J_N + J_W0, 1)]).then_inc(sem("lora_ev"), 1)
                act.wait_ge(sem("lora_mm"), it * 3 + 2)
                act.activation(h["aa"], ps[:, 7, :], ACT.Sigmoid, bias=jv[:, bass.ds(j * J_N + J_A0, 1)]).then_inc(sem("lora_ev"), 1)
                act.preload_act_table_set("natural_log_exp_and_others")

            def gate_and_squares(it):
                act.wait_ge(sem("kkr"), it + 1)
                act.activation(h["ksq"], h["kk"], ACT.Square).then_inc(sem("ksq"), 1)
                act.wait_ge(sem("lora_mm"), it * 3 + 3)
                act.activation(h["gg"], ps[:, 7, :], ACT.Copy).then_inc(sem("lora_ev"), 1)

            def decays(it):
                act.wait_ge(sem("cs"), it + 1)
                act.activation(pb[:, :].rearrange("p (c t) -> p c t", t=65)[:, :, 1:65],
                               h["cs"].rearrange("p (c t) -> p c t", t=CH), ACT.Exp, scale=-DEC).then_inc(sem("pexp"), 1)
                act.activation(h["pinv"], h["cs"], ACT.Exp, scale=DEC).then_inc(sem("pexp"), 1)

            def kk_norm(it):
                act.wait_ge(sem("kss_mm"), it + 1)
                act.activation(h["nrm"], ps[:, 7, :], ACT.Ln, bias=vec[:, V_TINY:V_TINY + 1]).then_inc(sem("kln"), 1)
                act.wait_ge(sem("kln"), it + 1)
                act.activation(h["nrm"], h["nrm"], ACT.Exp, scale=-0.5).then_inc(sem("nrm"), 1)

            def u_evac(it, par, c):
                cp, e = c // 2, c % 2
                r = slice(64 * e, 64 * e + 64)
                act.wait_ge(sem("u_mm"), it * 8 + c + 1)
                act.activation(us[r, cp, :], ps[r, 4, 0:P], ACT.Copy).then_inc(sem("u"), 1)

            def y_evac(it, cp):
                act.wait_ge(sem("y_mm"), it * NCP + cp + 1 + AHEAD["y_mm"])
                act.activation(h["y"][:, cp * P:(cp + 1) * P], ps[:, 6, 0:P], ACT.Copy).then_inc(sem("y"), 1)

            def y_var(it):
                act.wait_ge(sem("yc"), it + 1)
                act.activation(h["ysq"], h["yc"], ACT.Square).then_inc(sem("ysq"), 1)
                act.wait_ge(sem("yvar_mm"), it + 1)
                act.activation(h["ysq"], ps[:, 6, :], ACT.Ln, bias=vec[:, V_LEPS:V_LEPS + 1], scale=1.0 / HD).then_inc(sem("yln"), 1)
                act.wait_ge(sem("yln"), it + 1)
                act.activation(h["ysq"], h["ysq"], ACT.Exp, scale=-0.5).then_inc(sem("sd"), 1)

            def step(j, par, first=False, last=False):
                it = j * 2 + par
                jn = j if par == 0 else j + 1
                for cp in range(NCP):
                    act.wait_ge(sem("nat_mm"), it * NCP + cp + 1)
                    act.activation(nat[par][:, cp, :, :].rearrange("p a b -> p (a b)"), ps[:, cp, :], ACT.Copy).then_inc(sem("nat"), 1)
                if not last:
                    sigmoids(it + 1, jn)
                for lev in range(4):
                    if not first:
                        u_evac(it - 1, 1 - par, 2 * lev)
                        u_evac(it - 1, 1 - par, 2 * lev + 1)
                    if not last:
                        if lev == 0:
                            gate_and_squares(it + 1)
                        if lev == 1:
                            decays(it + 1)
                            kk_norm(it + 1)
                if not first:
                    for cp in range(NCP):
                        y_evac(it - 1, cp)
                for cp in range(NCP):
                    act.wait_ge(sem("wd_mm"), it * NCP + cp + 1)
                    act.activation(wd_[par][:, cp, :, :].rearrange("p a b -> p (a b)"), ps[:, cp, 0:384], ACT.Copy).then_inc(sem("wd"), 1)
                if not first:
                    y_var(it - 1)

            act.wait_ge(sem("jv_in"), 16)
            sigmoids(0, 0)
            gate_and_squares(0)
            decays(0)
            kk_norm(0)
            step(0, 0, first=True)
            step(0, 1)
            with act.Fori(1, NJ - 1) as j:
                step(j, 0)
                step(j, 1)
            step(NJ - 1, 0)
            step(NJ - 1, 1, last=True)
            for c in range(8):
                u_evac(2 * NJ - 1, 1, c)
            for cp in range(NCP):
                y_evac(2 * NJ - 1, cp)
            y_var(2 * NJ - 1)

            with act.Fori(0, KT // 2) as i:
                for p in range(2):
                    act.wait_ge(sem(f"mix_in{p}"), i * 16 + 16)
                    act.activation(HI[:, i * 2 + p, :], mst[:, p, :], ACT.Copy).then_inc(sem("mix_hi"), 1)

            with act.Fori(0, KT // 2) as i:
                for p in range(2):
                    split_hi(p, 16 * (NIN // 2) + i * 16 + 32, T_OUT + i * 2 + p + 1)
            norm(1)

            def down_hi(hf, n):
                act.wait_ge(sem(f"wd_in{hf}"), n)
                act.activation(dhi[hf][:, :], draw[hf][:, :], ACT.Copy).then_inc(sem("down_hi"), 1)

            def act_hi(k0, k1):
                for k in range(k0, k1):
                    act.wait_ge(sem("act_made"), k + 1 + AHEAD["act_made"])
                    act.activation(actH[k][:, :], actb[:, k, :], ACT.Copy).then_inc(sem("act_hi"), 1)

            def up(f, more):
                for p in range(2):
                    act.wait_ge(sem("tile_mm"), T_UP + f * 2 + p + 1)
                    act.wait_ge(sem("act_made"), f + AHEAD["act_made"])
                    c = V_CONV + (f * 2 + p) * 4
                    act.activation(gu[:, p, :], two(2 * p + 4 * up.par), ACT.Identity,
                                   bias=vec[:, bass.ds(c + 3, 1)], scale=vec[:, bass.ds(c + 2, 1)]).then_inc(sem("conv0"), 1)
                    if more:
                        split_hi(p, 16 * (NIN // 2 + KT // 2) + f * 16 + 32, T_UP + f * 2 + p + 1)
                if not more:
                    act_hi(2, 3)
                act.wait_ge(sem("convolved"), f * 2 + 1 + AHEAD["convolved"])
                act.activation(gu[:, 0, :], gu[:, 0, :], ACT.Silu).then_inc(sem("silu"), 1)

            down_hi(0, 16)
            with act.Fori(0, NF // 2 - 1) as i:
                for par in range(2):
                    up.par = par
                    up(i * 2 + par, True)
            up.par = 0
            up(NF - 2, True)
            act.wait_ge(sem("wlo_made"), T_UP + 2 * NF)
            act_hi(0, 2)
            up.par = 1
            up(NF - 1, False)
            act_hi(3, NF // 2)
            down_hi(1, 16)
            act_hi(NF // 2, NF)
            with act.Fori(1, KT) as d:
                for hf in range(2):
                    down_hi(hf, d * 16 + 16)

        @block.vector
        def _(dve):
            def lo_row(n, t):
                dve.wait_ge(sem("h_hi"), n * KT + t + 1)
                dve.tensor_tensor(LO[:, t, :], X[:, t, :], HI[:, t, :].bitcast(F32), ALU.subtract).then_inc(sem("h_lo_odd"), 1)

            def norm(n):
                sc, sh_, gain = (8, 0, V_GMIX) if n == 0 else (32, 24, V_GFFN)
                dve.scalar_tensor_tensor(out=modA[:, n * KT:(n + 1) * KT], in0=mod[:, sc:sc + KT], scalar=1.0,
                                         in1=vec[:, gain:gain + KT], op0=ALU.add, op1=ALU.mult).then_inc(sem("modA"), 1)
                dve.wait_ge(sem("rstd"), n + 1)
                dve.wait_ge(sem("modA"), n + 1)
                for t in range(KT):
                    dve.scalar_tensor_tensor(out=X[:, t, :], in0=X[:, t, :], scalar=modA[:, n * KT + t:n * KT + t + 1],
                                             in1=rstd[:, :], op0=ALU.mult, op1=ALU.mult).then_inc(sem("h_scaled"), 1)
                    dve.wait_ge(sem("h_scaled"), n * KT + t + 1)
                    dve.tensor_scalar(X[:, t, :], X[:, t, :], mod[:, sh_ + t:sh_ + t + 1], None, ALU.add).then_inc(sem("h_made"), 1)
                    if t >= 2 and t % 2 == 0:
                        lo_row(n, t - 1)
                lo_row(n, KT - 1)

            dve.wait_ge(sem("vec_in"), 16)
            dve.tensor_scalar(omu[:, :], vec[:, V_MU:V_MU + NIN], -1.0, 1.0, ALU.mult, ALU.add).then_inc(sem("omu"), 1)
            dve.wait_ge(sem("cond"), 1)

            def ada(col, s, nth):
                dve.wait_ge(sem(f"ada_in{s}"), nth)
                dve.wait_ge(sem("ada_used"), col + AHEAD["ada_used"])
                dve.scalar_tensor_tensor(out=junk[:, :], in0=adat[:, s, :], scalar=1.0, in1=cond[:, :], op0=ALU.mult,
                                         op1=ALU.mult, accum_out=mod[:, bass.ds(col, 1)]).then_inc(sem("ada_used"), 1)

            with dve.Fori(0, 4) as i:
                for s in range(4):
                    ada(i * 4 + s, s, i * 16 + 16)
            dve.wait_ge(sem("ada_used"), 16 + AHEAD["ada_used"])
            dve.tensor_tensor(mod[:, 0:16], mod[:, 0:16], vec[:, V_ADAB:V_ADAB + 16], ALU.add).then_inc(sem("mod"), 1)
            dve.wait_ge(sem("mod"), 1)
            norm(0)

            def head_norm(t):
                for hf in range(2):
                    dve.wait_ge(sem("qsd"), t * 2 + hf + 1 + AHEAD["qsd"])
                    w = aqkv[:, t, CH + hf * HALF:CH + (hf + 1) * HALF]
                    dve.scalar_tensor_tensor(out=w, in0=w, scalar=vec[:, bass.ds(V_GAIN + t, 1)], in1=asd[:, hf, :],
                                             op0=ALU.mult, op1=ALU.mult).then_inc(sem("qn"), 1)

            def ada4(i, p):
                for s in range(4):
                    ada(16 + i * 8 + 4 * p + s, s, 64 + i * 32 + 16 * p + 16)

            def mix(i, p):
                dve.wait_ge(sem("unmixed"), i * 2 + p + 1 - NATT)
                dve.scalar_tensor_tensor(out=pr[:, p, 1:S], in0=two(2 * p)[:, 0:S - 1],
                                         scalar=vec[:, bass.ds(V_MU + i * 2 + p, 1)], in1=pr[:, p, 1:S],
                                         op0=ALU.mult, op1=ALU.add).then_inc(sem("evac"), 1)

            def scores(c, e):
                b0 = e * 256
                dve.tensor_copy(sb_s[:, e, :, :].rearrange("p (g a) b -> p g (a b)", g=2),
                                ps[:, 4:6, b0:b0 + 256]).then_inc(sem("s_ev"), 1)

            def softmax_in(c, e):
                dve.wait_ge(sem("s_ev"), c + 1 + AHEAD["s_ev"])
                if isinstance(c, int) and c == 0:
                    dve.memset(sb_s[:, e, :, 0:CH], NEG).then_inc(sem("s_first"), 1)
                    dve.wait_ge(sem("s_first"), 1)
                dve.tensor_reduce(sm[:, e, 0, :], sb_s[:, e, :, :], AX_X, ALU.max).then_inc(sem("s_small"), 1)
                dve.wait_ge(sem("s_small"), c * 3 + 1)
                dve.scalar_tensor_tensor(out=sm[:, e, 0, :], in0=sm[:, e, 0, :], scalar=HD ** -0.5,
                                         in1=vec[:, V_SINK:V_SINK + 4], op0=ALU.mult, op1=ALU.max).then_inc(sem("s_small"), 1)
                dve.wait_ge(sem("s_small"), c * 3 + 2)
                dve.tensor_tensor(sm[:, e, 2, :], vec[:, V_SINK:V_SINK + 4], sm[:, e, 0, :], ALU.subtract).then_inc(sem("s_small"), 1)
                dve.wait_ge(sem("s_small"), c * 3 + 3)
                dve.tensor_scalar(sm[:, e, 1, :], sm[:, e, 0, :], -1.0, None, ALU.mult).then_inc(sem("s_nmax"), 1)

            def attn_round(rnd, c):
                dve.wait_ge(sem("s_qk"), rnd + 1 + AHEAD["s_qk"])
                scores(c, 0)
                scores(c + 1, 1)
                softmax_in(c, 0)
                softmax_in(c + 1, 1)
                dve.wait_ge(sem("v_mm"), rnd + 1 + AHEAD["v_mm"])
                dve.wait_ge(sem("o_mm"), c + AHEAD["o_mm"])
                dve.tensor_copy(vn[:, :, :], ps[:, 7, 0:2 * P].rearrange("p (a b) -> p a b", b=P)).then_inc(sem("vn"), 1)

            def probs(c, e):
                dve.wait_ge(sem("p_exp"), c * 4 + 4)
                dve.wait_ge(sem("sink_exp"), c + 1)
                dve.tensor_tensor(sm[:, e, 3, :], sm[:, e, 3, :], sm[:, e, 4, :], ALU.add).then_inc(sem("den"), 1)
                dve.wait_ge(sem("den"), c * 2 + 1)
                dve.reciprocal(sm[:, e, 4, :], sm[:, e, 3, :]).then_inc(sem("den"), 1)
                dve.wait_ge(sem("den"), c * 2 + 2)
                dve.tensor_tensor(pe_[:, e, :, :], pe_[:, e, :, :], sm[:, e, 4, :].unsqueeze(2).to_broadcast([P, 4, P]), ALU.mult).then_inc(sem("probs"), 1)

            def o_evac(c):
                dve.wait_ge(sem("o_mm"), c + 1 + AHEAD["o_mm"])
                dve.tensor_copy(aqkv[:, 0:4, bass.ds(c * CH + CH, CH)], ps[:, 7, 256:512].rearrange("p (a b) -> p a b", b=CH)).then_inc(sem("o_ev"), 1)

            ada4(0, 0)
            ada4(0, 1)
            dve.wait_ge(sem("h_lo"), KT // 2)
            dve.wait_ge(sem("h_lo_odd"), KT // 2)
            dve.memset(aqkv[:, 4, 0:CH], 0.0).then_inc(sem("pads"), 1)
            dve.memset(aqkv[:, 5, 0:CH], 0.0).then_inc(sem("pads"), 1)
            head_norm(0)
            with dve.Fori(1, 3) as i:
                ada4(i, 0)
                head_norm(i * 2 - 1)
                ada4(i, 1)
                head_norm(i * 2)
            for p in range(2):
                ada4(3, p)
                mix(3, p)

            def full_round(i, c):
                attn_round(i - 4, c)
                probs(c, 0)
                probs(c + 1, 1)
                mix(i, 0)
                o_evac(c)
                o_evac(c + 1)
                mix(i, 1)

            full_round(4, 0)
            with dve.Fori(5, NIN // 2) as i:
                full_round(i, i * 2 - 8)
            for c in (12, 14):
                attn_round(c // 2, c)
                probs(c, 0)
                probs(c + 1, 1)
                o_evac(c)
                o_evac(c + 1)
            dve.wait_ge(sem("ada_used"), NADA + AHEAD["ada_used"])
            dve.tensor_tensor(mod[:, 16:48], mod[:, 16:48], vec[:, V_ADAB + 16:V_ADAB + 48], ALU.add).then_inc(sem("mod"), 1)

            dve.wait_ge(sem("tile_mm"), NIN)
            for p in range(2):
                dve.wait_ge(sem(f"proj_out{p}"), 16 * (NIN - NATT) // 2 + AHEAD["proj_out"])
            dve.wait_ge(sem("o_out"), 64)
            dve.memset(sh[:, :, :], 0.0).then_inc(sem("sh_zero"), 1)
            pb3 = pb[:, :].rearrange("p (c t) -> p c t", t=65)
            dve.memset(pb3[:, :, 0:1], 1.0).then_inc(sem("pb_one"), 1)
            dve.wait_ge(sem("sh_zero"), 1)
            dve.wait_ge(sem("pb_one"), 1)

            h = half

            def bc(m, n):
                return m.unsqueeze(1).to_broadcast([P, n, P])

            def jcol(j, a):
                return jv[:, bass.ds(j * J_N + a, 1)]

            def rows(j, hf):
                return (rkv[:, a, hf * HALF:(hf + 1) * HALF] for a in range(3))

            def kk_raw(it, j, hf):
                r, k, v = rows(j, hf)
                dve.wait_ge(sem("rkv_in"), j * 32 + 32)
                dve.wait_ge(sem("ended"), it * 2)
                dve.tensor_scalar(h["kk"], k, jcol(j, J_KK), -1.0, ALU.mult, ALU.mult).then_inc(sem("kkr"), 1)

            def decay_sum(it):
                dve.wait_ge(sem("lora_ev"), it * 3 + 1)
                dve.tensor_tensor_scan(h["cs"], cm(C_RST, 4), h["sg"], 0.0, ALU.mult, ALU.add).then_inc(sem("cs"), 1)

            def k_scaled(it, j, hf):
                r, k, v = rows(j, hf)
                dve.wait_ge(sem("lora_ev"), it * 3 + 2)
                dve.wait_ge(sem("km_parts"), it * 3)
                dve.tensor_scalar(omka[:, :], jcol(j, J_KA), -1.0, 1.0, ALU.mult, ALU.add).then_inc(sem("km_parts"), 1)
                dve.wait_ge(sem("km_parts"), it * 3 + 1)
                dve.tensor_scalar(h["km"], h["aa"], jcol(j, J_KA), omka[:, 0:1], ALU.mult, ALU.add).then_inc(sem("km_parts"), 1)
                dve.wait_ge(sem("km_parts"), it * 3 + 2)
                dve.tensor_tensor(h["km"], k, h["km"], ALU.mult).then_inc(sem("km_parts"), 1)
                dve.wait_ge(sem("km_parts"), it * 3 + 3)
                dve.scalar_tensor_tensor(out=h["t3"], in0=r, scalar=jcol(j, J_RK), in1=h["km"], op0=ALU.mult, op1=ALU.mult).then_inc(sem("rk_prod"), 1)

            def kk_unit(it):
                dve.wait_ge(sem("nrm"), it + 1)
                dve.scalar_tensor_tensor(out=h["kk"], in0=h["nrm"], scalar=1e12, in1=h["kk"], op0=ALU.min, op1=ALU.mult).then_inc(sem("nkk"), 1)
                dve.wait_ge(sem("pexp"), it * 2 + 2)
                dve.scalar_tensor_tensor(out=h["t2"], in0=h["aa"], scalar=-1.0, in1=h["pinv"], op0=ALU.mult, op1=ALU.mult).then_inc(sem("t2"), 1)

            def bonus(it, j, hf):
                r, k, v = rows(j, hf)
                dve.wait_ge(sem("bon_mm"), it + 1)
                dve.tensor_tensor(h["bon"], ps[:, 7, :], v, ALU.mult).then_inc(sem("bon"), 1)

            def keep(it, j, par):
                dve.wait_ge(sem("lora_ev"), it * 3 + 3)
                dve.wait_ge(sem("bon"), it + 1)
                dve.tensor_scalar(g1[par][:, :], h["gg"], jcol(j, J_G), None, ALU.mult).then_inc(sem("kept"), 1)
                dve.scalar_tensor_tensor(out=g2[par][:, :], in0=h["bon"], scalar=jcol(j, J_B), in1=h["gg"], op0=ALU.add, op1=ALU.mult).then_inc(sem("kept"), 1)
                dve.tensor_copy(pend[par][:, :], pb[:, :].rearrange("p (c t) -> p c t", t=65)[:, :, 64]).then_inc(sem("kept"), 1)

            def state(it, par, c):
                dve.wait_ge(sem("s_mm"), it * 8 + c + 1)
                for hh in range(2):
                    d = slice(64 * hh, 64 * hh + 64)
                    dve.scalar_tensor_tensor(out=sh[d, c + 1, d], in0=sh[d, c, d], scalar=pend[par][d, c:c + 1],
                                             in1=ps[d, 5, d], op0=ALU.mult, op1=ALU.add).then_inc(sem("s"), 1)
                dve.wait_ge(sem("s"), it * 16 + 2 * c + 2)

            def first_state(it, par):
                dve.wait_ge(sem("kept"), it * 3 + 3)
                dve.wait_ge(sem("y_mm"), it * NCP + AHEAD["y_mm"])
                if par == 0:
                    dve.memset(sh[:, 0, :], 0.0).then_inc(sem("s0"), 1)
                else:
                    dve.tensor_copy(sh[:, 0, :], sh[:, 8, :]).then_inc(sem("s0"), 1)
                dve.wait_ge(sem("s0"), it + 1)

            def output(it):
                dve.wait_ge(sem("sd"), it + 1)
                dve.wait_ge(sem("y_out"), it * 16 + AHEAD["y_out"])
                dve.tensor_tensor(h["yo"], h["yc"], h["ysq"], ALU.mult).then_inc(sem("y_parts"), 1)
                dve.wait_ge(sem("y_parts"), it * 2 + 1)

            def output2(it, par):
                dve.tensor_tensor(h["yo"], h["yo"], g1[par][:, :], ALU.mult).then_inc(sem("y_parts"), 1)
                dve.wait_ge(sem("y_parts"), it * 2 + 2)
                dve.tensor_tensor(h["yo"], h["yo"], g2[par][:, :], ALU.add).then_inc(sem("y_ready"), 1)

            def y_centre(it):
                dve.wait_ge(sem("ymean_mm"), it + 1)
                dve.scalar_tensor_tensor(out=h["yc"], in0=ps[:, 6, :], scalar=-1.0 / HD, in1=h["y"], op0=ALU.mult, op1=ALU.add).then_inc(sem("yc"), 1)

            def t1_evac(it, lev, gq):
                dve.wait_ge(sem("t1_mm"), it * 2 * NLEV + 2 * lev + gq + 1)
                dve.tensor_tensor(T1[:, 4 * gq:4 * gq + 4, :], ps[:, gq, :].rearrange("p (a b) -> p a b", b=P),
                                  bc(cm(C_LEV + lev), 4), ALU.mult).then_inc(sem("t1"), 1)

            def dx_evac(it, lev, gq):
                g4 = slice(4 * gq, 4 * gq + 4)
                dve.wait_ge(sem("dx_mm"), it * 2 * NLEV + 2 * lev + gq + 1)
                if lev < NLEV - 1:
                    dve.tensor_tensor(Xi[:, g4, :], ps[:, 2, :].rearrange("p (a b) -> p a b", b=P), Xi[:, g4, :], ALU.add).then_inc(sem("xi"), 1)
                dve.tensor_tensor(XiT[:, g4, :], ps[:, 3, :].rearrange("p (a b) -> p a b", b=P), XiT[:, g4, :], ALU.add).then_inc(sem("xit"), 1)

            def step(j, par, first=False, last=False):
                it = j * 2 + par
                jn = j if par == 0 else j + 1
                for q in range(NQ):
                    dve.wait_ge(sem("am_mm"), it * NQ + q + 1)
                    dve.tensor_tensor(am[par][:, q, :, :].rearrange("p a b -> p (a b)"), ps[:, q % 4, :], cm(C_M4, 4), ALU.mult).then_inc(sem("am"), 1)
                    if q % 4 == 3:
                        g4 = slice(q - 3, q + 1)
                        dve.wait_ge(sem("am"), it * NQ + q + 1)
                        dve.tensor_tensor(Xi[:, g4, :], am[par][:, g4, 2, :], bc(cm(C_OFF1), 4), ALU.mult).then_inc(sem("x0a"), 1)
                        dve.tensor_tensor(XiT[:, g4, :], am[par][:, g4, 0, :], bc(cm(C_OFF1T), 4), ALU.mult).then_inc(sem("x0a"), 1)
                keep(it, j, par)
                for a in range(4):
                    hh, cpp = a // 2, a % 2
                    dve.wait_ge(sem("ark_mm"), it * 4 + a + 1)
                    dve.tensor_tensor(ark[par][:, hh, 2 * cpp:2 * cpp + 2, :], ps[:, a, 0:256].rearrange("p (a b) -> p a b", b=P),
                                      bc(cm(C_M4 + 1), 2), ALU.mult).then_inc(sem("ark"), 1)
                if not last:
                    kk_raw(it + 1, jn, 1 - par)
                if not first:
                    first_state(it - 1, 1 - par)
                for lev in range(NLEV):
                    z = not first and lev < 4
                    t1_evac(it, lev, 0)
                    if z:
                        state(it - 1, 1 - par, 2 * lev)
                    t1_evac(it, lev, 1)
                    dx_evac(it, lev, 0)
                    if z:
                        state(it - 1, 1 - par, 2 * lev + 1)
                    dx_evac(it, lev, 1)
                    if not last:
                        if lev == 0:
                            decay_sum(it + 1)
                        if lev == 1:
                            k_scaled(it + 1, jn, 1 - par)
                        if lev == 2:
                            kk_unit(it + 1)
                        if lev == 4:
                            bonus(it + 1, jn, 1 - par)
                if not first:
                    y_centre(it - 1)
                    output(it - 1)
                    output2(it - 1, 1 - par)

            dve.wait_ge(sem("jv_in"), 16)
            kk_raw(0, 0, 0)
            decay_sum(0)
            k_scaled(0, 0, 0)
            kk_unit(0)
            bonus(0, 0, 0)
            step(0, 0, first=True)
            step(0, 1)
            with dve.Fori(1, NJ - 1) as j:
                step(j, 0)
                step(j, 1)
            step(NJ - 1, 0)
            step(NJ - 1, 1, last=True)
            first_state(2 * NJ - 1, 1)
            for c in range(8):
                state(2 * NJ - 1, 1, c)
            y_centre(2 * NJ - 1)
            output(2 * NJ - 1)
            output2(2 * NJ - 1, 1)

            with dve.Fori(0, KT // 2) as i:
                dve.wait_ge(sem("mix_hi"), i * 2 + 2)
                dve.tensor_tensor(LO[:, i * 2 + 1, :], mst[:, 1, :], HI[:, i * 2 + 1, :].bitcast(F32), ALU.subtract).then_inc(sem("mix_lo_odd"), 1)

            with dve.Fori(0, KT // 2) as i:
                for p in range(2):
                    dve.wait_ge(sem("tile_mm"), T_OUT + i * 2 + p + 1)
                    dve.wait_ge(sem(f"xin_in{p}"), i * 16 + 16)
                    dve.scalar_tensor_tensor(out=X[:, i * 2 + p, :], in0=two(2 * p), scalar=mod[:, bass.ds(16 + i * 2 + p, 1)],
                                             in1=xin[:, p, :], op0=ALU.mult, op1=ALU.add).then_inc(sem("x1_made"), 1)
            dve.wait_ge(sem("x1_store"), 16 * KT)
            dve.wait_ge(sem("mod"), 2)
            norm(1)

            def up(f, par):
                for p in range(2):
                    c = V_CONV + (f * 2 + p) * 4
                    u = two(2 * p + 4 * par)
                    dve.wait_ge(sem("conv0"), f * 2 + p + 1)
                    dve.scalar_tensor_tensor(out=gu[:, p, 1:S], in0=u[:, 0:S - 1], scalar=vec[:, bass.ds(c + 1, 1)],
                                             in1=gu[:, p, 1:S], op0=ALU.mult, op1=ALU.add).then_inc(sem("conv1"), 1)
                    dve.wait_ge(sem("conv1"), f * 2 + p + 1)
                    dve.scalar_tensor_tensor(out=gu[:, p, 2:S], in0=u[:, 0:S - 2], scalar=vec[:, bass.ds(c, 1)],
                                             in1=gu[:, p, 2:S], op0=ALU.mult, op1=ALU.add).then_inc(sem("convolved"), 1)
                dve.wait_ge(sem("silu"), f + 1)
                dve.wait_ge(sem("convolved"), f * 2 + 2 + AHEAD["convolved"])
                dve.tensor_tensor(actb[:, f, :], gu[:, 0, :], gu[:, 1, :], ALU.mult).then_inc(sem("act_made"), 1)

            def down_lo(hf, n):
                dve.wait_ge(sem("down_hi"), n)
                dve.tensor_tensor(dlo[hf][:, :], draw[hf][:, :], dhi[hf][:, :].bitcast(F32), ALU.subtract).then_inc(sem("down_lo"), 1)

            def act_lo(k0, k1):
                for k in range(k0 | 1, k1, 2):
                    dve.wait_ge(sem("act_hi"), k + 1)
                    dve.tensor_tensor(actL[k][:, :], actb[:, k, :], actH[k][:, :].bitcast(F32), ALU.subtract).then_inc(sem("act_lo_odd"), 1)

            dve.wait_ge(sem("h_lo"), KT)
            down_lo(0, 1)
            with dve.Fori(0, NF // 2 - 1) as i:
                for par in range(2):
                    up(i * 2 + par, par)
            up(NF - 2, 0)
            act_lo(1, 2)
            up(NF - 1, 1)
            act_lo(3, NF // 2)
            down_lo(1, 2)
            act_lo(NF // 2, NF)

            def y2(d, p):
                dve.wait_ge(sem("down_mm"), d * 2 + 2)
                dve.wait_ge(sem("x1_in"), d * 16 + 16)
                dve.scalar_tensor_tensor(out=x1in[:, :], in0=two(2 * p), scalar=mod[:, bass.ds(40 + d, 1)],
                                         in1=x1in[:, :], op0=ALU.mult, op1=ALU.add).then_inc(sem("y2_made"), 1)

            def down_tile(d, p):
                down_lo(0, d * 2 + 3)
                y2(d, p)
                down_lo(1, d * 2 + 4)

            down_tile(0, 0)
            with dve.Fori(0, KT // 2 - 1) as i:
                down_tile(i * 2 + 1, 1)
                down_tile(i * 2 + 2, 0)
            y2(KT - 1, 1)

        @block.gpsimd
        def _(pool):
            def lo_rows(n):
                for t in range(0, KT, 2):
                    pool.wait_ge(sem("h_hi"), n * KT + t + 1)
                    pool.tensor_tensor(LO[:, t, :], X[:, t, :], HI[:, t, :].bitcast(F32), ALU.subtract).then_inc(sem("h_lo"), 1)

            def stage(c):
                for e in range(2):
                    pool.wait_ge(sem("qn"), 10 + AHEAD["qn"])
                    pool.tensor_copy(stg[:, e, 0:256].rearrange("p (a b) -> p a b", b=CH), aqkv[:, 0:4, bass.ds(CH + (c + e) * CH, CH)]).then_inc(sem("staged"), 1)
                    pool.tensor_copy(stg[:, e, 256:384], aqkv[:, 4, bass.ds((c + e) * CH, P)]).then_inc(sem("staged"), 1)
                    pool.tensor_copy(stg[:, e, 384:512], aqkv[:, 5, bass.ds((c + e) * CH, P)]).then_inc(sem("staged"), 1)

            def split_lo(p, n):
                pool.wait_ge(sem("whi_made"), n)
                pool.tensor_tensor(wlo[:, p, :], wraw[:, p, :], whi[:, p, :].bitcast(F32), ALU.subtract).then_inc(sem("wlo_made"), 1)

            lo_rows(0)
            with pool.Fori(0, 4) as i:
                for p in range(2):
                    split_lo(p, i * 2 + p + 1)
            split_lo(0, 9)
            pool.wait_ge(sem("evac"), NATT + AHEAD["evac"])
            pool.wait_ge(sem("pads"), 2)
            stage(0)
            split_lo(1, 10)
            with pool.Fori(5, NIN // 2 + 1) as i:
                split_lo(0, i * 2 + 1)
                pool.wait_ge(sem("v_mm"), i - 4 + AHEAD["v_mm"])
                stage(i * 2 - 8)
                split_lo(1, i * 2 + 2)
            pool.wait_ge(sem("v_mm"), 7 + AHEAD["v_mm"])
            stage(14)
            pool.wait_ge(sem("o_out"), 64)

            pool.wait_ge(sem("con_in"), 16)
            h = half

            def q4(t):
                return t.rearrange("p (c e t) -> p c e t", e=2, t=CH)

            def cpv(t):
                return t.rearrange("p (c t) -> p c t", t=P)

            pbv = pb[:, :].rearrange("p (c e t) -> p c e t", e=2, t=65)
            arv = ar[:, :, :, :].rearrange("p c a (e t) -> p c a e t", e=2)
            bkv = bk[:, :, :, :].rearrange("p c a (e t) -> p c a e t", e=2)

            def scaled(it, j, hf):
                r = rkv[:, 0, hf * HALF:(hf + 1) * HALF]
                pool.wait_ge(sem("km_parts"), it * 3 + 3)
                pool.wait_ge(sem("pexp"), it * 2 + 2)
                pool.wait_ge(sem("ark_mm"), it * 4)
                pool.tensor_tensor(arv[:, :, 1], q4(r), pbv[:, :, :, 1:CH + 1], ALU.mult).then_inc(sem("scaled"), 1)
                pool.tensor_tensor(bk[:, :, 1, :], cpv(h["km"]), cpv(h["pinv"]), ALU.mult).then_inc(sem("scaled"), 1)
                pool.wait_ge(sem("nkk"), it + 1)
                pool.tensor_tensor(arv[:, :, 0], q4(h["kk"]), pbv[:, :, :, 0:CH], ALU.mult).then_inc(sem("scaled"), 1)
                pool.wait_ge(sem("t2"), it + 1)
                pool.tensor_tensor(bk[:, :, 0, :], cpv(h["kk"]), cpv(h["t2"]), ALU.mult).then_inc(sem("scaled"), 1)
                pool.wait_ge(sem("scaled"), it * 4 + 4)
                pend_b = pbv[:, :, :, CH:CH + 1].to_broadcast([P, NCP, 2, CH])
                pool.tensor_tensor(q4(h["kh"]), bkv[:, :, 1], pend_b, ALU.mult).then_inc(sem("ended"), 1)
                pool.tensor_tensor(q4(h["bh"]), bkv[:, :, 0], pend_b, ALU.mult).then_inc(sem("ended"), 1)

            def step(j, par, last=False):
                it = j * 2 + par
                jn = j if par == 0 else j + 1
                pool.wait_ge(sem("scaled"), it * 4 + 4)
                pool.wait_ge(sem("y_mm"), (it - 1) * NCP + AHEAD["y_mm"])
                pool.tensor_tensor(rtz[par][:, :, :], ar[:, :, 1, :], onesb, ALU.mult).then_inc(sem("rtz"), 1)
                for g in range(2):
                    g4 = slice(4 * g, 4 * g + 4)
                    pool.wait_ge(sem("x0a"), it * 4 + 2 * g + 2)
                    pool.tensor_tensor(Xi[:, g4, :], Xi[:, g4, :], ident.unsqueeze(1).to_broadcast([P, 4, P]), ALU.add).then_inc(sem("x0"), 1)
                    pool.tensor_tensor(XiT[:, g4, :], XiT[:, g4, :], ident.unsqueeze(1).to_broadcast([P, 4, P]), ALU.add).then_inc(sem("x0"), 1)
                if not last:
                    scaled(it + 1, jn, 1 - par)

            onesb = ones.unsqueeze(1).to_broadcast([P, NCP, P])
            scaled(0, 0, 0)
            step(0, 0)
            step(0, 1)
            with pool.Fori(1, NJ - 1) as j:
                step(j, 0)
                step(j, 1)
            step(NJ - 1, 0)
            step(NJ - 1, 1, last=True)

            with pool.Fori(0, KT // 2) as i:
                pool.wait_ge(sem("mix_hi"), i * 2 + 1)
                pool.tensor_tensor(LO[:, i * 2, :], mst[:, 0, :], HI[:, i * 2, :].bitcast(F32), ALU.subtract).then_inc(sem("mix_lo"), 1)

            with pool.Fori(0, KT // 2) as i:
                for p in range(2):
                    split_lo(p, T_OUT + 2 + i * 2 + p + 1)
            lo_rows(1)
            with pool.Fori(0, NF - 1) as i:
                for p in range(2):
                    split_lo(p, T_UP + 2 + i * 2 + p + 1)
            for k in range(0, NF, 2):
                pool.wait_ge(sem("act_hi"), k + 1)
                pool.tensor_tensor(actL[k][:, :], actb[:, k, :], actH[k][:, :].bitcast(F32), ALU.subtract).then_inc(sem("act_lo"), 1)

        @block.tensor
        def _(pe):
            def ssq(n):
                for t in range(KT):
                    pe.wait_ge(sem("sq"), n * KT + t + 1)
                    for hf in range(2):
                        last = pe.matmul(ps[:, 4 + hf, :], ones, sqt[:, t % 2, hf * HALF:(hf + 1) * HALF], start=(t == 0), stop=(t == KT - 1))
                    last.then_inc(sem("ssq_mm"), 1)

            def tile(p, b, k0=0, k1=KT, ready=None):
                for k in range(k0, k1):
                    if ready is not None:
                        ready(k)
                    wh, wl = whi[:, p, k * P:(k + 1) * P], wlo[:, p, k * P:(k + 1) * P]
                    for n, (w, rows) in enumerate(((wh, HI), (wh, LO), (wl, HI))):
                        for hf in range(2):
                            last = pe.matmul(ps[:, b + hf, :], w, rows[:, k, hf * HALF:(hf + 1) * HALF],
                                             start=(k == 0 and n == 0), stop=(k == KT - 1 and n == 2))
                if k1 == KT:
                    last.then_inc(sem("tile_mm"), 1)

            def rows_ready(even, odd, n):
                def ready(k):
                    pe.wait_ge(sem(odd if k % 2 else even), n + k // 2 + 1 + AHEAD.get(odd if k % 2 else even, 0))
                return ready

            def head_sums(t):
                for hf in range(2):
                    pe.wait_ge(sem("qsq"), t * 2 + hf + 1)
                    pe.wait_ge(sem("qsd"), t * 2 + hf - 1 + AHEAD["qsd"])
                    pe.matmul(ps[:, 4 + hf, :], blk, asq[:, hf, :], start=True, stop=True).then_inc(sem("qn_mm"), 1)

            def in_tile(t, p, **kw):
                pe.wait_ge(sem("wlo_made"), t + 1)
                pe.wait_ge(sem("evac"), t - 1 + AHEAD["evac"])
                tile(p, 2 * p, **kw)

            def s_and_v(rnd, c):
                pe.wait_ge(sem("staged"), c * 3 + 6)
                pe.wait_ge(sem("s_ev"), c + AHEAD["s_ev"])
                pe.wait_ge(sem("vn"), rnd + AHEAD["vn"])
                pe.wait_ge(sem("o_ev"), c + AHEAD["o_ev"])
                for g in range(2):
                    r = slice(64 * g, 64 * g + 64)
                    for e in range(2):
                        for pp in range(2):
                            last = pe.matmul(ps[:, 4 + g, (2 * e + pp) * P:(2 * e + pp + 1) * P], stg[r, e, pp * P:(pp + 1) * P], stg[r, e, 256:384],
                                             start=(e == 0 and pp == 0), stop=True, skip_group_check=True)
                last.then_inc(sem("s_qk"), 1)
                for e in range(2):
                    last = pe.transpose(ps[:, 7, e * P:(e + 1) * P], stg[:, e, 384:512], ident)
                last.then_inc(sem("v_mm"), 1)

            def p_turn(c, e):
                pe.wait_ge(sem("probs"), c + 1)
                pe.wait_ge(sem("pt"), c + AHEAD["pt"])
                for g in range(4):
                    last = pe.transpose(ps[:, 6, g * P:(g + 1) * P], pe_[:, e, g, :], ident)
                last.then_inc(sem("p_mm"), 1)

            def pv(rnd, c, e):
                pe.wait_ge(sem("pt"), c + 1 + AHEAD["pt"])
                pe.wait_ge(sem("vn"), rnd + 1 + AHEAD["vn"])
                pe.wait_ge(sem("o_ev"), c + AHEAD["o_ev"])
                for g in range(2):
                    last = pe.matmul(ps[64 * g:64 * g + 64, 7, 256:512], vn[:, e, 64 * g:64 * g + 64],
                                     pt[:, e, 2 * g:2 * g + 2, :].rearrange("p a b -> p (a b)"), start=True, stop=True, skip_group_check=True)
                last.then_inc(sem("o_mm"), 1)

            pe.wait_ge(sem("con_in"), 16)
            ssq(0)
            in_tile(0, 0, ready=rows_ready("h_lo", "h_lo_odd", 0))
            in_tile(1, 1)
            head_sums(0)
            with pe.Fori(1, 3) as i:
                in_tile(i * 2, 0)
                head_sums(i * 2 - 1)
                in_tile(i * 2 + 1, 1)
                head_sums(i * 2)
            in_tile(6, 0)
            in_tile(7, 1)
            with pe.Fori(4, NIN // 2) as i:
                rnd, c = i - 4, i * 2 - 8
                s_and_v(rnd, c)
                in_tile(i * 2, 0)
                p_turn(c, 0)
                in_tile(i * 2 + 1, 1, k1=3)
                pv(rnd, c, 0)
                p_turn(c + 1, 1)
                tile(1, 2, k0=3, k1=6)
                pv(rnd, c + 1, 1)
                tile(1, 2, k0=6)
            for rnd in (6, 7):
                c = 2 * rnd
                s_and_v(rnd, c)
                for e in range(2):
                    p_turn(c + e, e)
                    pv(rnd, c + e, e)

            pe.wait_ge(sem("lora_act"), 2)
            pe.wait_ge(sem("evac"), NIN + AHEAD["evac"])
            pe.wait_ge(sem("o_ev"), 16 + AHEAD["o_ev"])
            h = half

            def lora(it, hf, n):
                tok = slice(hf * HALF, (hf + 1) * HALF)
                w, x = ((lw[0:DL, 0, :], lwa[0:DL, tok]), (lw[DL:DL + IL, 0, :], lwa[DL:DL + IL, tok]), (lw[0:GL, 1, :], lg[0:GL, tok]))[n]
                pe.matmul(ps[:, 7, :], w, x, start=True, stop=True).then_inc(sem("lora_mm"), 1)

            def sum_heads(bank, src, what):
                pe.matmul(ps[:, bank, :], blk, src, start=True, stop=True).then_inc(sem(what), 1)

            def u_mm(it, par, c):
                cp, e = c // 2, c % 2
                r = slice(64 * e, 64 * e + 64)
                if e == 0:
                    for hh in range(2):
                        pe.matmul(ps[:, 4, 64 * hh:64 * hh + 64], wd_[par][:, cp, 1 + hh, :], nat[par][:, cp, 0, 64 * hh:64 * hh + 64], start=(hh == 0), stop=True, skip_group_check=True)
                if c:
                    pe.wait_ge(sem("s"), it * 16 + 2 * c)
                pe.matmul(ps[r, 4, 0:P], wd_[par][:, cp, 0, r], sh[:, c, :], start=False, stop=True, skip_group_check=True).then_inc(sem("u_mm"), 1)

            def s_mm(it, par, c):
                cp, e = c // 2, c % 2
                r = slice(64 * e, 64 * e + 64)
                pe.matmul(ps[:, 5, 0:P], nat[par][r, cp, 1, :], nat[par][r, cp, 0, :], start=True, stop=False, skip_group_check=True)
                pe.wait_ge(sem("u"), it * 8 + c + 1)
                pe.matmul(ps[:, 5, 0:P], nat[par][r, cp, 2, :], us[r, cp, :], start=False, stop=True, skip_group_check=True).then_inc(sem("s_mm"), 1)

            def y_mm(it, par, cp):
                if cp:
                    pe.wait_ge(sem("y"), it * NCP + cp)
                else:
                    pe.wait_ge(sem("rtz"), it + 1)
                for e in range(2):
                    pe.matmul(ps[:, 6, 64 * e:64 * e + 64], sh[:, 2 * cp + e, :], rtz[par][:, cp, 64 * e:64 * e + 64], start=(e == 0), stop=False, skip_group_check=True)
                for hh in range(2):
                    q, d = 2 * cp + hh, slice(64 * hh, 64 * hh + 64)
                    pe.matmul(ps[d, 6, 0:P], us[:, cp, d], am[par][:, q, 1, :], start=False, stop=False, skip_group_check=True)
                    last = pe.matmul(ps[d, 6, 0:P], nat[par][:, cp, 0, d], ark[par][:, hh, cp, :], start=False, stop=True, skip_group_check=True)
                last.then_inc(sem("y_mm"), 1)

            def y_mean(it):
                pe.wait_ge(sem("y"), it * NCP + NCP)
                sum_heads(6, h["y"], "ymean_mm")

            def y_var(it):
                pe.wait_ge(sem("ysq"), it + 1)
                sum_heads(6, h["ysq"], "yvar_mm")

            def t1_mm(it, par, lev, gq):
                if lev:
                    pe.wait_ge(sem("xi"), (it * (NLEV - 1) + lev - 1) * 2 + gq + 1)
                else:
                    pe.wait_ge(sem("x0"), it * 4 + 2 * gq + 2)
                for n in range(4):
                    q = 4 * gq + n
                    last = pe.matmul(ps[:, gq, n * P:(n + 1) * P], am[par][:, q, 0, :], Xi[:, q, :], start=(n == 0), stop=True, skip_group_check=True)
                last.then_inc(sem("t1_mm"), 1)

            def dx_mm(it, par, lev, gq):
                pe.wait_ge(sem("t1"), it * 2 * NLEV + 2 * lev + gq + 1)
                if lev or gq:
                    pe.wait_ge(sem("xit"), (it * NLEV + lev) * 2 + gq)
                for n in range(4):
                    q = 4 * gq + n
                    if lev < NLEV - 1:
                        pe.matmul(ps[:, 2, n * P:(n + 1) * P], XiT[:, q, :], T1[:, q, :], start=(n == 0), stop=True, skip_group_check=True)
                    last = pe.matmul(ps[:, 3, n * P:(n + 1) * P], T1[:, q, :], XiT[:, q, :], start=(n == 0), stop=True, skip_group_check=True)
                last.then_inc(sem("dx_mm"), 1)

            def step(j, par, first=False, last=False):
                it = j * 2 + par
                jn = j if par == 0 else j + 1
                pe.wait_ge(sem("scaled"), it * 4 + 4)
                pe.wait_ge(sem("ended"), it * 2 + 2)
                if not first:
                    pe.wait_ge(sem("wd"), it * NCP)
                for cp in range(NCP):
                    t128 = slice(cp * P, (cp + 1) * P)
                    srcs = (rkv[:, 2, par * HALF + cp * P:par * HALF + (cp + 1) * P], h["kh"][:, t128], h["bh"][:, t128], ar[:, cp, 0, :])
                    for a, src in enumerate(srcs):
                        mm = pe.transpose(ps[:, cp, a * P:(a + 1) * P], src, ident)
                    mm.then_inc(sem("nat_mm"), 1)
                for q in range(NQ):
                    cp, hh = q // 2, q % 2
                    r = slice(64 * hh, 64 * hh + 64)
                    if q >= 4:
                        pe.wait_ge(sem("am"), it * NQ + q - 3)
                    else:
                        pe.wait_ge(sem("nat"), it * NCP + q + 1)
                    pe.matmul(ps[:, q % 4, 0:256], bk[r, cp, 0, :], ar[r, cp, :, :].rearrange("p a b -> p (a b)"), start=True, stop=True, skip_group_check=True)
                    pe.matmul(ps[:, q % 4, 256:512], ar[r, cp, 0, :], bk[r, cp, :, :].rearrange("p a b -> p (a b)"), start=False, stop=True, skip_group_check=True).then_inc(sem("am_mm"), 1)
                if not last:
                    pe.wait_ge(sem("rkv_in"), jn * 32 + 32)
                    pe.wait_ge(sem("bon"), it + 1)
                    lora(it + 1, 1 - par, 0)
                for a in range(4):
                    hh, cpp = a // 2, a % 2
                    r = slice(64 * hh, 64 * hh + 64)
                    pe.wait_ge(sem("am"), it * NQ + 4 + a + 1)
                    for n in range(2):
                        cp = 2 * cpp + n
                        mm = pe.matmul(ps[:, a, n * P:(n + 1) * P], bk[r, cp, 1, :], ar[r, cp, 1, :], start=(n == 0), stop=True, skip_group_check=True)
                    mm.then_inc(sem("ark_mm"), 1)
                if not last:
                    pe.wait_ge(sem("lora_ev"), it * 3 + 4)
                    lora(it + 1, 1 - par, 1)
                if not first:
                    pe.wait_ge(sem("s0"), it)
                pe.wait_ge(sem("ark"), it * 4 + 4)
                for lev in range(NLEV):
                    z = not first and lev < 4
                    t1_mm(it, par, lev, 0)
                    if z:
                        u_mm(it - 1, 1 - par, 2 * lev)
                    elif not first:
                        y_mm(it - 1, 1 - par, 0)
                    t1_mm(it, par, lev, 1)
                    if z:
                        s_mm(it - 1, 1 - par, 2 * lev)
                    elif not first:
                        y_mm(it - 1, 1 - par, 1)
                    dx_mm(it, par, lev, 0)
                    if z:
                        u_mm(it - 1, 1 - par, 2 * lev + 1)
                    elif not first:
                        y_mm(it - 1, 1 - par, 2)
                    dx_mm(it, par, lev, 1)
                    if z:
                        s_mm(it - 1, 1 - par, 2 * lev + 1)
                    elif not first:
                        y_mm(it - 1, 1 - par, 3)
                    if not last:
                        if lev == 0:
                            pe.wait_ge(sem("lora_ev"), it * 3 + 5)
                            lora(it + 1, 1 - par, 2)
                        if lev == 1:
                            pe.wait_ge(sem("lora_ev"), it * 3 + 6)
                            pe.wait_ge(sem("ksq"), it + 2)
                            sum_heads(7, h["ksq"], "kss_mm")
                        if lev == 3:
                            pe.wait_ge(sem("nrm"), it + 2)
                            pe.wait_ge(sem("rk_prod"), it + 2)
                            sum_heads(7, h["t3"], "bon_mm")
                for cp in range(NCP):
                    pe.wait_ge(sem("xit"), it * 2 * NLEV + 2 * NLEV)
                    for hh in range(2):
                        q = 2 * cp + hh
                        pe.matmul(ps[64 * hh:64 * hh + 64, cp, 0:P], nat[par][:, cp, 3, 64 * hh:64 * hh + 64], XiT[:, q, :], start=True, stop=True, skip_group_check=True)
                    for hh in range(2):
                        q = 2 * cp + hh
                        mm = pe.matmul(ps[:, cp, (1 + hh) * P:(2 + hh) * P], am[par][:, q, 3, :], XiT[:, q, :], start=False, stop=True, skip_group_check=True)
                    mm.then_inc(sem("wd_mm"), 1)
                    if cp == 1 and not first:
                        y_mean(it - 1)
                if not first:
                    y_var(it - 1)

            pe.wait_ge(sem("rkv_in"), 32)
            for n in range(3):
                if n:
                    pe.wait_ge(sem("lora_ev"), n)
                lora(0, 0, n)
            pe.wait_ge(sem("lora_ev"), 3)
            pe.wait_ge(sem("ksq"), 1)
            sum_heads(7, h["ksq"], "kss_mm")
            pe.wait_ge(sem("nrm"), 1)
            pe.wait_ge(sem("rk_prod"), 1)
            sum_heads(7, h["t3"], "bon_mm")
            step(0, 0, first=True)
            step(0, 1)
            with pe.Fori(1, NJ - 1) as j:
                step(j, 0)
                step(j, 1)
            step(NJ - 1, 0)
            step(NJ - 1, 1, last=True)
            end = 2 * NJ - 1
            pe.wait_ge(sem("wd"), end * NCP + NCP)
            pe.wait_ge(sem("s0"), end + 1)
            for c in range(8):
                u_mm(end, 1, c)
                s_mm(end, 1, c)
            for cp in range(NCP):
                y_mm(end, 1, cp)
            y_mean(end)
            y_var(end)

            pe.wait_ge(sem("y_ready"), 2 * NJ)

            def out_tile(i, p, **kw):
                pe.wait_ge(sem("wlo_made"), T_OUT + i * 2 + p + 1)
                pe.wait_ge(sem("x1_made"), i * 2 + p - 1 + AHEAD["x1_made"])
                tile(p, 2 * p, **kw)

            out_tile(0, 0, ready=rows_ready("mix_lo", "mix_lo_odd", 0))
            out_tile(0, 1)
            with pe.Fori(1, KT // 2) as i:
                out_tile(i, 0)
                out_tile(i, 1)
            ssq(1)

            def up_tiles(i, first=False):
                for par in range(2):
                    for p in range(2):
                        f = i * 2 + par
                        pe.wait_ge(sem("wlo_made"), T_UP + f * 2 + p + 1)
                        pe.wait_ge(sem("convolved"), f * 2 + p - 3 + AHEAD["convolved"])
                        tile(p, 2 * p + 4 * par, ready=rows_ready("h_lo", "h_lo_odd", KT // 2) if first and par == 0 and p == 0 else None)

            up_tiles(0, True)
            with pe.Fori(1, NF // 2) as i:
                up_tiles(i)

            def down_tile(d, p, first=False):
                pe.wait_ge(sem("y2_made"), d - 1 + AHEAD["y2_made"])
                for k in range(NF):
                    hf, kk = k // (NF // 2), k % (NF // 2)
                    if kk == 0:
                        pe.wait_ge(sem("down_lo"), d * 2 + hf + 1)
                    if first:
                        pe.wait_ge(sem("act_lo_odd" if k % 2 else "act_lo"), k // 2 + 1 + AHEAD.get("act_lo_odd" if k % 2 else "act_lo", 0))
                    wh, wl = dhi[hf][:, kk * P:(kk + 1) * P], dlo[hf][:, kk * P:(kk + 1) * P]
                    for n, (w, rows) in enumerate(((wh, actH), (wh, actL), (wl, actH))):
                        for nh in range(2):
                            last = pe.matmul(ps[:, 2 * p + nh, :], w, rows[k][:, nh * HALF:(nh + 1) * HALF],
                                             start=(k == 0 and n == 0), stop=(k == NF - 1 and n == 2))
                    if kk == NF // 2 - 1:
                        last.then_inc(sem("down_mm"), 1)

            pe.wait_ge(sem("convolved"), 2 * NF - 2 + AHEAD["convolved"])
            down_tile(0, 0, first=True)
            down_tile(1, 1)
            with pe.Fori(1, KT // 2) as i:
                down_tile(i * 2, 0)
                down_tile(i * 2 + 1, 1)


def kernel(**inputs):
    import concourse.bacc as _bacc
    from concourse import mybir as _mybir
    from concourse.bass_utils import run_bass_kernel_spmd as _run

    A = {k: np.asarray(v) for k, v in inputs.items()}

    def tiles(w):
        k, n = w.shape
        return np.ascontiguousarray(w.reshape(k // P, P, n // P, P).transpose(2, 1, 0, 3).reshape(n // P, P, k))

    def cols(v):
        return np.ascontiguousarray(v.reshape(-1, P).T)

    w0, mu0 = A["w_in0"], A["shift_mu0"]
    ro = 768
    zw = lambda n: np.zeros((D, n), np.float32)
    q_heads = [h for t in range(4) for h in (t, 4 + t)]
    qcols = np.concatenate([np.arange(h * HD, (h + 1) * HD) for h in q_heads])
    lo = 3 * RW
    parts = [w0[:, qcols], w0[:, RW:ro],
             w0[:, ro + lo:ro + lo + DL + IL], zw(P - DL - IL), w0[:, ro + lo + DL + IL:ro + lo + DL + IL + GL], zw(P - GL)]
    mus = [np.zeros(768, np.float32),
           mu0[lo:lo + DL + IL], np.zeros(P - DL - IL, np.float32), mu0[lo + DL + IL:], np.zeros(P - GL, np.float32)]
    for j in range(NJ):
        for a in range(3):
            s = a * RW + j * P
            parts.append(w0[:, ro + s:ro + s + P])
            mus.append(mu0[s:s + P])
    win = tiles(np.concatenate(parts, axis=1))
    mu = cols(np.concatenate(mus))

    sinks = A["attn_sinks"][0]
    scol = np.zeros((P, 4), np.float32)
    for g in range(2):
        for pp in range(2):
            for m in range(2):
                scol[64 * m:64 * m + 64, g * 2 + pp] = sinks[g * 4 + pp * 2 + m]
    full = lambda v: np.full((P, 1), v, np.float32)
    cw, cb = A["ffn_conv_w"][0], A["ffn_conv_b"][0]
    conv = np.stack([cw[0], cw[1], cw[2], cb]).reshape(4, 2, NF, P).transpose(3, 2, 1, 0).reshape(P, NF * 8)
    vecs = np.concatenate([mu, cols(A["ada_b"][0]), cols(A["norm_mix_g"][0]), cols(A["norm_ffn_g"][0]),
                           *[np.tile(A["attn_q_gain"][0], 2)[:, None]] * 4, np.tile(A["attn_k_gain"][0], 2)[:, None],
                           full(RMS_EPS), full(LNX_EPS), scol, full(1e-30), conv], axis=1)
    assert vecs.shape[1] == V_N
    loraw = np.zeros((NJ, P, 2, P), np.float32)
    for j in range(NJ):
        c = slice(j * P, (j + 1) * P)
        loraw[j, 0:DL, 0] = A["rwkv_w_up"][0][:, c]
        loraw[j, DL:DL + IL, 0] = A["rwkv_a_up"][0][:, c]
        loraw[j, 0:GL, 1] = A["rwkv_g_up"][0][:, c]
    jn = [A["rwkv_w0"][0], A["rwkv_a0"][0], A["rwkv_k_k"][0], A["rwkv_k_a"][0], A["rwkv_r_k"][0].reshape(-1),
          A["rwkv_lnx_g"][0], A["rwkv_lnx_b"][0], np.zeros(RW, np.float32)]
    jvecs = np.ascontiguousarray(np.stack(jn, axis=-1).reshape(NJ, P, J_N).transpose(1, 0, 2).reshape(P, NJ * J_N))
    wo = A["w_out"][0]
    wo = np.concatenate([wo[:RW], wo[RW:][qcols]], axis=0)
    up = A["ffn_w_up"][0].reshape(D, 2, NF, P).transpose(0, 2, 1, 3).reshape(D, 2 * FF)
    arrays = {
        "xT": np.ascontiguousarray(A["x"][0].T).reshape(KT, P, S),
        "condb": np.ascontiguousarray(np.broadcast_to(A["c"], (P, D))),
        "adaw": np.ascontiguousarray(A["ada_w"][0].T).reshape(NADA, P, D),
        "vecs": np.ascontiguousarray(vecs.astype(np.float32)),
        "consts": constants(),
        "win": win, "loraw": loraw, "jvecs": jvecs,
        "wout": tiles(wo), "wup": tiles(up), "wdown": tiles(A["ffn_w_down"][0]),
    }
    nc = _bacc.Bacc("TRN2", target_bir_lowering=False, num_devices=1)
    aps = {}
    for name, a in arrays.items():
        aps[name] = nc.dram_tensor(name, a.shape, _mybir.dt.from_np(a.dtype), kind="ExternalInput").ap()
    aps["outT"] = nc.dram_tensor("outT", (KT, P, S), F32, kind="ExternalOutput").ap()
    build(nc, **aps)
    r = _run(nc, [arrays], core_ids=[0])
    y = r.results[0]["outT"]
    return np.ascontiguousarray(y.reshape(D, S).T).reshape(1, S, D)
```

```python
import math
from contextlib import ExitStack

import numpy as np

import concourse.bass as bass
from concourse import mybir

F32 = mybir.dt.float32
F32R = mybir.dt.float32r
ALU = mybir.AluOpType
ACT = mybir.ActivationFunctionType
AX_X = mybir.AxisListType.X

P = 128
D = 1024
S = 1024
KT = D // P
HALF = 512
IN_STEP = 4
CH = 64
HD = 64
RW = 512
NJ = RW // P
FF = 2816
NF = FF // P
NIN = 20
NADA = 48
NATT = 6
RMS_EPS = 1e-6
LNX_EPS = 64e-5
DEC = math.exp(-0.5)
NEG = -1e30
DL, IL, GL = 32, 32, 96
NCP = HALF // P
NLEV = 5
NQ = 2 * NCP

V_MU, V_ADAB, V_GMIX, V_GFFN = 0, 20, 68, 76
V_GAIN, V_EPS, V_LEPS, V_SINK = 84, 89, 90, 91
V_TINY, V_CONV = 95, 96
V_N = V_CONV + NF * 2 * 4
J_W0, J_A0, J_KK, J_KA, J_RK, J_G, J_B, J_N = 0, 1, 2, 3, 4, 5, 6, 8
C_ID, C_BLK, C_ONE, C_M4, C_OFF1, C_OFF1T, C_LEV, C_RST = 0, 1, 2, 3, 7, 8, 9, 14
C_N = C_RST + 4


AHEAD = {
    "evac": 2, "x1_made": 2, "act_made": 2, "y2_made": 2, "ada_used": 4, "convolved": 4,
    "o_ev": 2, "o_mm": 2, "p_mm": 2, "pt": 2, "qn": 2, "qn_mm": 2, "qsd": 2, "s_ev": 2, "s_qk": 2,
    "v_mm": 2, "vn": 1, "shift": 2, "proj_out": 1, "y_out": 1,
    "y_mm": 8,
}


def constants():
    t = np.arange(P)
    same = (t[:, None] // CH) == (t[None, :] // CH)
    lower = same & (t[:, None] > t[None, :])
    mats = [np.eye(P), same, np.ones((P, P)),
            lower.T, same & (t[:, None] <= t[None, :]), lower, lower]
    offs = []
    for m in (1, 2, 4, 8, 16, 32):
        pair = (t[:, None] // (2 * m)) == (t[None, :] // (2 * m))
        offs.append(pair & ((t[:, None] // m) % 2 == 1) & ((t[None, :] // m) % 2 == 0))
    mats += [offs[0], offs[0].T] + offs[1:]
    reset = np.tile((np.arange(HALF) % CH != 0)[None, :], (P, 1))
    return np.concatenate([m.astype(np.float32) for m in mats] + [reset.astype(np.float32)], axis=1)


def build(nc, xT, condc, condb, adaw0, adaw, vecs, consts, win, loraw, jvecs, wout, wup, wdown, outT):
    with ExitStack() as ctx:
        sems = {}

        def sem(name):
            if name not in sems:
                sems[name] = ctx.enter_context(nc.semaphore(name))
            return sems[name]

        def at(name, kb, shape, dt=F32):
            return nc.alloc_sbuf_tensor_at(name, shape, dt, offset=int(kb * 1024))

        projD = nc.dram_tensor("projD", (NIN - NATT, P, S), F32, kind="Internal").ap()
        mixD = nc.dram_tensor("mixD", (KT, P, S), F32, kind="Internal").ap()
        x1D = nc.dram_tensor("x1D", (KT, P, S), F32, kind="Internal").ap()

        A0 = -(-nc.sbuf_base // 32) * 32 / 1024.0
        ctx.enter_context(nc.sbuf_tensor("arena", [P, 206 * 256], F32))
        vec = at("vec", A0 + 0, [P, V_N])
        jv = at("jv", A0 + 2.5, [P, NJ * J_N])
        omu = at("omu", A0 + 1.5, [P, NIN])
        mod = at("mod", A0 + 1.75, [P, NADA])
        modA = at("modA", A0 + 2, [P, 2 * KT])
        omka = at("omka", A0 + 2.25, [P, 1])
        ccol = at("ccol", A0 + 2.375, [P, KT])
        sbias = at("sbias", A0 + 2.4375, [P, KT])
        con = at("con", A0 + 3, [P, C_N * P])
        wraw = at("wraw", A0 + 13, [P, 2, 1024])
        whi = at("whi", A0 + 21, [P, 2, 1024], F32R)
        wlo = at("wlo", A0 + 29, [P, 2, 1024], F32R)
        B = A0 + 37
        HI = at("HI", B, [P, KT, S], F32R)
        LO = at("LO", B + 32, [P, KT, S], F32R)
        X = at("X", B + 64, [P, KT, S])
        adat = at("adat", B + 96, [P, 4, 1024])
        cond = at("cond", B + 112, [P, 1024])
        junk = at("junk", B + 116, [P, 1024])
        sqt = at("sqt", B + 120, [P, 2, S])
        rstd = at("rstd", B + 128, [P, S])
        sqa = at("sqa", B + 132, [P, S])
        adas = at("adas", B + 160, [P, 2, 1024])
        pr = at("pr", B + 136, [P, 2, S])
        mst = at("mst", B + 64, [P, 2, S])
        xin = at("xin", B + 104, [P, 2, S])
        actb = at("actb", B + 64, [P, NF, S])
        gu = at("gu", B + 152, [P, 2, S])
        actH = [at(f"actH{k}", A0 + 13 + 4 * k, [P, S], F32R) for k in range(NF)]
        actL = [at(f"actL{k}", B + 64 + 4 * k, [P, S], F32R) for k in range(NF)]
        DW = NF // 2 * P
        draw = [at("draw0", A0 + 3, [P, DW]), at("draw1", B + 157.5, [P, DW])]
        dlo = [at("dlo0", A0 + 3, [P, DW], F32R), at("dlo1", B + 157.5, [P, DW], F32R)]
        dhi = [at("dhi0", B + 163, [P, DW], F32R), at("dhi1", B + 152, [P, DW], F32R)]
        x1in = at("x1in", A0 + 8.5, [P, S])
        o = [B]

        def alloc(name, shape):
            words = 1
            for n in shape[1:]:
                words *= n
            t = at(name, o[0], shape)
            o[0] += words * 4 / 1024.0
            return t

        lwa = alloc("lwa", [P, S])
        lg = alloc("lg", [P, S])
        lw = [alloc(f"lw{i}", [P, 2, P]) for i in range(2)]
        rkv = [alloc(f"rkv{i}", [P, 3, HALF]) for i in range(2)]
        half = {n: alloc(n, [P, HALF])[:, :] for n in (
            "sg", "aa", "gg", "y", "yc", "cs", "pinv", "kk", "ksq", "nrm", "km", "t2", "kh", "bh", "t3", "bon")}
        T1 = alloc("T1", [P, NQ, P])
        pb = alloc("pb", [P, 8 * 65])
        o[0] = B + 62
        half["yo"] = alloc("yo", [P, HALF])[:, :]
        ar = alloc("ar", [P, NCP, 2, P])
        bk = alloc("bk", [P, NCP, 2, P])
        half["ysq"] = alloc("ysq", [P, HALF])[:, :]
        nat = [alloc(f"nat{i}", [P, NCP, 4, P]) for i in range(2)]
        am = [alloc(f"am{i}", [P, NQ, 4, P]) for i in range(2)]
        ark = [alloc(f"ark{i}", [P, 2, NCP, P]) for i in range(2)]
        wd_ = [alloc(f"wd{i}", [P, NCP, 3, P]) for i in range(2)]
        rtz = [alloc(f"rtz{i}", [P, NCP, P])  for i in range(2)]
        g1 = [alloc(f"g1{i}", [P, HALF]) for i in range(2)]
        g2 = [alloc(f"g2{i}", [P, HALF]) for i in range(2)]
        pend = [alloc(f"pend{i}", [P, 8]) for i in range(2)]
        Xi = alloc("Xi", [P, NQ, P])
        XiT = alloc("XiT", [P, NQ, P])
        sh = alloc("sh", [P, 9, P])
        us = alloc("us", [P, NCP, P])
        assert o[0] <= A0 + 206, o[0]
        o[0] = B + 64
        aqkv = alloc("aqkv", [P, NATT, CH + S])
        asq = alloc("asq", [P, 2, HALF])
        assert o[0] <= B + 96
        o[0] = B + 144
        asd = alloc("asd", [P, 2, HALF])
        stg = alloc("stg", [P, 2, 512])
        sb_s = alloc("sb_s", [P, 2, 4, P])
        pe_ = alloc("pe_", [P, 2, 4, P])
        pt = alloc("pt", [P, 2, 4, P])
        vn = alloc("vn", [P, 2, P])
        sm = alloc("sm", [P, 2, 5, 4])
        negc = alloc("negc", [P, P])
        assert o[0] <= B + 168.5
        ps = ctx.enter_context(nc.psum_tensor("ps", [P, 8, HALF], F32))

        def cm(n, k=1):
            return con[:, n * P:(n + k) * P]

        ident, blk, ones = cm(C_ID), cm(C_BLK), cm(C_ONE)

        def two(b):
            return ps[:, b:b + 2, :].rearrange("p a b -> p (a b)")

        T_OUT, T_UP = NIN, NIN + KT

        block = ctx.enter_context(nc.Block())

        @block.sync
        def _(sp):
            for name, n in AHEAD.items():
                for full in ((name + "0", name + "1") if name.endswith("_out") and name != "y_out" else (name,)):
                    sp.sem_inc(sem(full), n)
            sp.dma_start(vec[:, :], vecs).then_inc(sem("vec_in"), 16)
            sp.dma_start(ccol[:, :], condc).then_inc(sem("ccol_in"), 16)
            for t in range(KT):
                sp.dma_start(X[:, t, :], xT[t]).then_inc(sem(f"x_in{t}"), 16)
                if t == 5:
                    sp.dma_start(cond[:, :], condb).then_inc(sem("cond_in"), 16)
                if t == 3:
                    sp.dma_start(con[:, 0:3 * P], consts[:, 0:3 * P]).then_inc(sem("sums_in"), 16)
            for t in range(KT):
                if t >= 4:
                    sp.wait_ge(sem("ada_used"), t - 3 + AHEAD["ada_used"])
                sp.dma_start(adat[:, t % 4, :], adaw[t]).then_inc(sem(f"ada_in{t % 4}"), 16)
                if t >= 2:
                    sp.wait_ge(sem("ada_mm"), t - 1)
                sp.dma_start(adas[:, t % 2, :], adaw0[t]).then_inc(sem(f"adas_in{t % 2}"), 16)
                if t == 1:
                    for p in range(2):
                        sp.dma_start(wraw[:, p, :], win[p]).then_inc(sem(f"w_in{p}"), 16)
            sp.dma_start(con[:, 3 * P:], consts[:, 3 * P:]).then_inc(sem("con_in"), 16)

            def load_ada(n, s):
                sp.wait_ge(sem("ada_used"), n - 3 + AHEAD["ada_used"])
                sp.dma_start(adat[:, s, :], adaw[n]).then_inc(sem(f"ada_in{s}"), 16)

            def load_w(src, tile, p, n):
                sp.wait_ge(sem("wlo_made"), n)
                sp.dma_start(wraw[:, p, :], src[tile]).then_inc(sem(f"w_in{p}"), 16)

            def in_proj(i, ada=False, store=False, last=False):
                for p in range(2):
                    if ada:
                        for s in range(4):
                            load_ada(8 + i * 8 + 4 * p + s, s)
                    if not last:
                        load_w(win, i * 2 + 2 + p, p, i * 2 + 1 + p)
                    else:
                        load_w(wout, p, p, i * 2 + 1 + p)
                    if store:
                        sp.wait_ge(sem("evac"), i * 2 + 1 + p + AHEAD["evac"])
                        sp.dma_start(projD[i * 2 + p - NATT], pr[:, p, :]).then_inc(sem(f"proj_out{p}"), 16)

            with sp.Fori(0, 3) as i:
                in_proj(i, ada=True)
            in_proj(3, ada=True, store=True)
            with sp.Fori(4, 9) as i:
                in_proj(i, store=True)
            in_proj(9, store=True, last=True)
            for p in range(2):
                sp.wait_ge(sem(f"proj_out{p}"), 16 * (NIN - NATT) // 2 + AHEAD["proj_out"])
            sp.wait_ge(sem("tile_mm"), NIN)
            sp.dma_start(lwa[:, :], projD[0]).then_inc(sem("lora_in"), 16)
            sp.dma_start(lg[:, :], projD[1]).then_inc(sem("lora_in"), 16)
            sp.dma_start(jv[:, :], jvecs).then_inc(sem("jv_in"), 16)

            def load_half(j, hf):
                sp.dma_start(rkv[hf][:, :, :], projD[bass.ds(j * 3 + 2, 3), :, hf * HALF:(hf + 1) * HALF].rearrange("a p s -> p a s")).then_inc(sem(f"rkv_in{hf}"), 16)
                sp.dma_start(lw[hf][:, :, :], loraw[j]).then_inc(sem(f"rkv_in{hf}"), 16)

            def store_y(j, hf):
                sp.wait_ge(sem("y_ready"), j * 2 + hf + 1)
                sp.dma_start(mixD[4 + j, :, hf * HALF:(hf + 1) * HALF], half["yo"]).then_inc(sem("y_out"), 16)

            def next_half(j, hf):
                sp.wait_ge(sem("am"), (j * 2 + hf) * NQ + 1)
                load_half(j + 1, hf)

            load_half(0, 0)
            load_half(0, 1)
            for c0, c1 in ((0, 14), (14, 16)):
                sp.wait_ge(sem("o_ev"), c1 + AHEAD["o_ev"])
                sp.dma_start(mixD[0:4, :, c0 * CH:c1 * CH].rearrange("a p s -> p a s"), aqkv[:, 0:4, CH + c0 * CH:CH + c1 * CH]).then_inc(sem("o_out"), 16)
            for hf in range(2):
                next_half(0, hf)
            with sp.Fori(1, NJ - 1) as j:
                for hf in range(2):
                    next_half(j, hf)
                    store_y(j - 1, hf)
            for hf in range(2):
                store_y(NJ - 2, hf)
            sp.wait_ge(sem("ark_mm"), 4 * 2 * NJ)
            sp.wait_ge(sem("rtz"), 2 * NJ)
            for k in range(KT - 1):
                if k == 4:
                    sp.wait_ge(sem("y_out"), 16 * 2 * (NJ - 1) + AHEAD["y_out"])
                if k >= 2:
                    sp.wait_ge(sem("mix_lo"), k - 1)
                sp.dma_start(mst[:, k % 2, :], mixD[k]).then_inc(sem(f"mix_in{k % 2}"), 16)
            store_y(NJ - 1, 0)
            sp.wait_ge(sem("y_out"), 16 * (2 * NJ - 1) + AHEAD["y_out"])
            sp.wait_ge(sem("mix_lo"), KT - 2)
            sp.dma_start(mst[:, 1, 0:HALF], mixD[KT - 1, :, 0:HALF]).then_inc(sem("mix_in1"), 16)
            sp.wait_ge(sem("y_ready"), 2 * NJ)

            def out_proj(i, last):
                for p in range(2):
                    sp.wait_ge(sem("x1_made"), i * 2 + p - 1 + AHEAD["x1_made"])
                    sp.dma_start(xin[:, p, :], xT[i * 2 + p]).then_inc(sem(f"xin_in{p}"), 16)
                for p in range(2):
                    if not last:
                        load_w(wout, i * 2 + 2 + p, p, i * 2 + 1 + p + T_OUT)
                    else:
                        load_w(wup, p, p, i * 2 + 1 + p + T_OUT)
                    sp.wait_ge(sem("x1_made"), i * 2 + p + 1 + AHEAD["x1_made"])
                    sp.dma_start(x1D[i * 2 + p], X[:, bass.ds(i * 2 + p, 1), :].rearrange("p a s -> p (a s)") ).then_inc(sem("x1_store"), 16)

            with sp.Fori(0, KT // 2 - 1) as i:
                out_proj(i, False)
            out_proj(KT // 2 - 1, True)
            def load_down(d, hf):
                sp.dma_start(draw[hf][:, :], wdown[d, :, hf * DW:(hf + 1) * DW]).then_inc(sem(f"wd_in{hf}"), 16)

            sp.wait_ge(sem("rstd"), 2)
            load_down(0, 0)
            sp.wait_ge(sem("x1_store"), 16 * KT)
            sp.dma_start(x1in[:, :], x1D[0]).then_inc(sem("x1_in"), 16)
            with sp.Fori(0, NF - 1) as f:
                for p in range(2):
                    load_w(wup, f * 2 + 2 + p, p, f * 2 + 1 + p + T_UP)
            sp.wait_ge(sem("act_made"), NF + AHEAD["act_made"])
            load_down(0, 1)
            with sp.Fori(0, KT - 1) as d:
                for hf in range(2):
                    sp.wait_ge(sem("down_mm"), d * 2 + hf + 1)
                    load_down(d + 1, hf)
                sp.wait_ge(sem("y2_made"), d + 1 + AHEAD["y2_made"])
                sp.dma_start(outT[d], x1in[:, :]).then_inc(sem("out_out"), 16)
                sp.wait_ge(sem("out_out"), d * 16 + 16)
                sp.dma_start(x1in[:, :], x1D[d + 1]).then_inc(sem("x1_in"), 16)
            sp.wait_ge(sem("y2_made"), KT + AHEAD["y2_made"])
            sp.dma_start(outT[KT - 1], x1in[:, :]).then_inc(sem("out_out"), 16)
            sp.wait_ge(sem("out_out"), 16 * KT)

        @block.scalar
        def _(act):
            def squares():
                for t in range(KT):
                    act.wait_ge(sem(f"x_in{t}"), 16)
                    if t >= 2:
                        act.wait_ge(sem("sq_sum"), t - 1)
                    act.activation(sqt[:, t % 2, :], X[:, t, :], ACT.Square).then_inc(sem("sq"), 1)

            def squares1(t):
                act.wait_ge(sem("x1_made"), t + 1 + AHEAD["x1_made"])
                act.wait_ge(sem("sq_sum"), KT + t - 1)
                act.activation(sqt[:, t % 2, :], X[:, t, :], ACT.Square).then_inc(sem("sq"), 1)

            def norm(n):
                act.wait_ge(sem("ssq_mm"), n + 1)
                act.activation(rstd[:, :], two(4), ACT.Ln, bias=vec[:, V_EPS:V_EPS + 1], scale=1.0 / D).then_inc(sem("rms_ln"), 1)
                act.wait_ge(sem("rms_ln"), n + 1)
                act.activation(rstd[:, :], rstd[:, :], ACT.Exp, scale=-0.5).then_inc(sem("rstd"), 1)
                if n == 1:
                    act.wait_ge(sem("tile_mm"), T_UP)
                shift = 24 * n
                for t in range(KT):
                    act.wait_ge(sem("h_scaled"), n * KT + t + 1)
                    bias = mod[:, shift + t:shift + t + 1]
                    act.activation(HI[:, t, :], X[:, t, :], ACT.Identity, bias=bias).then_inc(sem("h_hi"), 1)
                    if t % 2:
                        act.activation(X[:, t, :], X[:, t, :], ACT.Identity, bias=bias).then_inc(sem("h_made"), 1)

            def split_hi(p, nth, tiles_before):
                act.wait_ge(sem(f"w_in{p}"), nth)
                act.wait_ge(sem("tile_mm"), tiles_before)
                act.activation(whi[:, p, :], wraw[:, p, :], ACT.Copy).then_inc(sem("whi_made"), 1)

            act.wait_ge(sem("ccol_in"), 16)
            act.activation(ccol[:, :], ccol[:, :], ACT.Silu).then_inc(sem("ccol"), 1)
            act.preload_act_table_set("natural_log_exp_and_others")
            act.wait_ge(sem("vec_in"), 16)
            squares()
            act.wait_ge(sem("cond_in"), 16)
            act.activation(cond[:, :], cond[:, :], ACT.Silu).then_inc(sem("cond"), 1)
            act.preload_act_table_set("natural_log_exp_and_others")
            for p in range(2):
                act.wait_ge(sem(f"w_in{p}"), 16)
                act.activation(whi[:, p, :], wraw[:, p, :], ACT.Copy).then_inc(sem("whi_made"), 1)
            norm(0)

            def exps(c, e):
                act.wait_ge(sem("s_nmax"), c + 1)
                act.wait_ge(sem("p_mm"), c - 1 + AHEAD["p_mm"])
                for g in range(4):
                    act.activation(pe_[:, e, g, :], sb_s[:, e, g, :], ACT.Exp, bias=sm[:, e, 1, g:g + 1],
                                   scale=HD ** -0.5, accum_out=sm[:, e, 3, g:g + 1]).then_inc(sem("p_exp"), 1)
                act.activation(sm[:, e, 4, :], sm[:, e, 2, :], ACT.Exp).then_inc(sem("sink_exp"), 1)

            def pt_evac(c, e):
                act.wait_ge(sem("p_mm"), c + 1 + AHEAD["p_mm"])
                act.wait_ge(sem("o_mm"), c - 1 + AHEAD["o_mm"])
                act.activation(pt[:, e, :, :].rearrange("p a b -> p (a b)"), ps[:, 6, :], ACT.Copy).then_inc(sem("pt"), 1)

            def head_std(t):
                for hf in range(2):
                    act.wait_ge(sem("qn_mm"), t * 2 + hf + 1 + AHEAD["qn_mm"])
                    act.wait_ge(sem("qn"), t * 2 + hf - 1 + AHEAD["qn"])
                    act.activation(asd[:, hf, :], ps[:, 4 + hf, :], ACT.Ln, bias=vec[:, V_EPS:V_EPS + 1], scale=1.0 / HD).then_inc(sem("qln"), 1)
                    act.wait_ge(sem("qln"), t * 2 + hf + 1)
                    act.activation(asd[:, hf, :], asd[:, hf, :], ACT.Exp, scale=-0.5).then_inc(sem("qsd"), 1)

            def attn_tile(i, p):
                t = i * 2 + p
                act.wait_ge(sem("tile_mm"), t + 1)
                act.activation(aqkv[:, t, CH:], two(2 * p), ACT.Copy).then_inc(sem("evac"), 1)
                split_hi(p, i * 16 + 32, t + 1)
                for hf in range(2):
                    act.wait_ge(sem("qn_mm"), t * 2 + hf - 1 + AHEAD["qn_mm"])
                    act.wait_ge(sem("evac"), t + 1 + AHEAD["evac"])
                    act.activation(asq[:, hf, :], aqkv[:, t, CH + hf * HALF:CH + (hf + 1) * HALF], ACT.Square).then_inc(sem("qsq"), 1)

            def rwkv_tile(i, p):
                act.wait_ge(sem("tile_mm"), i * 2 + p + 1)
                act.wait_ge(sem(f"proj_out{p}"), (i - 3) * 16 + AHEAD["proj_out"])
                act.activation(pr[:, p, :], two(2 * p), ACT.Copy, scale=omu[:, bass.ds(i * 2 + p, 1)]).then_inc(sem("unmixed"), 1)
                split_hi(p, i * 16 + 32, i * 2 + p + 1)

            act.wait_ge(sem("omu"), 1)
            act.wait_ge(sem("h_lo"), KT // 2)
            act.wait_ge(sem("h_lo_odd"), KT // 2)
            attn_tile(0, 0)
            attn_tile(0, 1)
            head_std(0)
            for i in range(1, 3):
                attn_tile(i, 0)
                head_std(i * 2 - 1)
                attn_tile(i, 1)
                head_std(i * 2)
            rwkv_tile(3, 0)
            rwkv_tile(3, 1)
            with act.Fori(4, NIN // 2) as i:
                c = i * 2 - 8
                exps(c, 0)
                exps(c + 1, 1)
                rwkv_tile(i, 0)
                pt_evac(c, 0)
                pt_evac(c + 1, 1)
                rwkv_tile(i, 1)
            exps(12, 0)
            exps(13, 1)
            pt_evac(12, 0)
            pt_evac(13, 1)
            act.preload_act_table_set("sigmoid_and_others")
            act.wait_ge(sem("lora_in"), 32)
            act.activation(lwa[0:DL, :], lwa[0:DL, :], ACT.Tanh).then_inc(sem("lora_act"), 1)
            act.activation(lg[0:GL, :], lg[0:GL, :], ACT.Sigmoid).then_inc(sem("lora_act"), 1)

            h = half

            def sigmoids(it, j, banks=(7, 7)):
                act.wait_ge(sem("lora_mm"), it * 3 + 1)
                act.activation(h["sg"], ps[:, banks[0], :], ACT.Sigmoid, bias=jv[:, bass.ds(j * J_N + J_W0, 1)]).then_inc(sem("lora_ev"), 1)
                act.wait_ge(sem("lora_mm"), it * 3 + 2)
                act.activation(h["aa"], ps[:, banks[1], :], ACT.Sigmoid, bias=jv[:, bass.ds(j * J_N + J_A0, 1)]).then_inc(sem("lora_ev"), 1)
                act.preload_act_table_set("natural_log_exp_and_others")

            def gate_and_squares(it, first=False, bank=7):
                act.wait_ge(sem("kkr"), it + 1)
                act.activation(h["ksq"], h["kk"], ACT.Square).then_inc(sem("ksq"), 1)
                act.wait_ge(sem("lora_mm"), it * 3 + 3)
                if not first:
                    act.wait_ge(sem("kept"), it * 3)
                act.activation(h["gg"], ps[:, bank, :], ACT.Copy).then_inc(sem("lora_ev"), 1)

            def decays(it):
                act.wait_ge(sem("cs"), it + 1)
                act.activation(pb[:, :].rearrange("p (c t) -> p c t", t=65)[:, :, 1:65],
                               h["cs"].rearrange("p (c t) -> p c t", t=CH), ACT.Exp, scale=-DEC).then_inc(sem("pexp"), 1)
                act.activation(h["pinv"], h["cs"], ACT.Exp, scale=DEC).then_inc(sem("pexp"), 1)

            def kk_norm(it, bank=7):
                act.wait_ge(sem("kss_mm"), it + 1)
                act.activation(h["nrm"], ps[:, bank, :], ACT.Ln, bias=vec[:, V_TINY:V_TINY + 1]).then_inc(sem("kln"), 1)
                act.wait_ge(sem("kln"), it + 1)
                act.activation(h["nrm"], h["nrm"], ACT.Exp, scale=-0.5).then_inc(sem("nrm"), 1)

            def u_evac(it, par, c):
                cp, e = c // 2, c % 2
                r = slice(64 * e, 64 * e + 64)
                act.wait_ge(sem("u_mm"), it * 8 + c + 1)
                act.activation(us[r, cp, :], ps[r, 4, 0:P], ACT.Copy).then_inc(sem("u"), 1)

            def y_evac(it, cp):
                act.wait_ge(sem("y_mm"), it * NCP + cp + 1 + AHEAD["y_mm"])
                act.activation(h["y"][:, cp * P:(cp + 1) * P], ps[:, 6, 0:P], ACT.Copy).then_inc(sem("y"), 1)

            def mix_hi(k):
                act.wait_ge(sem(f"mix_in{k % 2}"), k // 2 * 16 + 16)
                act.activation(HI[:, k, :], mst[:, k % 2, :], ACT.Copy).then_inc(sem("mix_hi"), 1)

            def y_square(it):
                act.wait_ge(sem("yc"), it + 1)
                act.activation(h["ysq"], h["yc"], ACT.Square).then_inc(sem("ysq"), 1)

            def y_var(it):
                act.wait_ge(sem("yvar_mm"), it + 1)
                act.activation(h["ysq"], ps[:, 6, :], ACT.Ln, bias=vec[:, V_LEPS:V_LEPS + 1], scale=1.0 / HD).then_inc(sem("yln"), 1)
                act.wait_ge(sem("yln"), it + 1)
                act.activation(h["ysq"], h["ysq"], ACT.Exp, scale=-0.5).then_inc(sem("sd"), 1)

            def step(j, par, first=False, second=False, last=False):
                it = j * 2 + par
                jn = j if par == 0 else j + 1
                for cp in range(NCP):
                    act.wait_ge(sem("nat_mm"), it * NCP + cp + 1)
                    act.activation(nat[par][:, cp, :, :].rearrange("p a b -> p (a b)"), ps[:, cp, :], ACT.Copy).then_inc(sem("nat"), 1)
                if not first and not second:
                    y_var(it - 2)
                if not last:
                    sigmoids(it + 1, jn)
                for lev in range(4):
                    if not first:
                        u_evac(it - 1, 1 - par, 2 * lev)
                        u_evac(it - 1, 1 - par, 2 * lev + 1)
                    if not last:
                        if lev == 1:
                            gate_and_squares(it + 1)
                        if lev == 2:
                            decays(it + 1)
                            kk_norm(it + 1)
                    elif lev >= 2:
                        mix_hi(lev - 2)
                if not first:
                    for cp in range(NCP):
                        y_evac(it - 1, cp)
                if last:
                    mix_hi(2)
                for cp in range(NCP):
                    act.wait_ge(sem("wd_mm"), it * NCP + cp + 1)
                    act.activation(wd_[par][:, cp, :, :].rearrange("p a b -> p (a b)"), ps[:, cp, 0:384], ACT.Copy).then_inc(sem("wd"), 1)
                if not first:
                    y_square(it - 1)

            act.wait_ge(sem("jv_in"), 16)
            sigmoids(0, 0, banks=(0, 1))
            exps(14, 0)
            exps(15, 1)
            gate_and_squares(0, first=True, bank=2)
            decays(0)
            pt_evac(14, 0)
            kk_norm(0, bank=3)
            pt_evac(15, 1)
            step(0, 0, first=True)
            step(0, 1, second=True)
            with act.Fori(1, NJ - 1) as j:
                step(j, 0)
                step(j, 1)
            step(NJ - 1, 0)
            step(NJ - 1, 1, last=True)
            mix_hi(3)
            for c in range(8):
                u_evac(2 * NJ - 1, 1, c)
                if c == 0:
                    y_var(2 * NJ - 2)
                if c in (2, 4, 6):
                    mix_hi(3 + c // 2)
            for cp in range(NCP):
                y_evac(2 * NJ - 1, cp)
            y_square(2 * NJ - 1)
            act.wait_ge(sem("mix_in1"), 16 * (KT // 2))
            act.activation(HI[:, KT - 1, 0:HALF], mst[:, 1, 0:HALF], ACT.Copy).then_inc(sem("mix_hi"), 1)
            y_var(2 * NJ - 1)
            act.wait_ge(sem("y_ready"), 2 * NJ)
            act.activation(HI[:, KT - 1, HALF:S], half["yo"], ACT.Copy).then_inc(sem("mix_hi"), 1)

            for t in range(KT):
                if t:
                    squares1(t - 1)
                if t == KT - 1:
                    squares1(t)
                split_hi(t % 2, 16 * (NIN // 2) + t // 2 * 16 + 32, T_OUT + t + 1)
            norm(1)

            def down_hi(hf, n):
                act.wait_ge(sem(f"wd_in{hf}"), n)
                act.activation(dhi[hf][:, :], draw[hf][:, :], ACT.Copy).then_inc(sem("down_hi"), 1)

            def act_hi(k0, k1):
                for k in range(k0, k1):
                    act.wait_ge(sem("act_made"), k + 1 + AHEAD["act_made"])
                    act.activation(actH[k][:, :], actb[:, k, :], ACT.Copy).then_inc(sem("act_hi"), 1)

            def up(f, more):
                for p in range(2):
                    act.wait_ge(sem("tile_mm"), T_UP + f * 2 + p + 1)
                    act.wait_ge(sem("act_made"), f + AHEAD["act_made"])
                    c = V_CONV + (f * 2 + p) * 4
                    act.activation(gu[:, p, :], two(2 * p + 4 * up.par), ACT.Identity,
                                   bias=vec[:, bass.ds(c + 3, 1)], scale=vec[:, bass.ds(c + 2, 1)]).then_inc(sem("conv0"), 1)
                    if more:
                        split_hi(p, 16 * (NIN // 2 + KT // 2) + f * 16 + 32, T_UP + f * 2 + p + 1)
                if not more:
                    act_hi(2, 3)
                act.wait_ge(sem("convolved"), f * 2 + 1 + AHEAD["convolved"])
                act.activation(gu[:, 0, :], gu[:, 0, :], ACT.Silu).then_inc(sem("silu"), 1)

            down_hi(0, 16)
            with act.Fori(0, NF // 2 - 1) as i:
                for par in range(2):
                    up.par = par
                    up(i * 2 + par, True)
            up.par = 0
            up(NF - 2, True)
            act.wait_ge(sem("wlo_made"), T_UP + 2 * NF)
            act_hi(0, 2)
            up.par = 1
            up(NF - 1, False)
            act_hi(3, NF // 2)
            down_hi(1, 16)
            act_hi(NF // 2, NF)
            with act.Fori(1, KT) as d:
                for hf in range(2):
                    down_hi(hf, d * 16 + 16)

        @block.vector
        def _(dve):
            def lo_row(n, t):
                dve.wait_ge(sem("h_hi"), n * KT + t + 1)
                dve.scalar_tensor_tensor(out=LO[:, t, :], in0=X[:, t, :], scalar=mod[:, 24 * n + t:24 * n + t + 1],
                                         in1=HI[:, t, :].bitcast(F32), op0=ALU.add, op1=ALU.subtract).then_inc(sem("h_lo"), 1)

            def scaled_row(n, t):
                dve.scalar_tensor_tensor(out=X[:, t, :], in0=X[:, t, :], scalar=modA[:, n * KT + t:n * KT + t + 1],
                                         in1=rstd[:, :], op0=ALU.mult, op1=ALU.mult).then_inc(sem("h_scaled"), 1)
                if t % 2:
                    lo_row(n, t - 1)

            def add_squares(t, p):
                dve.wait_ge(sem("sq"), t + 1)
                dve.wait_ge(sem("sq_sum"), t)
                dve.tensor_tensor(sqa[:, :], sqa[:, :], sqt[:, p, :], ALU.add).then_inc(sem("sq_sum"), 1)

            dve.memset(sqa[:, :], 0.0).then_inc(sem("sq_zero"), 1)
            dve.wait_ge(sem("vec_in"), 16)
            dve.tensor_scalar(omu[:, :], vec[:, V_MU:V_MU + NIN], -1.0, 1.0, ALU.mult, ALU.add).then_inc(sem("omu"), 1)
            dve.tensor_scalar(sbias[:, :], vec[:, V_ADAB + KT:V_ADAB + 2 * KT], 1.0, None, ALU.add).then_inc(sem("sbias"), 1)
            dve.wait_ge(sem("sq_zero"), 1)
            for t in range(KT):
                add_squares(t, t % 2)
            def ada(n, s, nth):
                dve.wait_ge(sem(f"ada_in{s}"), nth)
                dve.wait_ge(sem("ada_used"), n + AHEAD["ada_used"])
                dve.scalar_tensor_tensor(out=junk[:, :], in0=adat[:, s, :], scalar=1.0, in1=cond[:, :], op0=ALU.mult,
                                         op1=ALU.mult, accum_out=mod[:, bass.ds(n + KT, 1)]).then_inc(sem("ada_used"), 1)

            dve.wait_ge(sem("sbias"), 1)
            dve.wait_ge(sem("cond"), 1)
            for t in range(KT):
                ada(t, t % 4, t // 4 * 16 + 16)
                dve.wait_ge(sem("ada_used"), t + 1 + AHEAD["ada_used"])
                dve.scalar_tensor_tensor(out=modA[:, t:t + 1], in0=mod[:, KT + t:KT + t + 1], scalar=sbias[:, t:t + 1],
                                         in1=vec[:, V_GMIX + t:V_GMIX + t + 1], op0=ALU.add, op1=ALU.mult).then_inc(sem("modA"), 1)
                dve.wait_ge(sem("ada_mm"), t + 1)
                dve.tensor_tensor(mod[:, t:t + 1], ps[:, 6 + t % 2, 0:1], vec[:, V_ADAB + t:V_ADAB + t + 1], ALU.add).then_inc(sem("shift"), 1)
                if t == 0:
                    dve.wait_ge(sem("rstd"), 1)
                dve.wait_ge(sem("modA"), t + 1)
                scaled_row(0, t)
            def head_norm(t):
                for hf in range(2):
                    dve.wait_ge(sem("qsd"), t * 2 + hf + 1 + AHEAD["qsd"])
                    w = aqkv[:, t, CH + hf * HALF:CH + (hf + 1) * HALF]
                    dve.scalar_tensor_tensor(out=w, in0=w, scalar=vec[:, bass.ds(V_GAIN + t, 1)], in1=asd[:, hf, :],
                                             op0=ALU.mult, op1=ALU.mult).then_inc(sem("qn"), 1)

            def ada4(i, p):
                for s in range(4):
                    ada(8 + i * 8 + 4 * p + s, s, 32 + i * 32 + 16 * p + 16)

            def mix(i, p):
                dve.wait_ge(sem("unmixed"), i * 2 + p + 1 - NATT)
                dve.scalar_tensor_tensor(out=pr[:, p, 1:S], in0=two(2 * p)[:, 0:S - 1],
                                         scalar=vec[:, bass.ds(V_MU + i * 2 + p, 1)], in1=pr[:, p, 1:S],
                                         op0=ALU.mult, op1=ALU.add).then_inc(sem("evac"), 1)

            def scores(c, e):
                b0 = e * 256
                dve.tensor_copy(sb_s[:, e, :, :].rearrange("p (g a) b -> p g (a b)", g=2),
                                ps[:, 4:6, b0:b0 + 256]).then_inc(sem("s_ev"), 1)

            def softmax_in(c, e):
                dve.wait_ge(sem("s_ev"), c + 1 + AHEAD["s_ev"])
                if isinstance(c, int) and c == 0:
                    dve.memset(sb_s[:, e, :, 0:CH], NEG).then_inc(sem("s_first"), 1)
                    dve.wait_ge(sem("s_first"), 1)
                dve.tensor_reduce(sm[:, e, 0, :], sb_s[:, e, :, :], AX_X, ALU.max).then_inc(sem("s_small"), 1)
                dve.wait_ge(sem("s_small"), c * 3 + 1)
                dve.scalar_tensor_tensor(out=sm[:, e, 0, :], in0=sm[:, e, 0, :], scalar=HD ** -0.5,
                                         in1=vec[:, V_SINK:V_SINK + 4], op0=ALU.mult, op1=ALU.max).then_inc(sem("s_small"), 1)
                dve.wait_ge(sem("s_small"), c * 3 + 2)
                dve.tensor_tensor(sm[:, e, 2, :], vec[:, V_SINK:V_SINK + 4], sm[:, e, 0, :], ALU.subtract).then_inc(sem("s_small"), 1)
                dve.wait_ge(sem("s_small"), c * 3 + 3)
                dve.tensor_scalar(sm[:, e, 1, :], sm[:, e, 0, :], -1.0, None, ALU.mult).then_inc(sem("s_nmax"), 1)

            def attn_round(rnd, c):
                dve.wait_ge(sem("s_qk"), rnd + 1 + AHEAD["s_qk"])
                scores(c, 0)
                scores(c + 1, 1)
                softmax_in(c, 0)
                softmax_in(c + 1, 1)
                dve.wait_ge(sem("v_mm"), rnd + 1 + AHEAD["v_mm"])
                dve.wait_ge(sem("o_mm"), c + AHEAD["o_mm"])
                dve.tensor_copy(vn[:, :, :], ps[:, 7, 0:2 * P].rearrange("p (a b) -> p a b", b=P)).then_inc(sem("vn"), 1)

            def probs(c, e):
                dve.wait_ge(sem("p_exp"), c * 4 + 4)
                dve.wait_ge(sem("sink_exp"), c + 1)
                dve.tensor_tensor(sm[:, e, 3, :], sm[:, e, 3, :], sm[:, e, 4, :], ALU.add).then_inc(sem("den"), 1)
                dve.wait_ge(sem("den"), c * 2 + 1)
                dve.reciprocal(sm[:, e, 4, :], sm[:, e, 3, :]).then_inc(sem("den"), 1)
                dve.wait_ge(sem("den"), c * 2 + 2)
                dve.tensor_tensor(pe_[:, e, :, :], pe_[:, e, :, :], sm[:, e, 4, :].unsqueeze(2).to_broadcast([P, 4, P]), ALU.mult).then_inc(sem("probs"), 1)

            def o_evac(c):
                dve.wait_ge(sem("o_mm"), c + 1 + AHEAD["o_mm"])
                dve.tensor_copy(aqkv[:, 0:4, bass.ds(c * CH + CH, CH)], ps[:, 7, 256:512].rearrange("p (a b) -> p a b", b=CH)).then_inc(sem("o_ev"), 1)

            ada4(0, 0)
            ada4(0, 1)
            dve.wait_ge(sem("h_lo"), KT // 2)
            dve.wait_ge(sem("h_lo_odd"), KT // 2)
            dve.memset(aqkv[:, 4, 0:CH], 0.0).then_inc(sem("pads"), 1)
            dve.memset(aqkv[:, 5, 0:CH], 0.0).then_inc(sem("pads"), 1)
            head_norm(0)
            with dve.Fori(1, 3) as i:
                ada4(i, 0)
                head_norm(i * 2 - 1)
                ada4(i, 1)
                head_norm(i * 2)
            for p in range(2):
                ada4(3, p)
                mix(3, p)

            def full_round(i, c):
                attn_round(i - 4, c)
                probs(c, 0)
                probs(c + 1, 1)
                mix(i, 0)
                o_evac(c)
                o_evac(c + 1)
                mix(i, 1)

            full_round(4, 0)
            with dve.Fori(5, NIN // 2) as i:
                full_round(i, i * 2 - 8)
            attn_round(6, 12)
            probs(12, 0)
            probs(13, 1)
            o_evac(12)
            o_evac(13)
            dve.wait_ge(sem("ada_used"), NADA - KT + AHEAD["ada_used"])
            dve.tensor_tensor(mod[:, 16:48], mod[:, 16:48], vec[:, V_ADAB + 16:V_ADAB + 48], ALU.add).then_inc(sem("mod"), 1)

            dve.wait_ge(sem("tile_mm"), NIN)
            for p in range(2):
                dve.wait_ge(sem(f"proj_out{p}"), 16 * (NIN - NATT) // 2 + AHEAD["proj_out"])
            pb3 = pb[:, :].rearrange("p (c t) -> p c t", t=65)
            dve.memset(pb3[:, :, 0:1], 1.0).then_inc(sem("pb_one"), 1)
            dve.wait_ge(sem("pb_one"), 1)

            h = half

            def bc(m, n):
                return m.unsqueeze(1).to_broadcast([P, n, P])

            def jcol(j, a):
                return jv[:, bass.ds(j * J_N + a, 1)]

            def rows(j, hf):
                return (rkv[hf][:, a, :] for a in range(3))

            def kk_raw(it, j, hf):
                r, k, v = rows(j, hf)
                dve.wait_ge(sem(f"rkv_in{hf}"), j * 32 + 32)
                dve.wait_ge(sem("ended"), it * 2)
                dve.tensor_scalar(h["kk"], k, jcol(j, J_KK), -1.0, ALU.mult, ALU.mult).then_inc(sem("kkr"), 1)

            def decay_sum(it):
                dve.wait_ge(sem("lora_ev"), it * 3 + 1)
                dve.tensor_tensor_scan(h["cs"], cm(C_RST, 4), h["sg"], 0.0, ALU.mult, ALU.add).then_inc(sem("cs"), 1)

            def k_scaled(it, j, hf):
                r, k, v = rows(j, hf)
                dve.wait_ge(sem("lora_ev"), it * 3 + 2)
                dve.wait_ge(sem("km_parts"), it * 3)
                dve.tensor_scalar(omka[:, :], jcol(j, J_KA), -1.0, 1.0, ALU.mult, ALU.add).then_inc(sem("km_parts"), 1)
                dve.wait_ge(sem("km_parts"), it * 3 + 1)
                dve.tensor_scalar(h["km"], h["aa"], jcol(j, J_KA), omka[:, 0:1], ALU.mult, ALU.add).then_inc(sem("km_parts"), 1)
                dve.wait_ge(sem("km_parts"), it * 3 + 2)
                dve.tensor_tensor(h["km"], k, h["km"], ALU.mult).then_inc(sem("km_parts"), 1)
                dve.wait_ge(sem("km_parts"), it * 3 + 3)
                dve.scalar_tensor_tensor(out=h["t3"], in0=r, scalar=jcol(j, J_RK), in1=h["km"], op0=ALU.mult, op1=ALU.mult).then_inc(sem("rk_prod"), 1)

            def kk_unit(it):
                dve.wait_ge(sem("nrm"), it + 1)
                dve.scalar_tensor_tensor(out=h["kk"], in0=h["nrm"], scalar=1e12, in1=h["kk"], op0=ALU.min, op1=ALU.mult).then_inc(sem("nkk"), 1)
                dve.wait_ge(sem("pexp"), it * 2 + 2)
                dve.scalar_tensor_tensor(out=h["t2"], in0=h["aa"], scalar=-1.0, in1=h["pinv"], op0=ALU.mult, op1=ALU.mult).then_inc(sem("t2"), 1)

            def bonus(it, j, hf):
                r, k, v = rows(j, hf)
                dve.wait_ge(sem("bon_mm"), it + 1)
                dve.tensor_tensor(h["bon"], ps[:, 7, :], v, ALU.mult).then_inc(sem("bon"), 1)

            def keep(it, j, par):
                dve.wait_ge(sem("lora_ev"), it * 3 + 3)
                dve.wait_ge(sem("bon"), it + 1)
                dve.tensor_scalar(g1[par][:, :], h["gg"], jcol(j, J_G), None, ALU.mult).then_inc(sem("kept"), 1)
                dve.scalar_tensor_tensor(out=g2[par][:, :], in0=h["bon"], scalar=jcol(j, J_B), in1=h["gg"], op0=ALU.add, op1=ALU.mult).then_inc(sem("kept"), 1)
                dve.tensor_copy(pend[par][:, :], pb[:, :].rearrange("p (c t) -> p c t", t=65)[:, :, 64]).then_inc(sem("kept"), 1)

            def state(it, par, c):
                dve.wait_ge(sem("s_mm"), it * 8 + c + 1)
                for hh in range(2):
                    d = slice(64 * hh, 64 * hh + 64)
                    dve.scalar_tensor_tensor(out=sh[d, c + 1, d], in0=sh[d, c, d], scalar=pend[par][d, c:c + 1],
                                             in1=ps[d, 5, d], op0=ALU.mult, op1=ALU.add).then_inc(sem("s"), 1)
                dve.wait_ge(sem("s"), it * 16 + 2 * c + 2)

            def first_state(it, par):
                dve.wait_ge(sem("kept"), it * 3 + 3)
                dve.wait_ge(sem("y_mm"), it * NCP + AHEAD["y_mm"])
                if par == 0:
                    dve.memset(sh[:, 0, :], 0.0).then_inc(sem("s0"), 1)
                else:
                    dve.tensor_copy(sh[:, 0, :], sh[:, 8, :]).then_inc(sem("s0"), 1)
                dve.wait_ge(sem("s0"), it + 1)

            def output(it):
                dve.wait_ge(sem("sd"), it + 1)
                dve.wait_ge(sem("y_out"), it * 16 + AHEAD["y_out"])
                dve.tensor_tensor(h["yo"], h["yc"], h["ysq"], ALU.mult).then_inc(sem("y_parts"), 1)
                dve.wait_ge(sem("y_parts"), it * 2 + 1)

            def output2(it, par):
                dve.tensor_tensor(h["yo"], h["yo"], g1[par][:, :], ALU.mult).then_inc(sem("y_parts"), 1)
                dve.wait_ge(sem("y_parts"), it * 2 + 2)
                dve.tensor_tensor(h["yo"], h["yo"], g2[par][:, :], ALU.add).then_inc(sem("y_ready"), 1)

            def y_centre(it):
                dve.wait_ge(sem("ymean_mm"), it + 1)
                dve.scalar_tensor_tensor(out=h["yc"], in0=ps[:, 6, :], scalar=-1.0 / HD, in1=h["y"], op0=ALU.mult, op1=ALU.add).then_inc(sem("yc"), 1)

            def t1_evac(it, lev, gq):
                dve.wait_ge(sem("t1_mm"), it * 2 * NLEV + 2 * lev + gq + 1)
                dve.tensor_tensor(T1[:, 4 * gq:4 * gq + 4, :], ps[:, gq, :].rearrange("p (a b) -> p a b", b=P),
                                  bc(cm(C_LEV + lev), 4), ALU.mult).then_inc(sem("t1"), 1)

            def dx_evac(it, lev, gq):
                g4 = slice(4 * gq, 4 * gq + 4)
                dve.wait_ge(sem("dx_mm"), it * 2 * NLEV + 2 * lev + gq + 1)
                if lev < NLEV - 1:
                    dve.tensor_tensor(Xi[:, g4, :], ps[:, gq, :].rearrange("p (a b) -> p a b", b=P), Xi[:, g4, :], ALU.add).then_inc(sem("xi"), 1)
                dve.tensor_tensor(XiT[:, g4, :], ps[:, 2 + gq, :].rearrange("p (a b) -> p a b", b=P), XiT[:, g4, :], ALU.add).then_inc(sem("xit"), 1)

            def step(j, par, first=False, second=False, last=False):
                it = j * 2 + par
                jn = j if par == 0 else j + 1
                for q in range(NQ):
                    dve.wait_ge(sem("am_mm"), it * NQ + q + 1)
                    dve.tensor_tensor(am[par][:, q, :, :].rearrange("p a b -> p (a b)"), ps[:, q % 4, :], cm(C_M4, 4), ALU.mult).then_inc(sem("am"), 1)
                    if q % 4 == 3:
                        g4 = slice(q - 3, q + 1)
                        dve.wait_ge(sem("am"), it * NQ + q + 1)
                        dve.tensor_tensor(Xi[:, g4, :], am[par][:, g4, 2, :], bc(cm(C_OFF1), 4), ALU.mult).then_inc(sem("x0a"), 1)
                        dve.tensor_tensor(XiT[:, g4, :], am[par][:, g4, 0, :], bc(cm(C_OFF1T), 4), ALU.mult).then_inc(sem("x0a"), 1)
                for a in range(4):
                    hh, cpp = a // 2, a % 2
                    dve.wait_ge(sem("ark_mm"), it * 4 + a + 1)
                    dve.tensor_tensor(ark[par][:, hh, 2 * cpp:2 * cpp + 2, :], ps[:, a, 0:256].rearrange("p (a b) -> p a b", b=P),
                                      bc(cm(C_M4 + 1), 2), ALU.mult).then_inc(sem("ark"), 1)
                if not last:
                    kk_raw(it + 1, jn, 1 - par)
                if not first:
                    first_state(it - 1, 1 - par)
                for lev in range(NLEV):
                    z = not first and lev < 4
                    t1_evac(it, lev, 0)
                    if z:
                        state(it - 1, 1 - par, 2 * lev)
                    t1_evac(it, lev, 1)
                    dx_evac(it, lev, 0)
                    if z:
                        state(it - 1, 1 - par, 2 * lev + 1)
                    dx_evac(it, lev, 1)
                    if lev == 0:
                        if not first and not second:
                            output(it - 2)
                            output2(it - 2, par)
                            dve.wait_ge(sem("y_ready"), it - 1)
                    if lev == 1:
                        keep(it, j, par)
                    if not last:
                        if lev == 1:
                            decay_sum(it + 1)
                        if lev == 2:
                            k_scaled(it + 1, jn, 1 - par)
                        if lev == 3:
                            kk_unit(it + 1)
                        if lev == 4:
                            bonus(it + 1, jn, 1 - par)
                if not first:
                    y_centre(it - 1)

            dve.wait_ge(sem("jv_in"), 16)
            attn_round(7, 14)
            kk_raw(0, 0, 0)
            decay_sum(0)
            probs(14, 0)
            probs(15, 1)
            k_scaled(0, 0, 0)
            o_evac(14)
            kk_unit(0)
            o_evac(15)
            bonus(0, 0, 0)
            dve.wait_ge(sem("o_out"), 32)
            dve.memset(sh[:, :, :], 0.0).then_inc(sem("sh_zero"), 1)
            dve.wait_ge(sem("sh_zero"), 1)
            step(0, 0, first=True)
            step(0, 1, second=True)
            with dve.Fori(1, NJ - 1) as j:
                step(j, 0)
                step(j, 1)
            step(NJ - 1, 0)
            step(NJ - 1, 1, last=True)
            first_state(2 * NJ - 1, 1)
            for c in range(8):
                state(2 * NJ - 1, 1, c)
                if c == 1:
                    output(2 * NJ - 2)
                    output2(2 * NJ - 2, 0)
            y_centre(2 * NJ - 1)
            output(2 * NJ - 1)
            output2(2 * NJ - 1, 1)

            dve.wait_ge(sem("mix_hi"), KT + 1)
            dve.tensor_tensor(LO[:, KT - 1, HALF:S], half["yo"], HI[:, KT - 1, HALF:S].bitcast(F32), ALU.subtract).then_inc(sem("mix_lo_last"), 1)

            dve.memset(sqa[:, :], 0.0).then_inc(sem("sq_zero"), 1)
            dve.wait_ge(sem("sq_zero"), 2)

            def residual(i, p):
                dve.wait_ge(sem("tile_mm"), T_OUT + i * 2 + p + 1)
                dve.wait_ge(sem(f"xin_in{p}"), i * 16 + 16)
                dve.scalar_tensor_tensor(out=X[:, i * 2 + p, :], in0=two(2 * p), scalar=mod[:, bass.ds(16 + i * 2 + p, 1)],
                                         in1=xin[:, p, :], op0=ALU.mult, op1=ALU.add).then_inc(sem("x1_made"), 1)

            with dve.Fori(0, KT // 2) as i:
                for p in range(2):
                    residual(i, p)
                    add_squares(KT + i * 2 + p, p)
            dve.wait_ge(sem("mod"), 1)
            dve.scalar_tensor_tensor(out=modA[:, KT:2 * KT], in0=mod[:, 32:40], scalar=1.0,
                                     in1=vec[:, V_GFFN:V_GFFN + KT], op0=ALU.add, op1=ALU.mult).then_inc(sem("modA"), 1)
            dve.wait_ge(sem("x1_store"), 16 * KT)
            dve.wait_ge(sem("modA"), KT + 1)
            dve.wait_ge(sem("rstd"), 2)
            for t in range(KT):
                scaled_row(1, t)

            def up(f, par):
                for p in range(2):
                    c = V_CONV + (f * 2 + p) * 4
                    u = two(2 * p + 4 * par)
                    dve.wait_ge(sem("conv0"), f * 2 + p + 1)
                    dve.scalar_tensor_tensor(out=gu[:, p, 1:S], in0=u[:, 0:S - 1], scalar=vec[:, bass.ds(c + 1, 1)],
                                             in1=gu[:, p, 1:S], op0=ALU.mult, op1=ALU.add).then_inc(sem("conv1"), 1)
                    dve.wait_ge(sem("conv1"), f * 2 + p + 1)
                    dve.scalar_tensor_tensor(out=gu[:, p, 2:S], in0=u[:, 0:S - 2], scalar=vec[:, bass.ds(c, 1)],
                                             in1=gu[:, p, 2:S], op0=ALU.mult, op1=ALU.add).then_inc(sem("convolved"), 1)
                dve.wait_ge(sem("silu"), f + 1)
                dve.wait_ge(sem("convolved"), f * 2 + 2 + AHEAD["convolved"])
                dve.tensor_tensor(actb[:, f, :], gu[:, 0, :], gu[:, 1, :], ALU.mult).then_inc(sem("act_made"), 1)

            def down_lo(hf, n):
                dve.wait_ge(sem("down_hi"), n)
                dve.tensor_tensor(dlo[hf][:, :], draw[hf][:, :], dhi[hf][:, :].bitcast(F32), ALU.subtract).then_inc(sem("down_lo"), 1)

            def act_lo(k0, k1):
                for k in range(k0 | 1, k1, 2):
                    dve.wait_ge(sem("act_hi"), k + 1)
                    dve.tensor_tensor(actL[k][:, :], actb[:, k, :], actH[k][:, :].bitcast(F32), ALU.subtract).then_inc(sem("act_lo_odd"), 1)

            dve.wait_ge(sem("h_lo_odd"), KT)
            down_lo(0, 1)
            with dve.Fori(0, NF // 2 - 1) as i:
                for par in range(2):
                    up(i * 2 + par, par)
            up(NF - 2, 0)
            act_lo(1, 2)
            up(NF - 1, 1)
            act_lo(3, NF // 2)
            down_lo(1, 2)
            act_lo(NF // 2, NF)

            def y2(d, p):
                dve.wait_ge(sem("down_mm"), d * 2 + 2)
                dve.wait_ge(sem("x1_in"), d * 16 + 16)
                dve.scalar_tensor_tensor(out=x1in[:, :], in0=two(2 * p), scalar=mod[:, bass.ds(40 + d, 1)],
                                         in1=x1in[:, :], op0=ALU.mult, op1=ALU.add).then_inc(sem("y2_made"), 1)

            def down_tile(d, p):
                down_lo(0, d * 2 + 3)
                y2(d, p)
                down_lo(1, d * 2 + 4)

            down_tile(0, 0)
            with dve.Fori(0, KT // 2 - 1) as i:
                down_tile(i * 2 + 1, 1)
                down_tile(i * 2 + 2, 0)
            y2(KT - 1, 1)

        @block.gpsimd
        def _(pool):
            def lo_rows(n):
                for t in range(1, KT, 2):
                    pool.wait_ge(sem("h_made"), n * (KT // 2) + t // 2 + 1)
                    pool.tensor_tensor(LO[:, t, :], X[:, t, :], HI[:, t, :].bitcast(F32), ALU.subtract).then_inc(sem("h_lo_odd"), 1)

            def stage(c):
                for e in range(2):
                    pool.wait_ge(sem("qn"), 10 + AHEAD["qn"])
                    pool.tensor_copy(stg[:, e, 0:256].rearrange("p (a b) -> p a b", b=CH), aqkv[:, 0:4, bass.ds(CH + (c + e) * CH, CH)]).then_inc(sem("staged"), 1)
                    pool.tensor_copy(stg[:, e, 256:384], aqkv[:, 4, bass.ds((c + e) * CH, P)]).then_inc(sem("staged"), 1)
                    pool.tensor_copy(stg[:, e, 384:512], aqkv[:, 5, bass.ds((c + e) * CH, P)]).then_inc(sem("staged"), 1)

            def split_lo(p, n):
                pool.wait_ge(sem("whi_made"), n)
                pool.tensor_tensor(wlo[:, p, :], wraw[:, p, :], whi[:, p, :].bitcast(F32), ALU.subtract).then_inc(sem("wlo_made"), 1)

            split_lo(0, 1)
            split_lo(1, 2)
            lo_rows(0)
            with pool.Fori(1, 4) as i:
                for p in range(2):
                    split_lo(p, i * 2 + p + 1)
            split_lo(0, 9)
            pool.wait_ge(sem("evac"), NATT + AHEAD["evac"])
            pool.wait_ge(sem("pads"), 2)
            stage(0)
            split_lo(1, 10)
            with pool.Fori(5, NIN // 2 + 1) as i:
                split_lo(0, i * 2 + 1)
                pool.wait_ge(sem("v_mm"), i - 4 + AHEAD["v_mm"])
                stage(i * 2 - 8)
                split_lo(1, i * 2 + 2)
            pool.wait_ge(sem("v_mm"), 7 + AHEAD["v_mm"])
            stage(14)
            pool.wait_ge(sem("o_out"), 32)

            pool.wait_ge(sem("con_in"), 16)
            h = half

            def q4(t):
                return t.rearrange("p (c e t) -> p c e t", e=2, t=CH)

            def cpv(t):
                return t.rearrange("p (c t) -> p c t", t=P)

            pbv = pb[:, :].rearrange("p (c e t) -> p c e t", e=2, t=65)
            arv = ar[:, :, :, :].rearrange("p c a (e t) -> p c a e t", e=2)
            bkv = bk[:, :, :, :].rearrange("p c a (e t) -> p c a e t", e=2)

            def scaled(it, j, hf):
                r = rkv[hf][:, 0, :]
                pool.wait_ge(sem("km_parts"), it * 3 + 3)
                pool.wait_ge(sem("pexp"), it * 2 + 2)
                pool.wait_ge(sem("ark_mm"), it * 4)
                pool.tensor_tensor(arv[:, :, 1], q4(r), pbv[:, :, :, 1:CH + 1], ALU.mult).then_inc(sem("scaled"), 1)
                pool.tensor_tensor(bk[:, :, 1, :], cpv(h["km"]), cpv(h["pinv"]), ALU.mult).then_inc(sem("scaled"), 1)
                pool.wait_ge(sem("nkk"), it + 1)
                pool.tensor_tensor(arv[:, :, 0], q4(h["kk"]), pbv[:, :, :, 0:CH], ALU.mult).then_inc(sem("scaled"), 1)
                pool.wait_ge(sem("t2"), it + 1)
                pool.tensor_tensor(bk[:, :, 0, :], cpv(h["kk"]), cpv(h["t2"]), ALU.mult).then_inc(sem("scaled"), 1)
                pool.wait_ge(sem("scaled"), it * 4 + 4)
                pend_b = pbv[:, :, :, CH:CH + 1].to_broadcast([P, NCP, 2, CH])
                pool.tensor_tensor(q4(h["kh"]), bkv[:, :, 1], pend_b, ALU.mult).then_inc(sem("ended"), 1)
                pool.tensor_tensor(q4(h["bh"]), bkv[:, :, 0], pend_b, ALU.mult).then_inc(sem("ended"), 1)

            def step(j, par, last=False):
                it = j * 2 + par
                jn = j if par == 0 else j + 1
                pool.wait_ge(sem("scaled"), it * 4 + 4)
                pool.wait_ge(sem("y_mm"), (it - 1) * NCP + AHEAD["y_mm"])
                pool.tensor_tensor(rtz[par][:, :, :], ar[:, :, 1, :], onesb, ALU.mult).then_inc(sem("rtz"), 1)
                for g in range(2):
                    g4 = slice(4 * g, 4 * g + 4)
                    pool.wait_ge(sem("x0a"), it * 4 + 2 * g + 2)
                    pool.tensor_tensor(Xi[:, g4, :], Xi[:, g4, :], ident.unsqueeze(1).to_broadcast([P, 4, P]), ALU.add).then_inc(sem("x0"), 1)
                    pool.tensor_tensor(XiT[:, g4, :], XiT[:, g4, :], ident.unsqueeze(1).to_broadcast([P, 4, P]), ALU.add).then_inc(sem("x0"), 1)
                if not last:
                    scaled(it + 1, jn, 1 - par)

            onesb = ones.unsqueeze(1).to_broadcast([P, NCP, P])
            scaled(0, 0, 0)
            step(0, 0)
            step(0, 1)
            with pool.Fori(1, NJ - 1) as j:
                step(j, 0)
                step(j, 1)
            step(NJ - 1, 0)
            step(NJ - 1, 1, last=True)

            for k in range(KT):
                cols = slice(0, HALF if k == KT - 1 else S)
                pool.wait_ge(sem("mix_hi"), k + 1)
                if k == 5:
                    pool.wait_ge(sem("wd_mm"), 2 * NJ * NCP)
                    pool.wait_ge(sem("kept"), 3 * 2 * NJ)
                pool.tensor_tensor(LO[:, k, cols], mst[:, k % 2, cols], HI[:, k, cols].bitcast(F32), ALU.subtract).then_inc(sem("mix_lo"), 1)

            with pool.Fori(0, KT // 2) as i:
                for p in range(2):
                    split_lo(p, T_OUT + 2 + i * 2 + p + 1)
            lo_rows(1)
            with pool.Fori(0, NF - 1) as i:
                for p in range(2):
                    split_lo(p, T_UP + 2 + i * 2 + p + 1)
            for k in range(0, NF, 2):
                pool.wait_ge(sem("act_hi"), k + 1)
                pool.tensor_tensor(actL[k][:, :], actb[:, k, :], actH[k][:, :].bitcast(F32), ALU.subtract).then_inc(sem("act_lo"), 1)

        @block.tensor
        def _(pe):
            def ssq(n):
                pe.wait_ge(sem("sq_sum"), n * KT + KT)
                for hf in range(2):
                    last = pe.matmul(ps[:, 4 + hf, :], ones, sqa[:, hf * HALF:(hf + 1) * HALF], start=True, stop=True)
                last.then_inc(sem("ssq_mm"), 1)

            def tile_k(p, b, k, passes=(0, 1, 2), halves=(0, 1)):
                wh, wl = whi[:, p, k * P:(k + 1) * P], wlo[:, p, k * P:(k + 1) * P]
                for n in passes:
                    w, rows = ((wh, HI), (wh, LO), (wl, HI))[n]
                    for hf in halves:
                        last = pe.matmul(ps[:, b + hf, :], w, rows[:, k, hf * HALF:(hf + 1) * HALF],
                                         start=(k == 0 and n == 0), stop=(k == KT - 1 and n == 2))
                if k == KT - 1 and 1 in halves:
                    last.then_inc(sem("tile_mm"), 1)

            def first_tiles(even, odd, n):
                for k in range(IN_STEP):
                    pe.wait_ge(sem(odd if k % 2 else even), n + k // 2 + 1 + AHEAD.get(odd if k % 2 else even, 0))
                    for p in range(2):
                        tile_k(p, 2 * p, k)
                for p in range(2):
                    for k in range(IN_STEP, KT):
                        pe.wait_ge(sem(odd if k % 2 else even), n + k // 2 + 1 + AHEAD.get(odd if k % 2 else even, 0))
                        tile_k(p, 2 * p, k)

            def tile(p, b, k0=0, k1=KT):
                for k in range(k0, k1):
                    tile_k(p, b, k)

            def head_sums(t):
                for hf in range(2):
                    pe.wait_ge(sem("qsq"), t * 2 + hf + 1)
                    pe.wait_ge(sem("qsd"), t * 2 + hf - 1 + AHEAD["qsd"])
                    pe.matmul(ps[:, 4 + hf, :], blk, asq[:, hf, :], start=True, stop=True).then_inc(sem("qn_mm"), 1)

            def in_tile(t, p, **kw):
                pe.wait_ge(sem("wlo_made"), t + 1)
                pe.wait_ge(sem("evac"), t - 1 + AHEAD["evac"])
                tile(p, 2 * p, **kw)

            def s_and_v(rnd, c):
                pe.wait_ge(sem("staged"), c * 3 + 6)
                pe.wait_ge(sem("s_ev"), c + AHEAD["s_ev"])
                pe.wait_ge(sem("vn"), rnd + AHEAD["vn"])
                pe.wait_ge(sem("o_ev"), c + AHEAD["o_ev"])
                for g in range(2):
                    r = slice(64 * g, 64 * g + 64)
                    for e in range(2):
                        for pp in range(2):
                            last = pe.matmul(ps[:, 4 + g, (2 * e + pp) * P:(2 * e + pp + 1) * P], stg[r, e, pp * P:(pp + 1) * P], stg[r, e, 256:384],
                                             start=(e == 0 and pp == 0), stop=True, skip_group_check=True)
                last.then_inc(sem("s_qk"), 1)
                for e in range(2):
                    last = pe.transpose(ps[:, 7, e * P:(e + 1) * P], stg[:, e, 384:512], ident)
                last.then_inc(sem("v_mm"), 1)

            def p_turn(c, e):
                pe.wait_ge(sem("probs"), c + 1)
                pe.wait_ge(sem("pt"), c + AHEAD["pt"])
                for g in range(4):
                    last = pe.transpose(ps[:, 6, g * P:(g + 1) * P], pe_[:, e, g, :], ident)
                last.then_inc(sem("p_mm"), 1)

            def pv(rnd, c, e):
                pe.wait_ge(sem("pt"), c + 1 + AHEAD["pt"])
                pe.wait_ge(sem("vn"), rnd + 1 + AHEAD["vn"])
                pe.wait_ge(sem("o_ev"), c + AHEAD["o_ev"])
                for g in range(2):
                    last = pe.matmul(ps[64 * g:64 * g + 64, 7, 256:512], vn[:, e, 64 * g:64 * g + 64],
                                     pt[:, e, 2 * g:2 * g + 2, :].rearrange("p a b -> p (a b)"), start=True, stop=True, skip_group_check=True)
                last.then_inc(sem("o_mm"), 1)

            pe.wait_ge(sem("sums_in"), 16)
            ssq(0)
            pe.wait_ge(sem("ccol"), 1)
            with pe.Fori(0, KT // 2) as i:
                for s in range(2):
                    pe.wait_ge(sem(f"adas_in{s}"), i * 16 + 16)
                    pe.wait_ge(sem("shift"), i * 2 + s - 1 + AHEAD["shift"])
                    for k in range(KT):
                        last = pe.matmul(ps[:, 6 + s, 0:1], adas[:, s, k * P:(k + 1) * P], ccol[:, k:k + 1],
                                         start=(k == 0), stop=(k == KT - 1), skip_group_check=True)
                    last.then_inc(sem("ada_mm"), 1)
            pe.wait_ge(sem("wlo_made"), 2)
            first_tiles("h_lo", "h_lo_odd", 0)
            pe.wait_ge(sem("con_in"), 16)
            head_sums(0)
            with pe.Fori(1, 3) as i:
                in_tile(i * 2, 0)
                head_sums(i * 2 - 1)
                in_tile(i * 2 + 1, 1)
                head_sums(i * 2)
            in_tile(6, 0)
            in_tile(7, 1)
            with pe.Fori(4, NIN // 2) as i:
                rnd, c = i - 4, i * 2 - 8
                s_and_v(rnd, c)
                in_tile(i * 2, 0)
                p_turn(c, 0)
                in_tile(i * 2 + 1, 1, k1=3)
                pv(rnd, c, 0)
                p_turn(c + 1, 1)
                tile(1, 2, k0=3, k1=6)
                pv(rnd, c + 1, 1)
                tile(1, 2, k0=6)
            s_and_v(6, 12)
            for e in range(2):
                p_turn(12 + e, e)
                pv(6, 12 + e, e)

            h = half

            def lora(it, hf, n, bank=7):
                tok = slice(hf * HALF, (hf + 1) * HALF)
                w, x = ((lw[hf][0:DL, 0, :], lwa[0:DL, tok]), (lw[hf][DL:DL + IL, 0, :], lwa[DL:DL + IL, tok]), (lw[hf][0:GL, 1, :], lg[0:GL, tok]))[n]
                pe.matmul(ps[:, bank, :], w, x, start=True, stop=True).then_inc(sem("lora_mm"), 1)

            def sum_heads(bank, src, what):
                pe.matmul(ps[:, bank, :], blk, src, start=True, stop=True).then_inc(sem(what), 1)

            def u_mm(it, par, c):
                cp, e = c // 2, c % 2
                r = slice(64 * e, 64 * e + 64)
                if e == 0:
                    for hh in range(2):
                        pe.matmul(ps[:, 4, 64 * hh:64 * hh + 64], wd_[par][:, cp, 1 + hh, :], nat[par][:, cp, 0, 64 * hh:64 * hh + 64], start=(hh == 0), stop=True, skip_group_check=True)
                if c:
                    pe.wait_ge(sem("s"), it * 16 + 2 * c)
                pe.matmul(ps[r, 4, 0:P], wd_[par][:, cp, 0, r], sh[:, c, :], start=False, stop=True, skip_group_check=True).then_inc(sem("u_mm"), 1)

            def s_mm(it, par, c):
                cp, e = c // 2, c % 2
                r = slice(64 * e, 64 * e + 64)
                pe.matmul(ps[:, 5, 0:P], nat[par][r, cp, 1, :], nat[par][r, cp, 0, :], start=True, stop=False, skip_group_check=True)
                pe.wait_ge(sem("u"), it * 8 + c + 1)
                pe.matmul(ps[:, 5, 0:P], nat[par][r, cp, 2, :], us[r, cp, :], start=False, stop=True, skip_group_check=True).then_inc(sem("s_mm"), 1)

            def y_mm(it, par, cp):
                if cp:
                    pe.wait_ge(sem("y"), it * NCP + cp)
                elif isinstance(it, int) and it == 0:
                    pe.wait_ge(sem("rtz"), 1)
                else:
                    pe.wait_ge(sem("rtz"), it + 1)
                    pe.wait_ge(sem("yln"), it)
                for e in range(2):
                    pe.matmul(ps[:, 6, 64 * e:64 * e + 64], sh[:, 2 * cp + e, :], rtz[par][:, cp, 64 * e:64 * e + 64], start=(e == 0), stop=False, skip_group_check=True)
                for hh in range(2):
                    q, d = 2 * cp + hh, slice(64 * hh, 64 * hh + 64)
                    pe.matmul(ps[d, 6, 0:P], us[:, cp, d], am[par][:, q, 1, :], start=False, stop=False, skip_group_check=True)
                    last = pe.matmul(ps[d, 6, 0:P], nat[par][:, cp, 0, d], ark[par][:, hh, cp, :], start=False, stop=True, skip_group_check=True)
                last.then_inc(sem("y_mm"), 1)

            def y_mean(it):
                pe.wait_ge(sem("y"), it * NCP + NCP)
                sum_heads(6, h["y"], "ymean_mm")

            def y_var(it):
                pe.wait_ge(sem("ysq"), it + 1)
                sum_heads(6, h["ysq"], "yvar_mm")

            def t1_mm(it, par, lev, gq):
                if lev:
                    pe.wait_ge(sem("xi"), (it * (NLEV - 1) + lev - 1) * 2 + gq + 1)
                else:
                    pe.wait_ge(sem("x0"), it * 4 + 2 * gq + 2)
                for n in range(4):
                    q = 4 * gq + n
                    last = pe.matmul(ps[:, gq, n * P:(n + 1) * P], am[par][:, q, 0, :], Xi[:, q, :], start=(n == 0), stop=True, skip_group_check=True)
                last.then_inc(sem("t1_mm"), 1)

            def dx_mm(it, par, lev, gq):
                pe.wait_ge(sem("t1"), it * 2 * NLEV + 2 * lev + gq + 1)
                for n in range(4):
                    q = 4 * gq + n
                    if lev < NLEV - 1:
                        pe.matmul(ps[:, gq, n * P:(n + 1) * P], XiT[:, q, :], T1[:, q, :], start=(n == 0), stop=True, skip_group_check=True)
                    last = pe.matmul(ps[:, 2 + gq, n * P:(n + 1) * P], T1[:, q, :], XiT[:, q, :], start=(n == 0), stop=True, skip_group_check=True)
                last.then_inc(sem("dx_mm"), 1)

            def step(j, par, first=False, second=False, last=False):
                it = j * 2 + par
                jn = j if par == 0 else j + 1
                pe.wait_ge(sem("scaled"), it * 4 + 4)
                pe.wait_ge(sem("ended"), it * 2 + 2)
                for cp in range(NCP):
                    if not first:
                        pe.wait_ge(sem("wd"), it * NCP - NCP + cp + 1)
                    t128 = slice(cp * P, (cp + 1) * P)
                    srcs = (rkv[par][:, 2, t128], h["kh"][:, t128], h["bh"][:, t128], ar[:, cp, 0, :])
                    for a, src in enumerate(srcs):
                        mm = pe.transpose(ps[:, cp, a * P:(a + 1) * P], src, ident)
                    mm.then_inc(sem("nat_mm"), 1)
                for q in range(NQ):
                    cp, hh = q // 2, q % 2
                    r = slice(64 * hh, 64 * hh + 64)
                    if q >= 4:
                        pe.wait_ge(sem("am"), it * NQ + q - 3)
                    else:
                        pe.wait_ge(sem("nat"), it * NCP + q + 1)
                    pe.matmul(ps[:, q % 4, 0:256], bk[r, cp, 0, :], ar[r, cp, :, :].rearrange("p a b -> p (a b)"), start=True, stop=True, skip_group_check=True)
                    pe.matmul(ps[:, q % 4, 256:512], ar[r, cp, 0, :], bk[r, cp, :, :].rearrange("p a b -> p (a b)"), start=False, stop=True, skip_group_check=True).then_inc(sem("am_mm"), 1)
                if not first and not second:
                    y_var(it - 2)
                if not last:
                    pe.wait_ge(sem(f"rkv_in{1 - par}"), jn * 32 + 32)
                    pe.wait_ge(sem("bon"), it + 1)
                    lora(it + 1, 1 - par, 0)
                for a in range(4):
                    hh, cpp = a // 2, a % 2
                    r = slice(64 * hh, 64 * hh + 64)
                    pe.wait_ge(sem("am"), it * NQ + 4 + a + 1)
                    for n in range(2):
                        cp = 2 * cpp + n
                        mm = pe.matmul(ps[:, a, n * P:(n + 1) * P], bk[r, cp, 1, :], ar[r, cp, 1, :], start=(n == 0), stop=True, skip_group_check=True)
                    mm.then_inc(sem("ark_mm"), 1)
                if not last:
                    pe.wait_ge(sem("lora_ev"), it * 3 + 4)
                    lora(it + 1, 1 - par, 1)
                if not first:
                    pe.wait_ge(sem("s0"), it)
                pe.wait_ge(sem("ark"), it * 4 + 4)
                for lev in range(NLEV):
                    z = not first and lev < 4
                    t1_mm(it, par, lev, 0)
                    if z:
                        u_mm(it - 1, 1 - par, 2 * lev)
                    elif not first:
                        y_mm(it - 1, 1 - par, 0)
                    t1_mm(it, par, lev, 1)
                    if z:
                        s_mm(it - 1, 1 - par, 2 * lev)
                    elif not first:
                        y_mm(it - 1, 1 - par, 1)
                    dx_mm(it, par, lev, 0)
                    if z:
                        u_mm(it - 1, 1 - par, 2 * lev + 1)
                    elif not first:
                        y_mm(it - 1, 1 - par, 2)
                    dx_mm(it, par, lev, 1)
                    if z:
                        s_mm(it - 1, 1 - par, 2 * lev + 1)
                    elif not first:
                        y_mm(it - 1, 1 - par, 3)
                    if not last:
                        if lev == 0:
                            pe.wait_ge(sem("lora_ev"), it * 3 + 5)
                            lora(it + 1, 1 - par, 2)
                        if lev == 2:
                            pe.wait_ge(sem("lora_ev"), it * 3 + 6)
                            pe.wait_ge(sem("ksq"), it + 2)
                            sum_heads(7, h["ksq"], "kss_mm")
                        if lev == 3:
                            pe.wait_ge(sem("nrm"), it + 2)
                            pe.wait_ge(sem("rk_prod"), it + 2)
                            sum_heads(7, h["t3"], "bon_mm")
                for cp in range(NCP):
                    pe.wait_ge(sem("xit"), it * 2 * NLEV + 2 * NLEV)
                    for hh in range(2):
                        q = 2 * cp + hh
                        pe.matmul(ps[64 * hh:64 * hh + 64, cp, 0:P], nat[par][:, cp, 3, 64 * hh:64 * hh + 64], XiT[:, q, :], start=True, stop=True, skip_group_check=True)
                    for hh in range(2):
                        q = 2 * cp + hh
                        mm = pe.matmul(ps[:, cp, (1 + hh) * P:(2 + hh) * P], am[par][:, q, 3, :], XiT[:, q, :], start=False, stop=True, skip_group_check=True)
                    mm.then_inc(sem("wd_mm"), 1)
                    if cp == 1 and not first:
                        y_mean(it - 1)

            s_and_v(7, 14)
            pe.wait_ge(sem("evac"), NIN + AHEAD["evac"])
            pe.wait_ge(sem("lora_act"), 2)
            pe.wait_ge(sem("rkv_in0"), 32)
            for n in range(3):
                lora(0, 0, n, bank=n)
            p_turn(14, 0)
            pe.wait_ge(sem("lora_ev"), 3)
            pe.wait_ge(sem("ksq"), 1)
            sum_heads(3, h["ksq"], "kss_mm")
            pv(7, 14, 0)
            p_turn(15, 1)
            pv(7, 15, 1)
            pe.wait_ge(sem("o_ev"), 16 + AHEAD["o_ev"])
            pe.wait_ge(sem("nrm"), 1)
            pe.wait_ge(sem("rk_prod"), 1)
            sum_heads(7, h["t3"], "bon_mm")
            step(0, 0, first=True)
            step(0, 1, second=True)
            with pe.Fori(1, NJ - 1) as j:
                step(j, 0)
                step(j, 1)
            step(NJ - 1, 0)
            step(NJ - 1, 1, last=True)
            end = 2 * NJ - 1
            y_var(end - 1)
            pe.wait_ge(sem("wd"), end * NCP + NCP)
            pe.wait_ge(sem("s0"), end + 1)
            pe.wait_ge(sem("wlo_made"), T_OUT + 2)
            for c in range(8):
                p, k = c % 2, c // 2
                u_mm(end, 1, c)
                pe.wait_ge(sem("mix_lo"), k + 1)
                tile_k(p, 2 * p, k, passes=(0,))
                s_mm(end, 1, c)
                tile_k(p, 2 * p, k, passes=(1, 2))
            for cp in range(NCP):
                p, k = cp % 2, 4 + cp // 2
                y_mm(end, 1, cp)
                pe.wait_ge(sem("mix_lo"), k + 1)
                tile_k(p, 2 * p, k)
            y_mean(end)
            pe.wait_ge(sem("mix_lo"), KT - 1)
            tile_k(0, 0, KT - 2)
            y_var(end)
            tile_k(1, 2, KT - 2)
            pe.wait_ge(sem("mix_lo"), KT)
            for p in range(2):
                tile_k(p, 2 * p, KT - 1, halves=(0,))
            pe.wait_ge(sem("mix_lo_last"), 1)
            for p in range(2):
                tile_k(p, 2 * p, KT - 1, halves=(1,))

            def out_tile(i, p):
                pe.wait_ge(sem("wlo_made"), T_OUT + i * 2 + p + 1)
                pe.wait_ge(sem("x1_made"), i * 2 + p - 1 + AHEAD["x1_made"])
                tile(p, 2 * p)

            with pe.Fori(1, KT // 2) as i:
                out_tile(i, 0)
                out_tile(i, 1)
            ssq(1)

            def up_tiles(i, par):
                for p in range(2):
                    f = i * 2 + par
                    pe.wait_ge(sem("wlo_made"), T_UP + f * 2 + p + 1)
                    pe.wait_ge(sem("convolved"), f * 2 + p - 3 + AHEAD["convolved"])
                    tile(p, 2 * p + 4 * par)

            pe.wait_ge(sem("wlo_made"), T_UP + 2)
            first_tiles("h_lo", "h_lo_odd", KT // 2)
            up_tiles(0, 1)
            with pe.Fori(1, NF // 2) as i:
                up_tiles(i, 0)
                up_tiles(i, 1)

            def down_tile(d, p, first=False):
                pe.wait_ge(sem("y2_made"), d - 1 + AHEAD["y2_made"])
                for k in range(NF):
                    hf, kk = k // (NF // 2), k % (NF // 2)
                    if kk == 0:
                        pe.wait_ge(sem("down_lo"), d * 2 + hf + 1)
                    if first:
                        pe.wait_ge(sem("act_lo_odd" if k % 2 else "act_lo"), k // 2 + 1 + AHEAD.get("act_lo_odd" if k % 2 else "act_lo", 0))
                    wh, wl = dhi[hf][:, kk * P:(kk + 1) * P], dlo[hf][:, kk * P:(kk + 1) * P]
                    for n, (w, rows) in enumerate(((wh, actH), (wh, actL), (wl, actH))):
                        for nh in range(2):
                            last = pe.matmul(ps[:, 2 * p + nh, :], w, rows[k][:, nh * HALF:(nh + 1) * HALF],
                                             start=(k == 0 and n == 0), stop=(k == NF - 1 and n == 2))
                    if kk == NF // 2 - 1:
                        last.then_inc(sem("down_mm"), 1)

            pe.wait_ge(sem("convolved"), 2 * NF - 2 + AHEAD["convolved"])
            down_tile(0, 0, first=True)
            down_tile(1, 1)
            with pe.Fori(1, KT // 2) as i:
                down_tile(i * 2, 0)
                down_tile(i * 2 + 1, 1)


def kernel(**inputs):
    import concourse.bacc as _bacc
    from concourse import mybir as _mybir
    from concourse.bass_utils import run_bass_kernel_spmd as _run

    A = {k: np.asarray(v) for k, v in inputs.items()}

    def tiles(w):
        k, n = w.shape
        return np.ascontiguousarray(w.reshape(k // P, P, n // P, P).transpose(2, 1, 0, 3).reshape(n // P, P, k))

    def cols(v):
        return np.ascontiguousarray(v.reshape(-1, P).T)

    w0, mu0 = A["w_in0"], A["shift_mu0"]
    ro = 768
    zw = lambda n: np.zeros((D, n), np.float32)
    q_heads = [h for t in range(4) for h in (t, 4 + t)]
    qcols = np.concatenate([np.arange(h * HD, (h + 1) * HD) for h in q_heads])
    lo = 3 * RW
    parts = [w0[:, qcols], w0[:, RW:ro],
             w0[:, ro + lo:ro + lo + DL + IL], zw(P - DL - IL), w0[:, ro + lo + DL + IL:ro + lo + DL + IL + GL], zw(P - GL)]
    mus = [np.zeros(768, np.float32),
           mu0[lo:lo + DL + IL], np.zeros(P - DL - IL, np.float32), mu0[lo + DL + IL:], np.zeros(P - GL, np.float32)]
    for j in range(NJ):
        for a in range(3):
            s = a * RW + j * P
            parts.append(w0[:, ro + s:ro + s + P])
            mus.append(mu0[s:s + P])
    win = tiles(np.concatenate(parts, axis=1))
    mu = cols(np.concatenate(mus))

    sinks = A["attn_sinks"][0]
    scol = np.zeros((P, 4), np.float32)
    for g in range(2):
        for pp in range(2):
            for m in range(2):
                scol[64 * m:64 * m + 64, g * 2 + pp] = sinks[g * 4 + pp * 2 + m]
    full = lambda v: np.full((P, 1), v, np.float32)
    cw, cb = A["ffn_conv_w"][0], A["ffn_conv_b"][0]
    conv = np.stack([cw[0], cw[1], cw[2], cb]).reshape(4, 2, NF, P).transpose(3, 2, 1, 0).reshape(P, NF * 8)
    vecs = np.concatenate([mu, cols(A["ada_b"][0]), cols(A["norm_mix_g"][0]), cols(A["norm_ffn_g"][0]),
                           *[np.tile(A["attn_q_gain"][0], 2)[:, None]] * 4, np.tile(A["attn_k_gain"][0], 2)[:, None],
                           full(RMS_EPS), full(LNX_EPS), scol, full(1e-30), conv], axis=1)
    assert vecs.shape[1] == V_N
    loraw = np.zeros((NJ, P, 2, P), np.float32)
    for j in range(NJ):
        c = slice(j * P, (j + 1) * P)
        loraw[j, 0:DL, 0] = A["rwkv_w_up"][0][:, c]
        loraw[j, DL:DL + IL, 0] = A["rwkv_a_up"][0][:, c]
        loraw[j, 0:GL, 1] = A["rwkv_g_up"][0][:, c]
    jn = [A["rwkv_w0"][0], A["rwkv_a0"][0], A["rwkv_k_k"][0], A["rwkv_k_a"][0], A["rwkv_r_k"][0].reshape(-1),
          A["rwkv_lnx_g"][0], A["rwkv_lnx_b"][0], np.zeros(RW, np.float32)]
    jvecs = np.ascontiguousarray(np.stack(jn, axis=-1).reshape(NJ, P, J_N).transpose(1, 0, 2).reshape(P, NJ * J_N))
    wo = A["w_out"][0]
    wo = np.concatenate([wo[RW:][qcols], wo[:RW]], axis=0)
    up = A["ffn_w_up"][0].reshape(D, 2, NF, P).transpose(0, 2, 1, 3).reshape(D, 2 * FF)
    arrays = {
        "xT": np.ascontiguousarray(A["x"][0].T).reshape(KT, P, S),
        "condc": cols(A["c"][0]),
        "condb": np.ascontiguousarray(np.broadcast_to(A["c"], (P, D))),
        "adaw0": tiles(A["ada_w"][0][:, :D]),
        "adaw": np.ascontiguousarray(A["ada_w"][0][:, D:].T).reshape(NADA - KT, P, D),
        "vecs": np.ascontiguousarray(vecs.astype(np.float32)),
        "consts": constants(),
        "win": win, "loraw": loraw, "jvecs": jvecs,
        "wout": tiles(wo), "wup": tiles(up), "wdown": tiles(A["ffn_w_down"][0]),
    }
    nc = _bacc.Bacc("TRN2", target_bir_lowering=False, num_devices=1)
    aps = {}
    for name, a in arrays.items():
        aps[name] = nc.dram_tensor(name, a.shape, _mybir.dt.from_np(a.dtype), kind="ExternalInput").ap()
    aps["outT"] = nc.dram_tensor("outT", (KT, P, S), F32, kind="ExternalOutput").ap()
    build(nc, **aps)
    r = _run(nc, [arrays], core_ids=[0])
    y = r.results[0]["outT"]
    return np.ascontiguousarray(y.reshape(D, S).T).reshape(1, S, D)
```
